# Optimizing a Trainium2 kernel written in Bass

```python
import jax, jax.numpy as jnp
from jax import lax
import numpy as np

D_MODEL = 1024
BATCH = 1
SEQ = 1024
DEPTH = 1

HEAD_DIM = 64
NSA_HEADS = D_MODEL // (2 * HEAD_DIM)
FOX_HEADS = D_MODEL // (2 * HEAD_DIM)
NSA_KV_HEADS = max(1, NSA_HEADS // 4)
NSA_HPG = NSA_HEADS // NSA_KV_HEADS
NSA_WIDTH = NSA_HEADS * HEAD_DIM
FOX_WIDTH = FOX_HEADS * HEAD_DIM
MIX_WIDTH = NSA_WIDTH + FOX_WIDTH
KV_WIDTH = NSA_KV_HEADS * HEAD_DIM
CMP_BLOCK = 32
CMP_STRIDE = 16
CMP_HIDDEN = 2 * HEAD_DIM
SEL_BLOCK = 64
N_SELECT = 16
WINDOW = 512
NSA_Q_BLOCK = 64
FOX_Q_BLOCK = 128
ROPE_THETA = 500000.0
ROPE_DIM = HEAD_DIM // 4
N_GROUPS = 4
EXPERTS_PER_GROUP = 4
N_EXPERTS = N_GROUPS * EXPERTS_PER_GROUP
TOP_K_IN_GROUP = 2
D_EXPERT = D_MODEL // 2
PLE_DIM = 256
EPS = 1e-6
NEG_INF = -1e30
FORCE_BONUS = 1e4
IN_SPLITS = (NSA_WIDTH, KV_WIDTH, KV_WIDTH, KV_WIDTH, KV_WIDTH, KV_WIDTH, KV_WIDTH,
             3 * NSA_HEADS, FOX_WIDTH, FOX_WIDTH, FOX_WIDTH, FOX_HEADS)
IN_COLS = sum(IN_SPLITS)
IN_OFFSETS = tuple(int(v) for v in np.cumsum(IN_SPLITS)[:-1])

kernel_name = 'hymba_nsa_fox_hmoe_layer'

def _rmsnorm(x, g):
    xf = x.astype(jnp.float32)
    y = xf * lax.rsqrt(jnp.mean(xf * xf, axis=-1, keepdims=True) + EPS)
    return (y * g.astype(jnp.float32)).astype(x.dtype)

def _masked_softmax(logits, mask):
    l = jnp.where(mask, logits.astype(jnp.float32), NEG_INF)
    return jax.nn.softmax(l, axis=-1) * mask

def _partial_rope(x, pos):
    half = ROPE_DIM // 2
    inv_freq = jnp.power(jnp.float32(ROPE_THETA), -jnp.arange(half, dtype=jnp.float32) / half)
    ang = pos.astype(jnp.float32)[..., None] * inv_freq
    cos = jnp.cos(ang)[..., None, :]
    sin = jnp.sin(ang)[..., None, :]
    xf = x.astype(jnp.float32)
    x1 = xf[..., :half]
    x2 = xf[..., half:ROPE_DIM]
    out = jnp.concatenate([x1 * cos - x2 * sin, x2 * cos + x1 * sin, xf[..., ROPE_DIM:]], axis=-1)
    return out.astype(x.dtype)

def _compress(tok, pe, w1, w2, tok_idx):
    B = tok.shape[0]
    n_cmp = tok_idx.shape[0]
    blk = tok[:, tok_idx] + pe[None, None, :, None, :]
    blk = jnp.swapaxes(blk, 2, 3).reshape(B, n_cmp, NSA_KV_HEADS, CMP_BLOCK * HEAD_DIM)
    return jax.nn.silu(blk @ w1) @ w2

def _cmp_to_sel_matrix(n_cmp, n_blk):
    cs = np.arange(n_cmp)[:, None] * CMP_STRIDE
    ss = np.arange(n_blk)[None, :] * SEL_BLOCK
    ov = np.clip(np.minimum(cs + CMP_BLOCK, ss + SEL_BLOCK) - np.maximum(cs, ss), 0, None)
    return jnp.asarray(ov / CMP_BLOCK, dtype=jnp.float32)

def _nsa_mixer(q, kc_tok, vc_tok, ks, vs, kw, vw, gates, positions,
               pe_k, w_k1, w_k2, pe_v, w_v1, w_v2):
    B, S = q.shape[0], q.shape[1]
    G, HPG, HD = NSA_KV_HEADS, NSA_HPG, HEAD_DIM
    QB = NSA_Q_BLOCK
    scale = HEAD_DIM ** -0.5
    n_cmp = (S - CMP_BLOCK) // CMP_STRIDE + 1
    n_blk = S // SEL_BLOCK
    n_sel = min(N_SELECT, n_blk)
    tok_idx = np.arange(n_cmp)[:, None] * CMP_STRIDE + np.arange(CMP_BLOCK)[None, :]
    cmp_end = jnp.asarray(tok_idx[:, -1], dtype=jnp.int32)
    kc = _partial_rope(_compress(kc_tok, pe_k, w_k1, w_k2, tok_idx), positions[:, cmp_end])
    vc = _compress(vc_tok, pe_v, w_v1, w_v2, tok_idx)
    agg = _cmp_to_sel_matrix(n_cmp, n_blk)
    ks_blk = ks.reshape(B, n_blk, SEL_BLOCK, G, HD).transpose(0, 3, 1, 2, 4)
    vs_blk = vs.reshape(B, n_blk, SEL_BLOCK, G, HD).transpose(0, 3, 1, 2, 4)
    kw_pad = jnp.pad(kw, ((0, 0), (WINDOW, 0), (0, 0), (0, 0)))
    vw_pad = jnp.pad(vw, ((0, 0), (WINDOW, 0), (0, 0), (0, 0)))
    b_ix = jnp.arange(B)[:, None, None, None]
    g_ix = jnp.arange(G)[None, :, None, None]
    blk_ids = jnp.arange(n_blk)
    in_blk = jnp.arange(SEL_BLOCK)

    def block_fn(c):
        s0 = c * QB
        t = s0 + jnp.arange(QB)
        qg = lax.dynamic_slice_in_dim(q, s0, QB, axis=1).reshape(B, QB, G, HPG, HD)
        gt = lax.dynamic_slice_in_dim(gates, s0, QB, axis=1)
        s_c = jnp.einsum('bqghd,bngd->bghqn', qg, kc) * scale
        p_c = _masked_softmax(s_c, cmp_end[None, :] <= t[:, None])
        o_c = jnp.einsum('bghqn,bngd->bqghd', p_c.astype(vc.dtype), vc)
        imp = jnp.einsum('bghqn,nj->bgqj', p_c, agg)
        cur = t // SEL_BLOCK
        forced = (blk_ids[None] == 0) | (blk_ids[None] == cur[:, None]) | (blk_ids[None] == cur[:, None] - 1)
        future = blk_ids[None] * SEL_BLOCK > t[:, None]
        score = jnp.where(future, -1.0, imp + FORCE_BONUS * forced)
        _, sel = lax.top_k(score, n_sel)
        k_sel = ks_blk[b_ix, g_ix, sel].reshape(B, G, QB, n_sel * SEL_BLOCK, HD)
        v_sel = vs_blk[b_ix, g_ix, sel].reshape(B, G, QB, n_sel * SEL_BLOCK, HD)
        kpos = (sel[..., None] * SEL_BLOCK + in_blk).reshape(B, G, QB, n_sel * SEL_BLOCK)
        s_s = jnp.einsum('bqghd,bgqkd->bghqk', qg, k_sel) * scale
        p_s = _masked_softmax(s_s, (kpos <= t[:, None])[:, :, None])
        o_s = jnp.einsum('bghqk,bgqkd->bqghd', p_s.astype(v_sel.dtype), v_sel)
        k_w = lax.dynamic_slice_in_dim(kw_pad, s0, WINDOW + QB, axis=1)
        v_w = lax.dynamic_slice_in_dim(vw_pad, s0, WINDOW + QB, axis=1)
        wpos = s0 - WINDOW + jnp.arange(WINDOW + QB)
        rel = t[:, None] - wpos[None, :]
        w_mask = (rel >= 0) & (rel < WINDOW) & (wpos[None, :] >= 0)
        s_w = jnp.einsum('bqghd,bkgd->bghqk', qg, k_w) * scale
        p_w = _masked_softmax(s_w, w_mask)
        o_w = jnp.einsum('bghqk,bkgd->bqghd', p_w.astype(v_w.dtype), v_w)
        o = gt[..., 0:1] * o_c + gt[..., 1:2] * o_s + gt[..., 2:3] * o_w
        return o.reshape(B, QB, NSA_WIDTH)

    out = lax.map(block_fn, jnp.arange(S // QB))
    return out.transpose(1, 0, 2, 3).reshape(B, S, NSA_WIDTH)

def _fox_mixer(q, k, v, f_logit):
    B, S = q.shape[0], q.shape[1]
    QB = FOX_Q_BLOCK
    scale = HEAD_DIM ** -0.5
    log_f = jax.nn.log_sigmoid(f_logit.astype(jnp.float32))
    cum = jnp.cumsum(log_f, axis=1).transpose(0, 2, 1)
    kpos = jnp.arange(S)

    def block_fn(c):
        s0 = c * QB
        t = s0 + jnp.arange(QB)
        qb = lax.dynamic_slice_in_dim(q, s0, QB, axis=1)
        cq = lax.dynamic_slice_in_dim(cum, s0, QB, axis=2)
        logits = (jnp.einsum('bqhd,bkhd->bhqk', qb, k).astype(jnp.float32) * scale
                  + (cq[..., None] - cum[:, :, None, :]))
        p = _masked_softmax(logits, kpos[None, :] <= t[:, None])
        o = jnp.einsum('bhqk,bkhd->bqhd', p.astype(v.dtype), v)
        return o.reshape(B, QB, FOX_WIDTH)

    out = lax.map(block_fn, jnp.arange(S // QB))
    return out.transpose(1, 0, 2, 3).reshape(B, S, FOX_WIDTH)

def _hier_moe(u, w_group, b_group, w_router, b_router, w_gate_e, w_up_e, w_down_e):
    B, S = u.shape[0], u.shape[1]
    grp_logits = (u @ w_group + b_group).astype(jnp.float32)
    grp_prob = jax.nn.softmax(grp_logits, axis=-1)
    g_star = jnp.argmax(grp_logits, axis=-1)
    exp_logits = (u @ w_router + b_router).astype(jnp.float32).reshape(B, S, N_GROUPS, EXPERTS_PER_GROUP)
    in_logits = jnp.take_along_axis(exp_logits, g_star[..., None, None], axis=2)[..., 0, :]
    in_prob = jax.nn.softmax(in_logits, axis=-1)
    top_v, top_i = lax.top_k(in_prob, TOP_K_IN_GROUP)
    top_v = top_v / jnp.sum(top_v, axis=-1, keepdims=True)
    w = jnp.take_along_axis(grp_prob, g_star[..., None], axis=-1) * top_v
    expert_id = g_star[..., None] * EXPERTS_PER_GROUP + top_i
    combine = jnp.einsum('bsk,bske->bse', w.astype(u.dtype),
                         jax.nn.one_hot(expert_id, N_EXPERTS, dtype=u.dtype))
    y = jnp.zeros_like(u)
    for e in range(N_EXPERTS):
        hid = jax.nn.silu(u @ w_gate_e[e]) * (u @ w_up_e[e])
        y = y + combine[..., e:e + 1] * (hid @ w_down_e[e])
    return y

def setup_inputs(seed: int = 0) -> dict:
    key = jax.random.key(seed)
    ks = jax.random.split(key, 32)
    f32 = jnp.float32

    def nrm(k, shape, scale):
        return jax.random.normal(k, shape, f32) * scale

    def gain(k, shape):
        return 1.0 + 0.05 * jax.random.normal(k, shape, f32)

    L = DEPTH
    return {
        'x': nrm(ks[0], (BATCH, SEQ, D_MODEL), 1.0),
        'p': nrm(ks[1], (DEPTH, BATCH, SEQ, PLE_DIM), 1.0),
        'positions': (jnp.arange(SEQ, dtype=jnp.int32)[None, :]
                      + jax.random.randint(ks[2], (BATCH, 1), 0, SEQ, dtype=jnp.int32)),
        'g_mix': gain(ks[3], (L, D_MODEL)),
        'w_in': nrm(ks[4], (L, D_MODEL, IN_COLS), D_MODEL ** -0.5),
        'b_nsa_gate': nrm(ks[5], (L, 3 * NSA_HEADS), 0.01),
        'b_forget': 1.0 + 3.0 * jax.random.uniform(ks[6], (L, FOX_HEADS), f32),
        'pe_cmp_k': nrm(ks[7], (L, CMP_BLOCK, HEAD_DIM), 0.02),
        'w_cmp_k1': nrm(ks[8], (L, CMP_BLOCK * HEAD_DIM, CMP_HIDDEN), (CMP_BLOCK * HEAD_DIM) ** -0.5),
        'w_cmp_k2': nrm(ks[9], (L, CMP_HIDDEN, HEAD_DIM), CMP_HIDDEN ** -0.5),
        'pe_cmp_v': nrm(ks[10], (L, CMP_BLOCK, HEAD_DIM), 0.02),
        'w_cmp_v1': nrm(ks[11], (L, CMP_BLOCK * HEAD_DIM, CMP_HIDDEN), (CMP_BLOCK * HEAD_DIM) ** -0.5),
        'w_cmp_v2': nrm(ks[12], (L, CMP_HIDDEN, HEAD_DIM), CMP_HIDDEN ** -0.5),
        'beta_nsa': gain(ks[13], (L, NSA_WIDTH)),
        'beta_fox': gain(ks[14], (L, FOX_WIDTH)),
        'w_out': nrm(ks[15], (L, MIX_WIDTH, D_MODEL), MIX_WIDTH ** -0.5),
        'g_ffn': gain(ks[16], (L, D_MODEL)),
        'w_group': nrm(ks[17], (L, D_MODEL, N_GROUPS), D_MODEL ** -0.5),
        'b_group': nrm(ks[18], (L, N_GROUPS), 0.01),
        'w_router': nrm(ks[19], (L, D_MODEL, N_EXPERTS), D_MODEL ** -0.5),
        'b_router': nrm(ks[20], (L, N_EXPERTS), 0.01),
        'w_gate_e': nrm(ks[21], (L, N_EXPERTS, D_MODEL, D_EXPERT), D_MODEL ** -0.5),
        'w_up_e': nrm(ks[22], (L, N_EXPERTS, D_MODEL, D_EXPERT), D_MODEL ** -0.5),
        'w_down_e': nrm(ks[23], (L, N_EXPERTS, D_EXPERT, D_MODEL), D_EXPERT ** -0.5),
        'g_ple': gain(ks[24], (L, D_MODEL)),
        'w_ple_gate': nrm(ks[25], (L, D_MODEL, D_MODEL), D_MODEL ** -0.5),
        'b_ple_gate': nrm(ks[26], (L, D_MODEL), 0.01),
        'w_ple_proj': nrm(ks[27], (L, PLE_DIM, D_MODEL), PLE_DIM ** -0.5),
        'g_final': gain(ks[28], (D_MODEL,)),
    }

def reference(x, p, positions, g_mix, w_in, b_nsa_gate, b_forget,
              pe_cmp_k, w_cmp_k1, w_cmp_k2, pe_cmp_v, w_cmp_v1, w_cmp_v2,
              beta_nsa, beta_fox, w_out, g_ffn, w_group, b_group, w_router, b_router,
              w_gate_e, w_up_e, w_down_e, g_ple, w_ple_gate, b_ple_gate, w_ple_proj, g_final):
    B, S = x.shape[0], x.shape[1]
    h = x
    for i in range(DEPTH):
        hn = _rmsnorm(h, g_mix[i])
        proj = hn @ w_in[i]
        (q_a, kc_a, vc_a, ks_a, vs_a, kw_a, vw_a, gate_a,
         q_b, k_b, v_b, f_b) = jnp.split(proj, IN_OFFSETS, axis=-1)
        kv = lambda t: t.reshape(B, S, NSA_KV_HEADS, HEAD_DIM)
        q_nsa = _partial_rope(q_a.reshape(B, S, NSA_HEADS, HEAD_DIM), positions)
        gates = jax.nn.sigmoid(gate_a + b_nsa_gate[i]).reshape(B, S, NSA_KV_HEADS, NSA_HPG, 3)
        o_nsa = _nsa_mixer(q_nsa, kv(kc_a), kv(vc_a),
                           _partial_rope(kv(ks_a), positions), kv(vs_a),
                           _partial_rope(kv(kw_a), positions), kv(vw_a),
                           gates, positions,
                           pe_cmp_k[i], w_cmp_k1[i], w_cmp_k2[i],
                           pe_cmp_v[i], w_cmp_v1[i], w_cmp_v2[i])
        fh = lambda t: t.reshape(B, S, FOX_HEADS, HEAD_DIM)
        o_fox = _fox_mixer(fh(q_b), fh(k_b), fh(v_b), f_b + b_forget[i])
        mixed = jnp.concatenate([_rmsnorm(o_nsa, beta_nsa[i]), _rmsnorm(o_fox, beta_fox[i])], axis=-1)
        h = h + mixed @ w_out[i]
        u = _rmsnorm(h, g_ffn[i])
        h = h + _hier_moe(u, w_group[i], b_group[i], w_router[i], b_router[i],
                          w_gate_e[i], w_up_e[i], w_down_e[i])
        v_ple = _rmsnorm(h, g_ple[i])
        gate = jax.nn.sigmoid(v_ple @ w_ple_gate[i] + b_ple_gate[i])
        h = h + gate * (p[i] @ w_ple_proj[i])
    return _rmsnorm(h, g_final)


_drawn_inputs = setup_inputs


def setup_inputs(seed=0):
    import zlib

    import numpy as np

    out = dict(_drawn_inputs(seed))
    spreads = {}
    factors = {'b_nsa_gate': 8.0,
     'pe_cmp_k': 21.761,
     'b_group': 6.02,
     'b_router': 7.617,
     'g_ple': 8.0,
     'b_ple_gate': 64.0}
    for name, (base, spread) in spreads.items():
        noise = np.random.default_rng([zlib.crc32(name.encode()), seed]).standard_normal(out[name].shape)
        drawn = base * np.exp(spread * noise) if base else spread * noise
        out[name] = __import__('jax').numpy.asarray(drawn.astype(out[name].dtype))
    for name, factor in factors.items():
        out[name] = (out[name] * factor).astype(out[name].dtype)
    return out
```

```python
from contextlib import ExitStack

import numpy as np

import concourse.bass as bass
from concourse import mybir

F32 = mybir.dt.float32
F32R = mybir.dt.float32r
BF16 = mybir.dt.bfloat16
I32 = mybir.dt.int32
U32 = mybir.dt.uint32
ALU = mybir.AluOpType
ACT = mybir.ActivationFunctionType
X = mybir.AxisListType.X

P = 128
D = 1024
S = 1024
KD = D // P
NT = S // P
HD = 64
NH = 8
GROUPS = 2
SCALE = HD ** -0.5
CMP_BLOCK, CMP_STRIDE = 32, 16
N_CMP = (S - CMP_BLOCK) // CMP_STRIDE + 1
WINDOW = 512
WB = WINDOW // P
NG, EPG = 4, 4
NE = NG * EPG
FE = D // 2
KF = FE // P
PLE = 256
KP = PLE // P
EPS = 1e-6
NEG = -1e30
TILES = (2 * S) // P + NE - 1
SLOTS = (TILES + 1) * P
ROPE_HALF = HD // 8

C_Q, C_KC, C_VC, C_KS, C_VS, C_KW, C_VW, C_GATE = 0, 512, 640, 768, 896, 1024, 1152, 1280
C_QB, C_KB, C_VB, C_F = 1304, 1816, 2328, 2840

K_ID, K_ROT, K_LT, K_ONE, K_DIAG, K_FAR, K_CMP = 0, 128, 256, 384, 512, 640, 768
K_FREQ = K_CMP + NT * P
K_ISROPE, K_NOROPE, K_VALID, K_PRI, K_TILE, K_COLS = (
    K_FREQ + 1, K_FREQ + 2, K_FREQ + 3, K_FREQ + 4, K_FREQ + 8, K_FREQ + 8 + 32)
K_TOK = K_COLS
K_COLS = K_TOK + NT


def constants():
    c = np.zeros((P, K_COLS), np.float32)
    a = np.arange(P)
    c[:, K_ID:K_ID + P] = np.eye(P)
    rot = np.zeros((P, P), np.float32)
    for h in (0, HD):
        for d in range(ROPE_HALF):
            rot[h + d + ROPE_HALF, h + d] = -1.0
            rot[h + d, h + d + ROPE_HALF] = 1.0
    c[:, K_ROT:K_ROT + P] = rot
    c[:, K_LT:K_LT + P] = (a[:, None] < a[None, :])
    c[:, K_ONE:K_ONE + P] = 1.0
    c[:, K_DIAG:K_DIAG + P] = np.where(a[None, :] <= a[:, None], 0.0, NEG)
    c[:, K_FAR:K_FAR + P] = np.where(a[None, :] > a[:, None], 0.0, NEG)
    for qt in range(NT):
        t = qt * P + a
        end = a * CMP_STRIDE + CMP_BLOCK - 1
        c[:, K_CMP + qt * P:K_CMP + (qt + 1) * P] = np.where(
            (end[None, :] <= t[:, None]) & (a[None, :] < N_CMP), 0.0, NEG)
    inv = np.power(np.float32(500000.0), -np.arange(ROPE_HALF, dtype=np.float32) / np.float32(ROPE_HALF))
    rope = (a % HD) < 2 * ROPE_HALF
    c[:, K_FREQ] = np.where(rope, inv[a % ROPE_HALF], 0.0)
    c[:, K_ISROPE] = rope
    c[:, K_NOROPE] = ~rope
    c[:, K_VALID] = (a >= CMP_BLOCK - 1)
    c[:, K_PRI:K_PRI + 4] = np.arange(4, 0, -1)[None, :]
    c[:, K_TILE:K_TILE + 32] = np.arange(32)[None, :]
    c[:, K_TOK:K_TOK + NT] = a[:, None] + P * np.arange(NT)[None, :]
    return c


class Tally:

    def __init__(self, sem, base=0):
        self.sem, self.base, self.n = sem, base, 0

    def inc(self, ins):
        ins.then_inc(self.sem, 1)
        self.n += 1

    def wait(self, eng):
        eng.wait_ge(self.sem, self.base + self.n)


def mm3(nc, out, a_hi, a_lo, b_hi, b_lo, first, last):
    nc.tensor.matmul(out, a_hi, b_hi, start=first, stop=False)
    nc.tensor.matmul(out, a_hi, b_lo, start=False, stop=False)
    return nc.tensor.matmul(out, a_lo, b_hi, start=False, stop=last)


def wait_alone(eng, sem, value, passed):
    eng.wait_ge(sem, value)
    eng.sem_inc(passed, 1)


class Scope:

    def __init__(self, nc, name):
        self.nc, self.name, self.ctx, self.sems = nc, name, ExitStack(), []

    def __enter__(self):
        self.ctx.__enter__()
        return self

    def __exit__(self, *a):
        if self.sems:
            self.nc.all_engine_barrier()
            self.nc.clear_and_free_semaphores(self.sems)
            self.nc.all_engine_barrier()
        return self.ctx.__exit__(*a)

    def sb(self, name, shape, dt=F32):
        return self.ctx.enter_context(self.nc.sbuf_tensor(f"{self.name}_{name}", shape, dt))

    def ps(self, name, shape, dt=F32):
        return self.ctx.enter_context(self.nc.psum_tensor(f"{self.name}_{name}", shape, dt))

    def sem(self, name):
        self.sems.append(self.nc.alloc_semaphore(f"{self.name}_{name}"))
        return self.sems[-1]

    def block(self):
        return self.nc.Block()


def stage_load(nc, a, K):
    PI = float(np.pi)
    TWO_PI_HI = 6.28125
    TWO_PI_LO = float(2 * np.pi - TWO_PI_HI)
    with Scope(nc, "load") as sc:
        pos = sc.sb("pos", [P, S], I32)
        turns = sc.sb("turns", [P, S], I32)
        ang = sc.sb("ang", [P, S])
        whole = sc.sb("whole", [P, S])
        over = sc.sb("over", [P, S])
        ang_c = sc.sb("ang_c", [P, S])
        loaded, made, reduced, looked = (sc.sem(n) for n in ("loaded", "made", "reduced", "looked"))
        c = K["c"]
        with sc.block() as block:
            @block.sync
            def _(sp):
                sp.dma_start(c[:], a["consts"]).then_inc(loaded, 16)
                sp.dma_start(pos[:], a["positions"].to_broadcast((P, S))).then_inc(loaded, 16)
                sp.wait_ge(loaded, 32)

            @block.vector
            def _(dve):
                dve.wait_ge(loaded, 32)
                own = Tally(made)

                def step(ins):
                    own.inc(ins)
                    own.wait(dve)

                def wrap(x):
                    step(nc.vector.tensor_scalar(over[:], x[:], PI, -2 * PI, ALU.is_gt, ALU.mult))
                    step(nc.vector.tensor_tensor(x[:], x[:], over[:], ALU.add))
                    step(nc.vector.tensor_scalar(over[:], x[:], -PI, 2 * PI, ALU.is_lt, ALU.mult))
                    step(nc.vector.tensor_tensor(x[:], x[:], over[:], ALU.add))
                    step(nc.vector.tensor_scalar(x[:], x[:], 3.1415925, -3.1415925, ALU.min, ALU.max))

                own.inc(nc.vector.tensor_copy(K["maskb"][:], c[:, K_DIAG:K_DIAG + (2 + NT) * P]))
                own.inc(nc.vector.tensor_copy(K["identb"][:], c[:, K_ID:K_ID + P]))
                step(nc.vector.tensor_copy(ang[:], pos[:]))
                step(nc.vector.tensor_scalar(ang[:], ang[:], c[:, K_FREQ:K_FREQ + 1], None, ALU.mult))
                step(nc.vector.tensor_scalar(whole[:], ang[:], 1.0 / (2 * PI), None, ALU.mult))
                step(nc.vector.tensor_copy(turns[:], whole[:]))
                step(nc.vector.tensor_copy(whole[:], turns[:]))
                step(nc.vector.scalar_tensor_tensor(ang[:], whole[:], -TWO_PI_HI, ang[:], ALU.mult, ALU.add))
                step(nc.vector.scalar_tensor_tensor(ang[:], whole[:], -TWO_PI_LO, ang[:], ALU.mult, ALU.add))
                wrap(ang)
                step(nc.vector.tensor_scalar(ang_c[:], ang[:], PI / 2, None, ALU.add))
                wrap(ang_c)
                nc.vector.tensor_copy(over[:, 0:1], ang_c[:, 0:1]).then_inc(reduced, 1)
                dve.wait_ge(looked, 2)
                step(nc.vector.tensor_scalar(K["sin"][:], K["sin"][:], c[:, K_ISROPE:K_ISROPE + 1], None, ALU.mult))
                step(nc.vector.tensor_scalar(K["cos"][:], K["cos"][:], c[:, K_ISROPE:K_ISROPE + 1],
                                             c[:, K_NOROPE:K_NOROPE + 1], ALU.mult, ALU.add))

            @block.scalar
            def _(act):
                act.wait_ge(reduced, 1)
                nc.scalar.activation(K["sin"][:], ang[:], ACT.Sin).then_inc(looked, 1)
                nc.scalar.activation(K["cos"][:], ang_c[:], ACT.Sin).then_inc(looked, 1)


def stage_project(nc, a, K, T):
    with Scope(nc, "prj") as sc:
        XR = 3
        ss = sc.sb("ss", [P, NT])
        rstd = sc.sb("rstd", [P, 2 * NT])
        hT_hi = sc.sb("hT_hi", [P, KD, S], F32R)
        hT_lo = sc.sb("hT_lo", [P, KD, S], F32R)
        w_raw = sc.sb("w_raw", [P, 2, KD, P])
        w_hi = sc.sb("w_hi", [P, 2, KD, P], F32R)
        w_lo = sc.sb("w_lo", [P, 2, KD, P], F32R)
        feat = sc.sb("feat", [P, 2, S])
        turn = sc.sb("turn", [P, S // 2])
        cos_t = K["cos"]
        sin_t = K["sin"]
        VW = 256 + 24 + 8
        v_raw = K["o"][:, 2:5, :].rearrange("p a n -> p (a n)")[:, 0:KD * VW].rearrange("p (k n) -> p k n", k=KD)
        with Scope(nc, "prj_x") as early:
            xt = early.sb("x", [P, XR, D])
            xn = early.sb("xn", [P, 2, D])
            gain = early.sb("gain", [P, D])
            sq = early.sb("sq", [P, D], BF16)
        v_hi = sc.sb("v_hi", [P, KD, VW], F32R)
        v_lo = sc.sb("v_lo", [P, KD, VW], F32R)
        ps_x = sc.ps("ps_x", [P, 2, 512])
        ps_w = sc.ps("ps_w", [P, 2, 512])
        ps_r = sc.ps("ps_r", [P, 512])

        x_in = [sc.sem(f"x_in{i}") for i in range(XR)]
        gain_in, normed, scaled, turned, up_hi, up_lo, own_act, own_dve = (
            sc.sem(n) for n in ("gain_in", "normed", "scaled", "turned", "up_hi", "up_lo", "own_act", "own_dve"))
        squared = sc.sem("squared")
        rooted = sc.sem("rooted")
        var = sc.sem("var")
        w_in_ = [sc.sem(f"w_in{i}") for i in range(2)]
        split_hi, split_lo, product, evac, rotated, turn_made = (
            sc.sem(n) for n in ("split_hi", "split_lo", "product", "evac", "rotated", "turn_made"))
        roped = sc.sem("roped")
        stored = T["stored"]
        v_in = sc.sem("v_in")
        vs_hi, vs_lo, v_product, v_evac = (sc.sem(n) for n in ("vs_hi", "vs_lo", "v_product", "v_evac"))

        x_d = a["x"].rearrange("b (t p) d -> (b t) p d", p=P)
        w_d = a["w_in"].rearrange("l (k p) n -> (l p) k n", p=P)
        FIXED = [(C_Q + P * j, j, True) for j in range(4)] + [
            (C_KC, None, False), (C_VC, None, False), (C_KS, 6, True), (C_KW, 7, True)]
        NFIX = len(FIXED)

        def stores_before(n):
            return sum(1 for m in range(n % 2, n, 2) if FIXED[m][1] is not None)

        VCH = [[(C_VB, 256)], [(C_VB + 256, 256)], [(C_VS, 128), (C_VW, 128), (C_GATE, 24), (C_F, 8)]]

        with sc.block() as block:
            @block.sync
            def _(sp):
                sp.dma_start(gain[:], a["g_mix"].to_broadcast((P, D))).then_inc(gain_in, 16)
                for t in range(NT):
                    if t >= XR:
                        sp.wait_ge(scaled, t - XR + 1)
                    sp.dma_start(xt[:, t % XR, :], x_d[t]).then_inc(x_in[t % XR], 16)
                    if t < 2:
                        c = FIXED[t][0]
                        sp.dma_start(w_raw[:, t, :, :], w_d[:, :, c:c + P]).then_inc(w_in_[t], 16)
                for n in range(2, NFIX):
                    sp.wait_ge(split_hi, n - 1)
                    sp.wait_ge(split_lo, n - 1)
                    c = FIXED[n][0]
                    sp.dma_start(w_raw[:, n % 2, :, :], w_d[:, :, c:c + P]).then_inc(w_in_[n % 2], 16)
                with sp.Fori(0, NFIX // 2) as i:
                    for s in range(2):
                        sp.wait_ge(split_hi, i * 2 + (NFIX + s - 1))
                        sp.wait_ge(split_lo, i * 2 + (NFIX + s - 1))
                        sp.dma_start(w_raw[:, s, :, :],
                                     w_d[:, :, bass.ds(i * (2 * P) + (C_QB + s * P), P)]).then_inc(w_in_[s], 16)
                for n, cols in enumerate(VCH):
                    if n:
                        sp.wait_ge(vs_hi, n)
                        sp.wait_ge(vs_lo, n)
                    o = 0
                    for c, w in cols:
                        sp.dma_start(v_raw[:, :, o:o + w], w_d[:, :, c:c + w]).then_inc(v_in, 16)
                        o += w

            @block.gpsimd
            def _(pool):
                halves = 0
                for n, (_, row, rope) in enumerate(FIXED):
                    if row is None:
                        continue
                    if rope:
                        halves += 2
                        pool.wait_ge(roped, halves)
                    pool.dma_start(T["feat"][row], feat[:, n % 2, :]).then_inc(stored[n % 2], 16)
                with pool.Fori(0, NFIX // 2) as i:
                    for s in range(2):
                        pool.wait_ge(evac, i * 4 + (2 * NFIX + 2 * s + 2))
                        pool.dma_start(T["feat"][bass.ds(i * 2 + (NFIX + s), 1)].rearrange("a p n -> p (a n)"),
                                       feat[:, s, :]).then_inc(stored[s], 16)
                for s in range(2):
                    pool.wait_ge(stored[s], 16 * (stores_before(NFIX + s) + NFIX // 2))

            @block.scalar
            def _(act):
                for t in range(NT):
                    act.wait_ge(x_in[t % XR], 16 * (t // XR + 1))
                    if t:
                        act.wait_ge(squared, t)
                    nc.scalar.activation(sq[:], xt[:, t % XR, :], ACT.Square,
                                         accum_out=ss[:, t:t + 1]).then_inc(squared, 1)
                    act.wait_ge(var, t + 1)
                    nc.scalar.activation(rstd[:, NT + t:NT + t + 1], rstd[:, t:t + 1], ACT.Sqrt).then_inc(rooted, 1)
                    for h in range(2):
                        act.wait_ge(turned, 2 * t + h + 1)
                        nc.scalar.activation(hT_hi[:, 4 * h:4 * h + 4, t * P:(t + 1) * P],
                                             ps_x[:, h, :].rearrange("p (k n) -> p k n", k=4),
                                             ACT.Copy).then_inc(up_hi, 1)

                def split(n, s):
                    act.wait_ge(w_in_[s], n[0])
                    act.wait_ge(product, n[1])
                    nc.scalar.activation(w_hi[:, s], w_raw[:, s], ACT.Copy).then_inc(split_hi, 1)

                def copy_out(s, h, product_at, stored_at, kept=None):
                    act.wait_ge(product, product_at)
                    if stored_at is not None:
                        act.wait_ge(stored[s], stored_at)
                    out = feat[:, s, :] if kept is None else K["tokT"][:, kept, :]
                    nc.scalar.activation(out[:, h * 512:(h + 1) * 512], ps_w[:, h, :], ACT.Copy).then_inc(evac, 1)

                for s in range(2):
                    act.wait_ge(w_in_[s], 16)
                    nc.scalar.activation(w_hi[:, s], w_raw[:, s], ACT.Copy).then_inc(split_hi, 1)
                for n in range(NFIX):
                    kept = n - 4 if FIXED[n][1] is None else None
                    for h in range(2):
                        copy_out(n % 2, h, 2 * n + h + 1, 16 * stores_before(n) or None, kept)
                    split((16 * (n // 2 + 2), 2 * n + 2), n % 2)
                SB = [stores_before(NFIX + s) for s in range(2)]
                with act.Fori(0, NFIX // 2 - 1) as i:
                    for s in range(2):
                        for h in range(2):
                            copy_out(s, h, i * 4 + (2 * NFIX + 2 * s + h + 1), i * 16 + 16 * SB[s])
                        split((i * 16 + 16 * (NFIX // 2 + 2), i * 4 + (2 * NFIX + 2 * s + 2)), s)
                for s in range(2):
                    for h in range(2):
                        copy_out(s, h, 4 * NFIX - 4 + 2 * s + h + 1, 16 * (SB[s] + NFIX // 2 - 1))

                for n in range(3):
                    act.wait_ge(v_in, 16 * (6 if n == 2 else n + 1))
                    if n:
                        act.wait_ge(v_product, NT * n)
                    w = sum(x[1] for x in VCH[n])
                    nc.scalar.activation(v_hi[:, :, 0:w], v_raw[:, :, 0:w], ACT.Copy).then_inc(vs_hi, 1)

            @block.vector
            def _(dve):
                own = Tally(own_dve)
                dve.wait_ge(gain_in, 16)
                for t in range(NT):
                    dve.wait_ge(squared, t + 1)
                    nc.vector.tensor_scalar(rstd[:, t:t + 1], ss[:, t:t + 1], 1.0 / D, EPS, ALU.mult,
                                            ALU.add).then_inc(var, 1)
                    dve.wait_ge(rooted, t + 1)
                    own.inc(nc.vector.reciprocal(rstd[:, t:t + 1], rstd[:, NT + t:NT + t + 1]))
                    own.wait(dve)
                    if t >= 2:
                        dve.wait_ge(turned, 2 * (t - 1))
                    nc.vector.scalar_tensor_tensor(xn[:, t % 2, :], xt[:, t % XR, :], rstd[:, t:t + 1], gain[:],
                                                   ALU.mult, ALU.mult).then_inc(scaled, 1)
                    for h in range(2):
                        dve.wait_ge(up_hi, 2 * t + h + 1)
                        nc.vector.tensor_tensor(hT_lo[:, 4 * h:4 * h + 4, t * P:(t + 1) * P],
                                                ps_x[:, h, :].rearrange("p (k n) -> p k n", k=4),
                                                hT_hi[:, 4 * h:4 * h + 4, t * P:(t + 1) * P].bitcast(F32),
                                                ALU.subtract).then_inc(up_lo, 1)

                def split(s, at):
                    dve.wait_ge(split_hi, at)
                    nc.vector.tensor_tensor(w_lo[:, s], w_raw[:, s], w_hi[:, s].bitcast(F32),
                                            ALU.subtract).then_inc(split_lo, 1)

                for s in range(2):
                    split(s, s + 1)
                halves = 0
                for n, (_, _, rope) in enumerate(FIXED):
                    if rope:
                        for h in range(2):
                            halves += 1
                            dve.wait_ge(rotated, halves)
                            f = feat[:, n % 2, h * 512:(h + 1) * 512]
                            nc.vector.tensor_tensor(turn[:], ps_r[:], sin_t[:, h * 512:(h + 1) * 512],
                                                    ALU.mult).then_inc(turn_made, 1)
                            own.inc(nc.vector.tensor_tensor(f, f, cos_t[:, h * 512:(h + 1) * 512], ALU.mult))
                            own.wait(dve)
                            dve.wait_ge(turn_made, halves)
                            nc.vector.tensor_tensor(f, f, turn[:], ALU.add).then_inc(roped, 1)
                            dve.wait_ge(roped, halves)
                    split(n % 2, n + 3)
                with dve.Fori(0, NFIX // 2 - 1) as i:
                    for s in range(2):
                        split(s, i * 2 + (NFIX + s + 3))

                def v_split(n):
                    w = sum(x[1] for x in VCH[n])
                    dve.wait_ge(vs_hi, n + 1)
                    nc.vector.tensor_tensor(v_lo[:, :, 0:w], v_raw[:, :, 0:w], v_hi[:, :, 0:w].bitcast(F32),
                                            ALU.subtract).then_inc(vs_lo, 1)

                v_split(0)
                for n in range(3):
                    w = sum(x[1] for x in VCH[n])
                    for t in range(NT):
                        dve.wait_ge(v_product, n * NT + t + 1)
                        out = K["vb"][:, t, n * 256:(n + 1) * 256] if n < 2 else K["vsw"][:, t, 0:w]
                        nc.vector.tensor_copy(out, ps_w[:, t % 2, 0:w]).then_inc(v_evac, 1)
                    if n < 2:
                        v_split(n + 1)

            @block.tensor
            def _(pe):
                ident = K["c"][:, K_ID:K_ID + P]
                for t in range(NT):
                    pe.wait_ge(scaled, t + 1)
                    for h in range(2):
                        if t:
                            pe.wait_ge(up_lo, 2 * t + h - 1)
                        for j in range(4):
                            k = 4 * h + j
                            last = nc.tensor.transpose(ps_x[:, h, j * P:(j + 1) * P],
                                                       xn[:, t % 2, k * P:(k + 1) * P], ident)
                        last.then_inc(turned, 1)
                pe.wait_ge(up_lo, 2 * NT)

                def block_of(s, split_at, evac_at):
                    pe.wait_ge(split_hi, split_at)
                    pe.wait_ge(split_lo, split_at)
                    for h in range(2):
                        if evac_at is not None:
                            pe.wait_ge(evac, evac_at + h)
                        for k in range(KD):
                            last = mm3(nc, ps_w[:, h, :], w_hi[:, s, k, :], w_lo[:, s, k, :],
                                       hT_hi[:, k, h * 512:(h + 1) * 512], hT_lo[:, k, h * 512:(h + 1) * 512],
                                       k == 0, k == KD - 1)
                        last.then_inc(product, 1)

                halves = 0
                for n, (_, _, rope) in enumerate(FIXED):
                    block_of(n % 2, n + 1, 2 * n - 1 if n else None)
                    if rope:
                        for h in range(2):
                            pe.wait_ge(evac, 2 * n + h + 1)
                            if halves:
                                pe.wait_ge(turn_made, halves)
                            nc.tensor.matmul(ps_r[:], K["c"][:, K_ROT:K_ROT + P],
                                             feat[:, n % 2, h * 512:(h + 1) * 512], start=True,
                                             stop=True).then_inc(rotated, 1)
                            halves += 1
                with pe.Fori(0, NFIX // 2) as i:
                    for s in range(2):
                        block_of(s, i * 2 + (NFIX + s + 1), i * 4 + (2 * NFIX + 2 * s - 1))
                pe.wait_ge(evac, 4 * NFIX)
                for n in range(3):
                    w = sum(x[1] for x in VCH[n])
                    pe.wait_ge(vs_hi, n + 1)
                    pe.wait_ge(vs_lo, n + 1)
                    for t in range(NT):
                        m = n * NT + t
                        if m >= 2:
                            pe.wait_ge(v_evac, m - 1)
                        for k in range(KD):
                            ts = slice(t * P, (t + 1) * P)
                            last = mm3(nc, ps_w[:, t % 2, 0:w], hT_hi[:, k, ts], hT_lo[:, k, ts],
                                       v_hi[:, k, 0:w], v_lo[:, k, 0:w], k == 0, k == KD - 1)
                        last.then_inc(v_product, 1)


def stage_compress(nc, a, K, T):
    with Scope(nc, "cmp") as sc:
        w1 = sc.sb("w1", [P, 2, CMP_BLOCK, P])
        w2 = sc.sb("w2", [P, 2, HD])
        pe_rows = sc.sb("pe_rows", [CMP_BLOCK, 2, HD])
        peT = sc.sb("peT", [HD, 2, CMP_BLOCK])
        bias = sc.sb("bias", [P, 2])
        hid = sc.sb("hid", [P, 4, 64])
        kc = sc.sb("kc", [P, 64])
        kc_turn = sc.sb("kc_turn", [P, 64])
        kc_dup = sc.sb("kc_dup", [P, GROUPS, 64])
        fT = sc.sb("fT", [NH, S])
        fe = sc.sb("fe", [NH, S])
        ones = sc.sb("ones", [NH, S])
        cum = sc.sb("cum", [NH, S])
        bf = sc.sb("bf", [NH, 1])
        cum_hi = sc.sb("cum_hi", [NH, S], F32R)
        cum_lo = sc.sb("cum_lo", [NH, S], F32R)
        bg = sc.sb("bg", [P, 3 * NH])
        ps_h = sc.ps("ps_h", [P, 4, 512])
        ps_b = sc.ps("ps_b", [P, 512])
        ps_k = sc.ps("ps_k", [P, 512])
        ps_f = sc.ps("ps_f", [P, 1024])
        w1_in, small_in, own_dve, own_act, dup_in, cum_out = (
            sc.sem(n) for n in ("w1_in", "small_in", "own_dve", "own_act", "dup_in", "cum_out"))
        f_turned, f_copied, f_exp, f_ln, cum_made, pe_turned, pe_copied, bias_made, bias_copied = (
            sc.sem(n) for n in ("f_turned", "f_copied", "f_exp", "f_ln", "cum_made", "pe_turned", "pe_copied",
                                "bias_made", "bias_copied"))
        hid_made, hid_act, k_made, k_copied, k_rotated, k_roped, v_made, fe_made = (
            sc.sem(n) for n in ("hid_made", "hid_act", "k_made", "k_copied", "k_rotated", "k_roped", "v_made",
                                "fe_made"))
        g_exp, gate_in = sc.sem("g_exp"), sc.sem("gate_in")
        hid_sig = sc.sem("hid_sig")
        c = K["c"]
        with sc.block() as block:
            @block.sync
            def _(sp):
                for kv, (w, pe_) in enumerate((("w_cmp_k1", "pe_cmp_k"), ("w_cmp_v1", "pe_cmp_v"))):
                    for g in range(GROUPS):
                        sp.dma_start(w1[g * HD:(g + 1) * HD, kv, :, :],
                                     a[w].rearrange("l (j d) n -> (l d) j n", d=HD)).then_inc(w1_in, 16)
                    sp.dma_start(pe_rows[:, kv, :], a[pe_][0]).then_inc(small_in, 16)
                sp.dma_start(w2[:, 0, :], a["w_cmp_k2"][0]).then_inc(small_in, 16)
                sp.dma_start(w2[:, 1, :], a["w_cmp_v2"][0]).then_inc(small_in, 16)
                sp.dma_start(bf[:], a["b_forget"].rearrange("l h -> h l")).then_inc(small_in, 16)
                sp.dma_start(bg[:], a["b_nsa_gate"].to_broadcast((P, 3 * NH))).then_inc(gate_in, 16)
                sp.wait_ge(k_roped, 1)
                for g in range(GROUPS):
                    for half in range(2):
                        sp.dma_start(kc_dup[half * HD:(half + 1) * HD, g, :],
                                     kc[g * HD:(g + 1) * HD, :]).then_inc(dup_in, 16)
                sp.wait_ge(cum_made, 1)
                sp.dma_start(T["cum"][:, 0, :], cum_hi[:].bitcast(F32)).then_inc(cum_out, 16)
                sp.dma_start(T["cum"][:, 1, :], cum_lo[:].bitcast(F32)).then_inc(cum_out, 16)
                sp.wait_ge(cum_out, 32)

            @block.tensor
            def _(pe):
                ident = c[:, K_ID:K_ID + P]
                for t in range(NT):
                    last = nc.tensor.transpose(ps_f[0:NH, t * P:(t + 1) * P], K["vsw"][:, t, 280:288], ident)
                last.then_inc(f_turned, 1)
                pe.wait_ge(small_in, 80)
                for kv in range(2):
                    last = nc.tensor.transpose(ps_b[0:HD, kv * 32:(kv + 1) * 32], pe_rows[:, kv, :],
                                               ident[0:CMP_BLOCK, 0:CMP_BLOCK])
                last.then_inc(pe_turned, 1)
                pe.wait_ge(pe_copied, 1)
                pe.wait_ge(w1_in, 64)
                for kv in range(2):
                    for j in range(CMP_BLOCK):
                        last = nc.tensor.matmul(ps_b[:, 128 + kv:129 + kv], w1[0:HD, kv, j, :],
                                                peT[:, kv, j:j + 1], start=(j == 0), stop=(j == CMP_BLOCK - 1))
                last.then_inc(bias_made, 1)
                for kv in range(2):
                    for g in range(GROUPS):
                        r = slice(g * HD, (g + 1) * HD)
                        for j in range(CMP_BLOCK):
                            tok = K["tokT"][r, kv, j:j + CMP_STRIDE * (N_CMP - 1) + 1:CMP_STRIDE]
                            last = nc.tensor.matmul(ps_h[:, 2 * kv + g, 0:N_CMP], w1[r, kv, j, :], tok,
                                                    start=(j == 0), stop=(j == CMP_BLOCK - 1))
                        last.then_inc(hid_made, 1)
                pe.wait_ge(hid_act, 1)
                for g in range(GROUPS):
                    last = nc.tensor.matmul(ps_k[g * HD:(g + 1) * HD, 0:N_CMP], w2[:, 0, :], hid[:, g, 0:N_CMP],
                                            start=True, stop=True)
                last.then_inc(k_made, 1)
                for g in range(GROUPS):
                    last = nc.tensor.matmul(ps_b[0:N_CMP, 256 + g * HD:256 + (g + 1) * HD], hid[:, 2 + g, 0:N_CMP],
                                            w2[:, 1, :], start=(g == 0), stop=(g == 1), skip_group_check=True)
                last.then_inc(v_made, 1)
                pe.wait_ge(k_copied, 1)
                nc.tensor.matmul(ps_k[:, 256:256 + N_CMP], c[:, K_ROT:K_ROT + P], kc[:, 0:N_CMP], start=True,
                                 stop=True).then_inc(k_rotated, 1)

            @block.scalar
            def _(act):
                act.wait_ge(fe_made, 1)
                nc.scalar.activation(fe[:], fe[:], ACT.Exp).then_inc(f_exp, 1)
                act.wait_ge(gate_in, 17)
                nc.scalar.activation(K["gate"][:], K["gate"][:], ACT.Exp, scale=-1.0).then_inc(g_exp, 1)
                act.wait_ge(f_exp, 1)
                nc.scalar.activation(fe[:], fe[:], ACT.Ln, bias=1.0).then_inc(f_ln, 1)
                act.wait_ge(bias_copied, 1)
                act.wait_ge(hid_made, 4)
                for n in range(4):
                    last = nc.scalar.activation(hid[:, n, 0:N_CMP], ps_h[:, n, 0:N_CMP], ACT.Sigmoid,
                                                bias=bias[:, n // 2:n // 2 + 1])
                last.then_inc(hid_sig, 1)

            @block.vector
            def _(dve):
                own = Tally(own_dve)

                def step(ins):
                    own.inc(ins)
                    own.wait(dve)

                own.inc(nc.vector.memset(ones[:], 1.0))
                own.inc(nc.vector.memset(K["vc"][:], 0.0))
                own.inc(nc.vector.memset(K["kc_raw"][:], 0.0))
                own.inc(nc.vector.memset(kc[:], 0.0))
                dve.wait_ge(small_in, 80)
                dve.wait_ge(f_turned, 1)
                step(nc.vector.tensor_scalar(fT[:], ps_f[0:NH, :], bf[:, 0:1], None, ALU.add))
                step(nc.vector.tensor_scalar(fe[:], fT[:], -1.0, None, ALU.mult))
                step(nc.vector.tensor_tensor(fe[:], fe[:], fT[:], ALU.min))
                nc.vector.tensor_scalar(fT[:], fT[:], 0.0, None, ALU.min).then_inc(fe_made, 1)
                dve.wait_ge(gate_in, 16)
                nc.vector.tensor_tensor(K["gate"][:], K["vsw"][:, :, 256:280],
                                        bg[:].unsqueeze(1).to_broadcast((P, NT, 3 * NH)),
                                        ALU.add).then_inc(gate_in, 1)
                dve.wait_ge(pe_turned, 1)
                nc.vector.tensor_copy(peT[:], ps_b[0:HD, 0:2 * CMP_BLOCK].rearrange("p (a j) -> p a j", a=2)
                                      ).then_inc(pe_copied, 1)
                dve.wait_ge(g_exp, 1)
                step(nc.vector.tensor_scalar(K["gate"][:], K["gate"][:], 1.0, None, ALU.add))
                step(nc.vector.reciprocal(K["gate"][:], K["gate"][:]))
                dve.wait_ge(f_ln, 1)
                dve.wait_ge(fe_made, 1)
                step(nc.vector.tensor_tensor(fT[:], fT[:], fe[:], ALU.subtract))
                step(nc.vector.tensor_tensor_scan(cum[:], ones[:], fT[:], 0.0, ALU.mult, ALU.add))
                step(nc.vector.tensor_scalar(cum[:], cum[:], -1.0 / SCALE, None, ALU.mult))
                step(nc.vector.tensor_copy(cum_hi[:], cum[:]))
                nc.vector.tensor_tensor(cum_lo[:], cum[:], cum_hi[:].bitcast(F32), ALU.subtract).then_inc(cum_made, 1)
                dve.wait_ge(bias_made, 1)
                nc.vector.tensor_copy(bias[:], ps_b[:, 128:130]).then_inc(bias_copied, 1)
                dve.wait_ge(bias_copied, 1)
                dve.wait_ge(hid_sig, 1)
                for n in range(4):
                    last = nc.vector.scalar_tensor_tensor(hid[:, n, 0:N_CMP], ps_h[:, n, 0:N_CMP],
                                                          bias[:, n // 2:n // 2 + 1], hid[:, n, 0:N_CMP],
                                                          ALU.add, ALU.mult)
                last.then_inc(hid_act, 1)
                dve.wait_ge(k_made, 1)
                nc.vector.tensor_copy(kc[:, 0:N_CMP], ps_k[:, 0:N_CMP]).then_inc(k_copied, 1)
                dve.wait_ge(k_copied, 1)
                dve.wait_ge(v_made, 1)
                step(nc.vector.tensor_copy(K["vc"][0:N_CMP, :, :],
                                           ps_b[0:N_CMP, 256:384].rearrange("p (g d) -> p g d", g=GROUPS)))
                dve.wait_ge(k_rotated, 1)
                ends = slice(CMP_BLOCK - 1, CMP_BLOCK + CMP_STRIDE * (N_CMP - 1), CMP_STRIDE)
                step(nc.vector.tensor_tensor(kc_turn[:, 0:N_CMP], ps_k[:, 256:256 + N_CMP], K["sin"][:, ends], ALU.mult))
                step(nc.vector.tensor_tensor(kc[:, 0:N_CMP], kc[:, 0:N_CMP], K["cos"][:, ends], ALU.mult))
                nc.vector.tensor_tensor(kc[:, 0:N_CMP], kc[:, 0:N_CMP], kc_turn[:, 0:N_CMP], ALU.add
                                        ).then_inc(k_roped, 1)
                dve.wait_ge(dup_in, 64)
                step(nc.vector.tensor_copy(K["kc_raw"][:, :, 0:64], kc_dup[:]))
                step(nc.vector.tensor_copy(K["kc_hi"][:], K["kc_raw"][:]))
                step(nc.vector.tensor_tensor(K["kc_lo"][:], K["kc_raw"][:], K["kc_hi"][:].bitcast(F32), ALU.subtract))


class Soft:

    def __init__(self, at, blocks, gate):
        self.at, self.blocks, self.gate = at, blocks, gate


def attention_steps(sparse):
    steps = []
    for qt in range(NT):
        full = [("k", kt, "diag" if kt == qt else None) for kt in range(qt + 1)]
        steps.append((qt, full, [Soft(0, [("v", kt) for kt in range(qt + 1)], 1)]))
        if sparse:
            lo = max(0, qt - WB)
            near = [("w", kt, "diag" if kt == qt else "far" if kt == qt - WB else None) for kt in range(lo, qt + 1)]
            steps.append((qt, near + [("c", 0, ("cmp", qt))],
                          [Soft(0, [("vw", kt) for kt in range(lo, qt + 1)], 2), Soft(len(near), [("vc", 0)], 0)]))
    return steps


def stage_attention(nc, K, T, sparse):
    name = "nsa" if sparse else "fox"
    with Scope(nc, name) as sc:
        q_raw = [sc.sb(f"q_raw{s}", [P, S]) for s in range(2)]
        q_st = [sc.sb(f"q_st{s}", [P, S], F32R) for s in range(2)]
        q_tmp = sc.sb("q_tmp", [P, S], F32R)
        NK = GROUPS if sparse else 2
        k_raw = [sc.sb(f"k_raw{s}", [P, S]) for s in range(NK)]
        k_hi = [sc.sb(f"k_hi{s}", [P, S], F32R) for s in range(NK)]
        k_lo = [sc.sb(f"k_lo{s}", [P, S], F32R) for s in range(NK)]
        if sparse:
            w_hi = [sc.sb(f"w_hi{s}", [P, S], F32R) for s in range(NK)]
            w_lo = [sc.sb(f"w_lo{s}", [P, S], F32R) for s in range(NK)]
            gate_h = [sc.sb(f"gate_h{s}", [P, NT, 3]) for s in range(2)]
        else:
            v_h = [sc.sb(f"v_h{s}", [P, NT, HD]) for s in range(2)]
            cum_k = [sc.sb(f"cum_k{s}", [P, S], F32R) for s in range(2)]
            sel2 = sc.sb("sel2", [P, P], F32R)
        prob = sc.sb("prob", [P, 2, S])
        probT = sc.sb("probT", [P, 2, 4, P])
        o_h = [sc.sb(f"o_h{s}", [P, NT, HD]) for s in range(2)]
        mx = sc.sb("mx", [P, 2, 2])
        sums = sc.sb("sums", [P, 4, 2])
        wt = sc.sb("wt", [P, 4, 2])
        ps_s = sc.ps("ps_s", [P, 2, 1024])
        ps_t = sc.ps("ps_t", [P, 2, 512])
        ps_o = sc.ps("ps_o", [P, 2, 512])

        q_in = [sc.sem(f"q_in{s}") for s in range(2)]
        k_in = [sc.sem(f"k_in{s}") for s in range(2)]
        head_ready, head_done, o_kept, o_made = (
            [sc.sem(f"{n}{s}") for s in range(2)] for n in ("head_ready", "head_done", "o_kept", "o_made"))
        scored, maxed, expd, turned, weighed = (
            sc.sem(n) for n in ("scored", "maxed", "expd", "turned", "weighed"))
        evac = [sc.sem(f"evac{b}") for b in range(2)]
        passed = sc.sem("passed")
        pv_group, own_pool, own_dve, k_ready, k_rounded = (
            sc.sem(n) for n in ("pv_group", "own_pool", "own_dve", "k_ready", "k_rounded"))

        one = attention_steps(sparse)
        steps = [(s, *x) for s in range(2) for x in one]
        N = len(steps)
        groups = []
        for n, (s, qt, cols, softs) in enumerate(steps):
            for b in range(0, len(cols), 4):
                groups.append((n, b, min(4, len(cols) - b)))
        NGR = len(groups)
        assert NGR % 2 == 0
        first_group = [min(i for i, g in enumerate(groups) if g[0] == n) for n in range(N)] + [NGR]
        TURNS = NH // 2
        runs = [(0, 0, 2), (1, 2, 4)] if sparse else [(None, 0, TURNS)]
        head0 = 0 if sparse else NH

        def feat_rows(row, half):
            return T["feat"][row, half * HD:(half + 1) * HD, :]

        with sc.block() as block:
            @block.sync
            def _(sp):
                if sparse:
                    for w in range(2):
                        for g in range(GROUPS):
                            if w:
                                sp.wait_ge(k_ready, g + 1)
                            for half in range(2):
                                sp.dma_start(k_raw[g][half * HD:(half + 1) * HD, :],
                                             feat_rows(6 + w, g)).then_inc(k_in[g], 16)
                def load_raw(s, it):
                    for row0, dst in ((0 if sparse else 8, q_raw[s]),) + (() if sparse else ((12, k_raw[s]),)):
                        row = T["feat"][bass.ds(it + row0, 1)].rearrange("a p n -> p (a n)")
                        for half in range(2):
                            sp.dma_start(dst[half * HD:(half + 1) * HD, :],
                                         row[s * HD:(s + 1) * HD, :]).then_inc(q_in[s], 16)

                def load_cum(s, it):
                    sp.dma_start(cum_k[s][0:2, :].bitcast(F32),
                                 T["cum"][bass.ds(it * 2 + s, 1)].rearrange("a b n -> (a b) n")).then_inc(k_in[s], 16)

                for s in range(2):
                    load_raw(s, 0)
                if not sparse:
                    sp.wait_ge(own_dve, 3)
                    for s in range(2):
                        load_cum(s, 0)
                with sp.Fori(1, TURNS) as it:
                    for s in range(2):
                        sp.wait_ge(head_ready[s], it)
                        load_raw(s, it)
                    if not sparse:
                        for s in range(2):
                            sp.wait_ge(head_done[s], it)
                            load_cum(s, it)

            @block.gpsimd
            def _(pool):
                for s in range(2):
                    pool.sem_inc(o_kept[s], 1)
                base0 = 0
                PER = 3 if sparse else 5

                def prepare(s, it):
                    own = Tally(own_pool, it * (2 * PER) + (base0 + s * PER))
                    q_bytes = 32 if sparse else 64
                    wait_alone(pool, q_in[s], it * q_bytes + q_bytes, passed)
                    own.inc(nc.gpsimd.tensor_copy(q_tmp[:], q_raw[s][:]))
                    wait_alone(pool, own.sem, own.base + own.n, passed)
                    own.inc(nc.gpsimd.tensor_copy(q_st[s][0:HD, :], q_tmp[0:HD, :].bitcast(F32)))
                    if sparse:
                        own.inc(nc.gpsimd.tensor_copy(gate_h[s][:], K["gate"][:, :, bass.ds(it * 6 + s * 3, 3)]))
                    else:
                        own.inc(nc.gpsimd.tensor_copy(k_hi[s][:], k_raw[s][:]))
                        wait_alone(pool, own.sem, own.base + own.n, passed)
                        own.inc(nc.gpsimd.tensor_tensor(k_lo[s][:], k_raw[s][:], k_hi[s][:].bitcast(F32),
                                                        ALU.subtract))
                        own.inc(nc.gpsimd.tensor_copy(v_h[s][:], K["vb"][:, :, bass.ds(it * (2 * HD) + s * HD, HD)]))
                    wait_alone(pool, own.sem, own.base + own.n, passed)
                    nc.gpsimd.tensor_tensor(q_st[s][HD:P, :], q_raw[s][HD:P, :], q_tmp[HD:P, :].bitcast(F32),
                                            ALU.subtract).then_inc(head_ready[s], 1)
                    wait_alone(pool, head_ready[s], it + 1, passed)

                def keep(s, it):
                    wait_alone(pool, o_made[s], it + 1, passed)
                    nc.gpsimd.tensor_copy(K["o"][:, :, bass.ds(it * (2 * HD) + (head0 * HD + s * HD), HD)],
                                          o_h[s][:]).then_inc(o_kept[s], 1)

                for s in range(2):
                    prepare(s, 0)
                with pool.Fori(0, TURNS - 1) as it:
                    for s in range(2):
                        keep(s, it)
                        wait_alone(pool, head_done[s], it + 1, passed)
                        prepare(s, it + 1)
                for s in range(2):
                    keep(s, TURNS - 1)
                    pool.wait_ge(o_kept[s], TURNS + 1)

            def turns(eng, body):
                for g, a0, a1 in runs:
                    with eng.Fori(a0, a1) as it:
                        body(g, it)

            @block.tensor
            def _(pe):
                ident = K["c"][:, K_ID:K_ID + P]
                if sparse:
                    pe.wait_ge(k_ready, 2 * GROUPS)
                if not sparse:
                    pe.wait_ge(own_dve, 3)

                def scores(g, it, n):
                    s, qt, cols, softs = steps[n]
                    if n % len(one) == 0:
                        pe.wait_ge(head_ready[s], it + 1)
                        if not sparse:
                            pe.wait_ge(k_in[s], it * 16 + 16)
                    pe.wait_ge(expd, it * N + (n - 1 if n >= 2 else 0) + 1)
                    q = q_st[s][:, qt * P:(qt + 1) * P]
                    pieces, b = [], 0
                    while b < len(cols):
                        e = b + 1
                        while e < len(cols) and e % 4 and cols[e][0] == cols[b][0]:
                            e += 1
                        pieces.append((b, e))
                        b = e
                    started = set()
                    for i, (b, e) in enumerate(pieces):
                        src, kt, _ = cols[b]
                        out = ps_s[:, n % 2, b * P:e * P]
                        ks = slice(kt * P, (kt + e - b) * P)
                        kk = g if sparse else s
                        if src == "k":
                            parts = (k_hi[kk][:, ks], k_lo[kk][:, ks])
                        elif src == "w":
                            parts = (w_hi[kk][:, ks], w_lo[kk][:, ks])
                        else:
                            parts = (K["kc_hi"][:, kk, :], K["kc_lo"][:, kk, :])
                        bank = b // 4
                        masks = [(j, cols[j][2]) for j in range(b, e) if cols[j][2]]
                        lastpiece = i + 1 == len(pieces) or pieces[i + 1][0] // 4 != bank
                        last = nc.tensor.matmul(out, q, parts[0], start=bank not in started, stop=False,
                                                skip_group_check=True)
                        started.add(bank)
                        last = nc.tensor.matmul(out, q, parts[1], start=False,
                                                stop=lastpiece and not masks and sparse, skip_group_check=True)
                        if not sparse:
                            last = nc.tensor.matmul(out, sel2[:], cum_k[s][:, ks], start=False,
                                                    stop=lastpiece and not masks, skip_group_check=True)
                        for m, (j, kind) in enumerate(masks):
                            col = 0 if kind == "diag" else P if kind == "far" else (2 + kind[1]) * P
                            last = nc.tensor.matmul(ps_s[:, n % 2, j * P:(j + 1) * P], K["identb"][:],
                                                    K["maskb"][:, col:col + P], start=False,
                                                    stop=lastpiece and m == len(masks) - 1, skip_group_check=True)
                    last.then_inc(scored, 1)

                def turn_group(g, it, gr):
                    n, b, w = groups[gr]
                    pe.wait_ge(evac[gr % 2], it * (NGR // 2) + (gr // 2) + 1)
                    for j in range(w):
                        last = nc.tensor.transpose(ps_t[:, gr % 2, j * P:(j + 1) * P],
                                                   prob[:, n % 2, (b + j) * P:(b + j + 1) * P], ident)
                    last.then_inc(turned, 1)

                def values(g, it, gr):
                    n, b, w = groups[gr]
                    s, qt, cols, softs = steps[n]
                    pe.wait_ge(evac[gr % 2], it * (NGR // 2) + (gr // 2) + 2)
                    if gr == first_group[n]:
                        pe.wait_ge(weighed, it * N + (n - 1 if n >= 2 else 0) + 1)
                    for j in range(w):
                        blk = b + j
                        i = max(k for k, so in enumerate(softs) if so.at <= blk)
                        src, kt = softs[i].blocks[blk - softs[i].at]
                        if src == "v":
                            val = K["vsw"][:, kt, g * HD:(g + 1) * HD] if sparse else v_h[s][:, kt, :]
                        elif src == "vw":
                            val = K["vsw"][:, kt, 128 + g * HD:128 + (g + 1) * HD]
                        else:
                            val = K["vc"][:, g, :]
                        last = nc.tensor.matmul(ps_o[:, n % 2, i * HD:(i + 1) * HD], probT[:, gr % 2, j, :], val,
                                                start=(blk == 0), stop=(blk == softs[i].at + len(softs[i].blocks) - 1),
                                                skip_group_check=True)
                    last.then_inc(pv_group, 1)

                def body(g, it):
                    scores(g, it, 0)
                    scores(g, it, 1)
                    for n in range(N):
                        pe.wait_ge(expd, it * N + (n + 2))
                        a0, a1 = first_group[n], first_group[n + 1]
                        for gr in range(a0, a1):
                            turn_group(g, it, gr)
                        if n + 2 < N:
                            scores(g, it, n + 2)
                        for gr in range(a0, a1):
                            values(g, it, gr)
                        if n % len(one) == len(one) - 1:
                            pe.wait_ge(pv_group, it * NGR + a1)
                            pe.sem_inc(head_done[steps[n][0]], 1)

                turns(pe, body)

            def copy_group(eng, it, gr, copy):
                n, b, w = groups[gr]
                eng.wait_ge(turned, it * NGR + (gr + 1))
                if gr >= 2:
                    eng.wait_ge(pv_group, it * NGR + (gr - 1))
                copy(probT[:, gr % 2, 0:w, :], ps_t[:, gr % 2, 0:w * P].rearrange("p (j n) -> p j n", n=P)
                     ).then_inc(evac[gr % 2], 1)

            @block.scalar
            def _(act):
                act.sem_inc(expd, 1)
                act.sem_inc(evac[1], 1)
                if sparse:
                    for w in range(2):
                        for g in range(GROUPS):
                            act.wait_ge(k_in[g], 32 * (w + 1))
                            nc.scalar.activation((w_hi if w else k_hi)[g][:], k_raw[g][:],
                                                 ACT.Copy).then_inc(k_rounded, 1)

                def exps(it, n):
                    s, qt, cols, softs = steps[n]
                    act.wait_ge(maxed, it * N + (n + 1))
                    if n >= 2:
                        act.wait_ge(turned, it * NGR + first_group[n - 1])
                    for i, so in enumerate(softs):
                        r = slice(so.at * P, (so.at + len(so.blocks)) * P)
                        last = nc.scalar.activation(prob[:, n % 2, r], ps_s[:, n % 2, r], ACT.Exp,
                                                    bias=mx[:, n % 2, i:i + 1], scale=SCALE,
                                                    accum_out=sums[:, n % 4, i:i + 1])
                    last.then_inc(expd, 1)

                def body(g, it):
                    exps(it, 0)
                    exps(it, 1)
                    for n in range(N):
                        for gr in range(first_group[n], first_group[n + 1]):
                            if gr % 2 == 1:
                                copy_group(act, it, gr, lambda o, x: nc.scalar.activation(o, x, ACT.Copy))
                        if n + 2 < N:
                            exps(it, n + 2)

                turns(act, body)

            @block.vector
            def _(dve):
                dve.sem_inc(evac[0], 1)
                dve.sem_inc(weighed, 1)
                if sparse:
                    for w in range(2):
                        for g in range(GROUPS):
                            hi, lo = (w_hi, w_lo) if w else (k_hi, k_lo)
                            dve.wait_ge(k_rounded, 2 * w + g + 1)
                            nc.vector.tensor_tensor(lo[g][:], k_raw[g][:], hi[g][:].bitcast(F32),
                                                    ALU.subtract).then_inc(k_ready, 1)
                if not sparse:
                    nc.vector.tensor_copy(sel2[:], K["c"][:, K_ONE:K_ONE + P]).then_inc(own_dve, 1)
                    for s in range(2):
                        nc.vector.tensor_scalar(cum_k[s][:], K["cos"][:], 0.0, None, ALU.mult).then_inc(own_dve, 1)

                OWN0 = 0 if sparse else 3

                def max_of(it, n, own):
                    s, qt, cols, softs = steps[n]
                    dve.wait_ge(scored, it * N + (n + 1))
                    if n >= 2:
                        dve.wait_ge(expd, it * N + n)
                    else:
                        dve.wait_ge(expd, it * N + 1)
                    for i, so in enumerate(softs):
                        r = slice(so.at * P, (so.at + len(so.blocks)) * P)
                        last = nc.vector.tensor_reduce(mx[:, n % 2, i:i + 1], ps_s[:, n % 2, r], X, ALU.max)
                    own.inc(last)
                    own.wait(dve)
                    k = len(softs)
                    nc.vector.tensor_scalar(mx[:, n % 2, 0:k], mx[:, n % 2, 0:k], -SCALE, None,
                                            ALU.mult).then_inc(maxed, 1)

                def weigh(it, n, own):
                    s, qt, cols, softs = steps[n]
                    k = len(softs)
                    dve.wait_ge(pv_group, it * NGR + first_group[n + 1])
                    own.inc(nc.vector.reciprocal(wt[:, n % 4, 0:k], sums[:, n % 4, 0:k]))
                    own.wait(dve)
                    o = o_h[s][:, qt, :]
                    if not sparse:
                        if n % len(one) == 0:
                            dve.wait_ge(o_kept[s], it + 1)
                        last = nc.vector.tensor_scalar(o, ps_o[:, n % 2, 0:HD], wt[:, n % 4, 0:1], None, ALU.mult)
                        last.then_inc(weighed, 1)
                    else:
                        for i, so in enumerate(softs):
                            gt = gate_h[s][:, qt, so.gate:so.gate + 1]
                            last = nc.vector.tensor_tensor(wt[:, n % 4, i:i + 1], wt[:, n % 4, i:i + 1], gt, ALU.mult)
                        own.inc(last)
                        own.wait(dve)
                        if k == 2 and qt == 0:
                            own.inc(nc.vector.tensor_tensor(wt[:, n % 4, 1:2], wt[:, n % 4, 1:2],
                                                            K["c"][:, K_VALID:K_VALID + 1], ALU.mult))
                            own.wait(dve)
                        if k == 1:
                            if n % len(one) == 0:
                                dve.wait_ge(o_kept[s], it + 1)
                            last = nc.vector.tensor_scalar(o, ps_o[:, n % 2, 0:HD], wt[:, n % 4, 0:1], None, ALU.mult)
                            last.then_inc(weighed, 1)
                        else:
                            dve.wait_ge(weighed, it * N + (n + 1))
                            own.inc(nc.vector.scalar_tensor_tensor(o, ps_o[:, n % 2, 0:HD], wt[:, n % 4, 0:1], o,
                                                                   ALU.mult, ALU.add))
                            own.wait(dve)
                            last = nc.vector.scalar_tensor_tensor(o, ps_o[:, n % 2, HD:2 * HD], wt[:, n % 4, 1:2], o,
                                                                  ALU.mult, ALU.add)
                            last.then_inc(weighed, 1)
                    if n % len(one) == len(one) - 1:
                        dve.wait_ge(weighed, it * N + (n + 2))
                        dve.sem_inc(o_made[s], 1)

                def plan(own, it):
                    max_of(it, 0, own)
                    max_of(it, 1, own)
                    for n in range(N):
                        for gr in range(first_group[n], first_group[n + 1]):
                            if gr % 2 == 0:
                                copy_group(dve, it, gr, nc.vector.tensor_copy)
                        if n:
                            weigh(it, n - 1, own)
                        if n + 2 < N:
                            max_of(it, n + 2, own)
                    weigh(it, N - 1, own)

                OWN = 2 * N if not sparse else 2 * N + N + N // 2 + 2

                def body(g, it):
                    own = Tally(own_dve, it * OWN + OWN0)
                    plan(own, it)
                    assert own.n == OWN, (own.n, OWN)

                turns(dve, body)


def stage_mix(nc, a, K, T):
    with Scope(nc, "mix") as sc:
        HALF = NH * HD
        w_raw = sc.sb("w_raw", [P, 2, D])
        w_hi = sc.sb("w_hi", [P, KD, D], F32R)
        w_lo = sc.sb("w_lo", [P, KD, D], F32R)
        beta = sc.sb("beta", [P, D])
        gain = sc.sb("gain", [P, D])
        w_rt = sc.sb("w_rt", [P, KD, NG + NE])
        b_rt = sc.sb("b_rt", [1, NG + NE])
        junk = sc.sb("junk", [P, D], BF16)
        ss = sc.sb("ss", [P, NT, 3])
        rt = sc.sb("rt", [P, NT, 3])
        rs = sc.sb("rs", [P, NT, 3])
        xt = sc.sb("x", [P, 2, D])
        mT_hi = sc.sb("mT_hi", [P, 2, KD, P], F32R)
        mT_lo = sc.sb("mT_lo", [P, 2, KD, P], F32R)
        ht = sc.sb("h", [P, 2, D])
        ut = sc.sb("u", [P, 2, D])
        uT = sc.sb("uT", [P, KD, P])
        ps_x = sc.ps("ps_x", [P, 2, 512])
        ps_y = sc.ps("ps_y", [P, 2, 512])
        ps_u = sc.ps("ps_u", [P, 2, 512])
        ps_l = sc.ps("ps_l", [P, 512])
        w_in = [sc.sem(f"w_in{i}") for i in range(2)]
        x_in = [sc.sem(f"x_in{i}") for i in range(2)]
        h_out = [sc.sem(f"h_out{i}") for i in range(2)]
        u_out = [sc.sem(f"u_out{i}") for i in range(2)]
        (vec_in, rt_in, split_hi, split_lo, o_sq, o_var, o_root, o_norm, turned, m_hi, m_lo, product, h_made, h_sq,
         h_var, h_root, u_made, u_turned, u_copied, logits, own_dve) = (
            sc.sem(n) for n in ("vec_in", "rt_in", "split_hi", "split_lo", "o_sq", "o_var", "o_root", "o_norm",
                                "turned", "m_hi", "m_lo", "product", "h_made", "h_sq", "h_var", "h_root", "u_made",
                                "u_turned", "u_copied", "logits", "own_dve"))
        x_d = a["x"].rearrange("b (t p) d -> (b t) p d", p=P)
        w_d = a["w_out"].rearrange("l (k p) n -> (l k) p n", p=P)
        with sc.block() as block:
            @block.sync
            def _(sp):
                sp.dma_start(beta[:, 0:HALF], a["beta_nsa"].to_broadcast((P, HALF))).then_inc(vec_in, 16)
                sp.dma_start(beta[:, HALF:D], a["beta_fox"].to_broadcast((P, HALF))).then_inc(vec_in, 16)
                sp.dma_start(gain[:], a["g_ffn"].to_broadcast((P, D))).then_inc(vec_in, 16)
                for k in range(KD):
                    if k >= 2:
                        sp.wait_ge(split_hi, k - 1)
                        sp.wait_ge(split_lo, k - 1)
                    sp.dma_start(w_raw[:, k % 2, :], w_d[k]).then_inc(w_in[k % 2], 16)
                    if k < 2:
                        sp.dma_start(xt[:, k, :], x_d[k]).then_inc(x_in[k], 16)
                sp.dma_start(w_rt[:, :, 0:NG], a["w_group"].rearrange("l (k p) n -> (l p) k n", p=P)).then_inc(rt_in, 16)
                sp.dma_start(w_rt[:, :, NG:], a["w_router"].rearrange("l (k p) n -> (l p) k n", p=P)).then_inc(rt_in, 16)
                sp.dma_start(b_rt[:, 0:NG], a["b_group"]).then_inc(rt_in, 16)
                sp.dma_start(b_rt[:, NG:], a["b_router"]).then_inc(rt_in, 16)
                for t in range(NT):
                    sp.wait_ge(h_made, 2 * t + 2)
                    sp.dma_start(T["h"][t], ht[:, t % 2, :]).then_inc(h_out[t % 2], 16)
                    if t + 2 < NT:
                        sp.dma_start(xt[:, t % 2, :], x_d[t + 2]).then_inc(x_in[t % 2], 16)
                    sp.wait_ge(u_made, t + 1)
                    sp.dma_start(T["u"][t * P:(t + 1) * P, :], ut[:, t % 2, :]).then_inc(u_out[t % 2], 16)
                for s in range(2):
                    sp.wait_ge(h_out[s], 16 * (NT // 2))
                    sp.wait_ge(u_out[s], 16 * (NT // 2))

            def tiles(norm, turn, mix, route, split):
                norm(0)
                split()
                for i in range(NT + 2):
                    if i + 1 < NT:
                        norm(i + 1)
                    if i < NT:
                        turn(i)
                    if 1 <= i <= NT:
                        mix(i - 1)
                    if i >= 2:
                        route(i - 2)

            @block.scalar
            def _(act):
                def split():
                    for k in range(KD):
                        act.wait_ge(w_in[k % 2], 16 * (k // 2 + 1))
                        nc.scalar.activation(w_hi[:, k, :], w_raw[:, k % 2, :], ACT.Copy).then_inc(split_hi, 1)

                def norm(t):
                    for g in range(2):
                        nc.scalar.activation(junk[:, g * HALF:(g + 1) * HALF],
                                             K["o"][:, t, g * HALF:(g + 1) * HALF], ACT.Square,
                                             accum_out=ss[:, t, g:g + 1]).then_inc(o_sq, 1)
                    act.wait_ge(o_var, t + 1)
                    nc.scalar.activation(rt[:, t, 0:2], rt[:, t, 0:2], ACT.Sqrt).then_inc(o_root, 1)

                def turn(t):
                    for h in range(2):
                        act.wait_ge(turned, 2 * t + h + 1)
                        if t >= 2:
                            act.wait_ge(product, t - 1)
                        nc.scalar.activation(mT_hi[:, t % 2, 4 * h:4 * h + 4, :],
                                             ps_x[:, h, :].rearrange("p (k n) -> p k n", k=4),
                                             ACT.Copy).then_inc(m_hi, 1)

                def mix(t):
                    act.wait_ge(h_made, 2 * t + 2)
                    nc.scalar.activation(junk[:], ht[:, t % 2, :], ACT.Square,
                                         accum_out=ss[:, t, 2:3]).then_inc(h_sq, 1)
                    act.wait_ge(h_var, t + 1)
                    nc.scalar.activation(rt[:, t, 2:3], rt[:, t, 2:3], ACT.Sqrt).then_inc(h_root, 1)

                def route(t):
                    for h in range(2):
                        act.wait_ge(u_turned, 2 * t + h + 1)
                        if t:
                            act.wait_ge(logits, t)
                        nc.scalar.activation(uT[:, 4 * h:4 * h + 4, :],
                                             ps_u[:, h, :].rearrange("p (k n) -> p k n", k=4),
                                             ACT.Copy).then_inc(u_copied, 1)

                tiles(norm, turn, mix, route, split)

            @block.vector
            def _(dve):
                own = Tally(own_dve)

                def split():
                    for k in range(KD):
                        dve.wait_ge(split_hi, k + 1)
                        nc.vector.tensor_tensor(w_lo[:, k, :], w_raw[:, k % 2, :], w_hi[:, k, :].bitcast(F32),
                                                ALU.subtract).then_inc(split_lo, 1)

                dve.wait_ge(vec_in, 48)

                def norm(t):
                    dve.wait_ge(o_sq, 2 * t + 2)
                    nc.vector.tensor_scalar(rt[:, t, 0:2], ss[:, t, 0:2], 1.0 / HALF, EPS, ALU.mult,
                                            ALU.add).then_inc(o_var, 1)
                    dve.wait_ge(o_root, t + 1)
                    own.inc(nc.vector.reciprocal(rs[:, t, 0:2], rt[:, t, 0:2]))
                    own.wait(dve)
                    for g in range(2):
                        og = K["o"][:, t, g * HALF:(g + 1) * HALF]
                        nc.vector.scalar_tensor_tensor(og, og, rs[:, t, g:g + 1], beta[:, g * HALF:(g + 1) * HALF],
                                                       ALU.mult, ALU.mult).then_inc(o_norm, 1)

                def turn(t):
                    for h in range(2):
                        dve.wait_ge(m_hi, 2 * t + h + 1)
                        nc.vector.tensor_tensor(mT_lo[:, t % 2, 4 * h:4 * h + 4, :],
                                                ps_x[:, h, :].rearrange("p (k n) -> p k n", k=4),
                                                mT_hi[:, t % 2, 4 * h:4 * h + 4, :].bitcast(F32),
                                                ALU.subtract).then_inc(m_lo, 1)

                def mix(t):
                    dve.wait_ge(product, t + 1)
                    dve.wait_ge(x_in[t % 2], 16 * (t // 2 + 1))
                    if t >= 2:
                        dve.wait_ge(h_out[t % 2], 16 * (t // 2))
                    for h in range(2):
                        r = slice(h * 512, (h + 1) * 512)
                        nc.vector.tensor_tensor(ht[:, t % 2, r], ps_y[:, h, :], xt[:, t % 2, r],
                                                ALU.add).then_inc(h_made, 1)
                    dve.wait_ge(h_sq, t + 1)
                    nc.vector.tensor_scalar(rt[:, t, 2:3], ss[:, t, 2:3], 1.0 / D, EPS, ALU.mult,
                                            ALU.add).then_inc(h_var, 1)
                    dve.wait_ge(h_root, t + 1)
                    own.inc(nc.vector.reciprocal(rs[:, t, 2:3], rt[:, t, 2:3]))
                    own.wait(dve)
                    if t >= 2:
                        dve.wait_ge(u_out[t % 2], 16 * (t // 2))
                        dve.wait_ge(u_turned, 2 * (t - 1))
                    nc.vector.scalar_tensor_tensor(ut[:, t % 2, :], ht[:, t % 2, :], rs[:, t, 2:3], gain[:],
                                                   ALU.mult, ALU.mult).then_inc(u_made, 1)

                def route(t):
                    pass

                tiles(norm, turn, mix, route, split)
                dve.wait_ge(logits, NT)
                own.inc(nc.vector.tensor_copy(K["lg"][:], ps_l[:, 0:NT * (NG + NE)].rearrange("p (t n) -> p t n", t=NT)))
                own.wait(dve)

            @block.tensor
            def _(pe):
                ident = K["c"][:, K_ID:K_ID + P]

                def norm(t):
                    pass

                def split():
                    pass

                def turn(t):
                    pe.wait_ge(o_norm, 2 * t + 2)
                    for h in range(2):
                        if t:
                            pe.wait_ge(m_lo, 2 * t + h - 1)
                        for j in range(4):
                            k = 4 * h + j
                            last = nc.tensor.transpose(ps_x[:, h, j * P:(j + 1) * P],
                                                       K["o"][:, t, k * P:(k + 1) * P], ident)
                        last.then_inc(turned, 1)

                def mix(t):
                    pe.wait_ge(m_lo, 2 * t + 2)
                    if t:
                        pe.wait_ge(h_made, 2 * t)
                    for h in range(2):
                        for k in range(KD):
                            if t == 0 and h == 0:
                                pe.wait_ge(split_lo, k + 1)
                            last = mm3(nc, ps_y[:, h, :], mT_hi[:, t % 2, k, :], mT_lo[:, t % 2, k, :],
                                       w_hi[:, k, h * 512:(h + 1) * 512], w_lo[:, k, h * 512:(h + 1) * 512],
                                       k == 0, k == KD - 1)
                    last.then_inc(product, 1)

                def route(t):
                    pe.wait_ge(u_made, t + 1)
                    for h in range(2):
                        if t:
                            pe.wait_ge(u_copied, 2 * t + h - 1)
                        for j in range(4):
                            k = 4 * h + j
                            last = nc.tensor.transpose(ps_u[:, h, j * P:(j + 1) * P],
                                                       ut[:, t % 2, k * P:(k + 1) * P], ident)
                        last.then_inc(u_turned, 1)
                    pe.wait_ge(u_copied, 2 * t + 2)
                    pe.wait_ge(rt_in, 64)
                    out = ps_l[:, t * (NG + NE):(t + 1) * (NG + NE)]
                    for k in range(KD):
                        nc.tensor.matmul(out, uT[:, k, :], w_rt[:, k, :], start=(k == 0), stop=False)
                    nc.tensor.matmul(out, K["c"][0:1, K_ONE:K_ONE + P], b_rt[:], start=False,
                                     stop=True).then_inc(logits, 1)

                tiles(norm, turn, mix, route, split)


def stage_route(nc, K, T):
    with Scope(nc, "rte") as sc:
        def sb(name, *shape):
            return sc.sb(name, [P, *shape])

        gmax, gsum, gp, pm = (sb(n, NT) for n in ("gmax", "gsum", "gp", "pm"))
        dlt, pri, ohg, il, oh1, oh2, il2 = (sb(n, NT, 4) for n in ("dlt", "pri", "ohg", "il", "oh1", "oh2", "il2"))
        m1, m2, e2, v1 = (sb(n, NT) for n in ("m1", "m2", "e2", "v1"))
        prod = sb("prod", NT, NG, EPG)
        pick = [sb(f"pick{k}", NT, NG, EPG) for k in range(2)]
        both = sb("both", NT * NE)
        off = sb("off", NT + 1, NE)
        tot = sb("tot", NT, NE)
        where = sb("where", NT, NE)
        cnt_i = sc.sb("cnt_i", [P, NE], I32)
        ntl, cend, cbeg, ones = (sb(n, NE) for n in ("ntl", "cend", "cbeg", "ones"))
        tile_ge = sb("tile_ge", 32, NE)
        tile_e = sb("tile_e", 32)
        slot_f = sb("slot_f", NT)
        tok_i = sc.sb("tok_i", [P, NT], U32)
        zeros_i = sc.sb("zeros_i", [P, SLOTS // P], U32)
        ps_r = sc.ps("ps_r", [P, 512])
        ps_t = sc.ps("ps_t", [P, 512])
        own_dve, expd, want_exp, ranked, both_made, slots_made, zero_made = (
            sc.sem(n) for n in ("own_dve", "expd", "want_exp", "ranked", "both_made", "slots_made", "zero_made"))
        zero_out, scattered, back = T["zero_out"], T["scattered"], T["back"]
        c = K["c"]
        lg = K["lg"]
        slots_d = T["slots"]
        with sc.block() as block:
            @block.vector
            def _(dve):
                own = Tally(own_dve)

                def step(ins):
                    own.inc(ins)
                    own.wait(dve)

                V = nc.vector

                def wide(x, n=4):
                    return x[:].unsqueeze(2).to_broadcast((P, NT, n))

                def first_max(x, top, out):
                    step(V.tensor_tensor(pri[:], x, wide(top), ALU.is_equal))
                    step(V.tensor_tensor(pri[:], pri[:], c[:, K_PRI:K_PRI + 4].unsqueeze(1).to_broadcast((P, NT, 4)),
                                         ALU.mult))
                    step(V.tensor_reduce(pm[:], pri[:], X, ALU.max))
                    step(V.tensor_tensor(out[:], pri[:], wide(pm), ALU.is_equal))

                V.memset(zeros_i[:], 0).then_inc(zero_made, 1)
                step(V.memset(ones[:], 1.0))
                step(V.tensor_reduce(gmax[:], lg[:, :, 0:NG], X, ALU.max))
                V.tensor_tensor(dlt[:], lg[:, :, 0:NG], wide(gmax), ALU.subtract).then_inc(want_exp, 1)
                first_max(lg[:, :, 0:NG], gmax, ohg)
                step(V.tensor_tensor(prod[:], lg[:, :, NG:].rearrange("p t (g j) -> p t g j", g=NG),
                                     ohg[:].unsqueeze(3).to_broadcast((P, NT, NG, EPG)), ALU.mult))
                step(V.tensor_reduce(il[:], prod[:].rearrange("p t g j -> p t j g"), X, ALU.add))
                step(V.tensor_reduce(m1[:], il[:], X, ALU.max))
                first_max(il[:], m1, oh1)
                step(V.scalar_tensor_tensor(il2[:], oh1[:], NEG, il[:], ALU.mult, ALU.add))
                step(V.tensor_reduce(m2[:], il2[:], X, ALU.max))
                first_max(il2[:], m2, oh2)
                V.tensor_tensor(e2[:], m2[:], m1[:], ALU.subtract).then_inc(want_exp, 1)
                for k, oh in enumerate((oh1, oh2)):
                    step(V.tensor_tensor(pick[k][:], ohg[:].unsqueeze(3).to_broadcast((P, NT, NG, EPG)),
                                         oh[:].unsqueeze(2).to_broadcast((P, NT, NG, EPG)), ALU.mult))
                V.tensor_tensor(both[:], pick[0][:].rearrange("p t g j -> p (t g j)"),
                                pick[1][:].rearrange("p t g j -> p (t g j)"), ALU.add).then_inc(both_made, 1)
                dve.wait_ge(expd, 2)
                step(V.tensor_reduce(gsum[:], dlt[:], X, ALU.add))
                step(V.reciprocal(gp[:], gsum[:]))
                step(V.tensor_scalar(v1[:], e2[:], 1.0, None, ALU.add))
                step(V.reciprocal(v1[:], v1[:]))
                step(V.tensor_tensor(K["cw"][:, 0, :], v1[:], gp[:], ALU.mult))
                step(V.tensor_tensor(K["cw"][:, 1, :], K["cw"][:, 0, :], e2[:], ALU.mult))
                dve.wait_ge(ranked, 2)
                step(V.tensor_copy(tot[:], ps_t[:, 0:NT * NE].rearrange("p (t e) -> p t e", t=NT)))
                step(V.memset(off[:, 0, :], 0.0))
                for t in range(NT):
                    step(V.tensor_tensor(off[:, t + 1, :], off[:, t, :], tot[:, t, :], ALU.add))
                step(V.tensor_scalar(ntl[:], off[:, NT, :], float(P - 1), None, ALU.add))
                step(V.tensor_copy(cnt_i[:], ntl[:]))
                step(V.tensor_scalar(cnt_i[:], cnt_i[:], 7, None, ALU.arith_shift_right))
                step(V.tensor_copy(ntl[:], cnt_i[:]))
                step(V.tensor_tensor_scan(cend[:], ones[:], ntl[:], 0.0, ALU.mult, ALU.add))
                step(V.tensor_tensor(cbeg[:], cend[:], ntl[:], ALU.subtract))
                step(V.tensor_tensor(where[:], ps_r[:, 0:NT * NE].rearrange("p (t e) -> p t e", t=NT),
                                     off[:, 0:NT, :], ALU.add))
                step(V.scalar_tensor_tensor(where[:], cbeg[:].unsqueeze(1).to_broadcast((P, NT, NE)), float(P),
                                            where[:], ALU.mult, ALU.add))
                for k in range(2):
                    step(V.tensor_tensor(prod[:].rearrange("p t g j -> p t (g j)"), where[:],
                                         pick[k][:].rearrange("p t g j -> p t (g j)"), ALU.mult))
                    step(V.tensor_reduce(slot_f[:], prod[:].rearrange("p t g j -> p t (g j)"), X, ALU.add))
                    step(V.tensor_copy(K["slot"][:, k, :], slot_f[:]))
                step(V.tensor_tensor(tile_ge[:], c[:, K_TILE:K_TILE + 32].unsqueeze(2).to_broadcast((P, 32, NE)),
                                     cend[:].unsqueeze(1).to_broadcast((P, 32, NE)), ALU.is_ge))
                step(V.tensor_reduce(tile_e[:], tile_ge[:], X, ALU.add))
                step(V.tensor_scalar(tile_e[:], tile_e[:], float(NE - 1), None, ALU.min))
                step(V.tensor_copy(K["texp"][:], tile_e[:]))
                step(V.memset(K["tnew"][:], 1))
                step(V.tensor_tensor(K["tnew"][:, 1:], tile_e[:, 1:], tile_e[:, 0:31], ALU.not_equal))
                V.tensor_copy(tok_i[:], c[:, K_TOK:K_TOK + NT]).then_inc(slots_made, 1)

            @block.scalar
            def _(act):
                act.wait_ge(want_exp, 1)
                nc.scalar.activation(dlt[:], dlt[:], ACT.Exp).then_inc(expd, 1)
                act.wait_ge(want_exp, 2)
                nc.scalar.activation(e2[:], e2[:], ACT.Exp).then_inc(expd, 1)

            @block.tensor
            def _(pe):
                pe.wait_ge(both_made, 1)
                nc.tensor.matmul(ps_r[:, 0:NT * NE], c[:, K_LT:K_LT + P], both[:], start=True, stop=True).then_inc(ranked, 1)
                nc.tensor.matmul(ps_t[:, 0:NT * NE], c[:, K_ONE:K_ONE + P], both[:], start=True, stop=True).then_inc(ranked, 1)

            @block.gpsimd
            def _(pool):
                pool.wait_ge(zero_made, 1)
                pool.dma_start(slots_d.rearrange("(p n) a -> p (n a)", p=P), zeros_i[:]).then_inc(zero_out, 16)
                pool.wait_ge(zero_out, 16)
                pool.wait_ge(slots_made, 1)
                for k in range(2):
                    for t in range(NT):
                        pool.indirect_dma_start(slots_d, bass.IndirectOffsetOnAxis(ap=K["slot"][:, k, t:t + 1], axis=0),
                                                tok_i[:, t:t + 1], None).then_inc(scattered, 16)
                pool.wait_ge(scattered, 16 * 2 * NT)
                pool.dma_start(K["stok"][:], slots_d.rearrange("(n p) a -> p (n a)", p=P),
                               allow_slow_non_contiguous=True).then_inc(back, 16)
                pool.wait_ge(back, 16)


def stage_moe(nc, a, K, T):
    GC, DC = KD, KF
    EARLY = 4
    GR, DR = GC, DC
    with Scope(nc, "moe") as sc:
        g_raw = sc.sb("g_raw", [P, GC, 2, FE])
        d_raw = sc.sb("d_raw", [P, DC, D])
        g_hi = sc.sb("g_hi", [P, GR, 2, FE], F32R)
        g_lo = sc.sb("g_lo", [P, GR, 2, FE], F32R)
        d_hi = sc.sb("d_hi", [P, DR, D], F32R)
        d_lo = sc.sb("d_lo", [P, DR, D], F32R)
        xg = sc.sb("xg", [P, D])
        idx = sc.sb("idx", [P, 1], U32)
        xT_hi = sc.sb("xT_hi", [P, KD, P], F32R)
        xT_lo = sc.sb("xT_lo", [P, KD, P], F32R)
        act_g = sc.sb("act_g", [P, FE])
        hid = sc.sb("hid", [P, FE])
        hT_hi = sc.sb("hT_hi", [P, KF, P], F32R)
        hT_lo = sc.sb("hT_lo", [P, KF, P], F32R)
        y = sc.sb("y", [P, D])
        ps_x = sc.ps("ps_x", [P, 2, 512])
        ps_g = sc.ps("ps_g", [P, 2, 512])
        ps_h = sc.ps("ps_h", [P, 512])
        ps_y = sc.ps("ps_y", [P, 2, 512])
        g_in = [sc.sem(f"g_in{c}") for c in range(GC)]
        d_in = [sc.sem(f"d_in{c}") for c in range(DC)]
        (s_ghi, s_glo, s_dhi, s_dlo, g_used, d_used, idx_set, x_turned, x_hi, x_lo, silu_made, h_made, h_turned,
         h_hi, h_lo, y_made, y_out) = (
            sc.sem(n) for n in ("s_ghi", "s_glo", "s_dhi", "s_dlo", "g_used", "d_used", "idx_set", "x_turned",
                                "x_hi", "x_lo", "silu_made", "h_made", "h_turned", "h_hi", "h_lo", "y_made", "y_out"))
        passed = sc.sem("passed")
        x_in = T["xg_in"]
        wg_d, wu_d, wd_d = a["w_gate_e"][0], a["w_up_e"][0], a["w_down_e"][0]
        c = K["c"]
        LAST = TILES - 1
        with sc.block() as block:
            @block.sync
            def _(sp):
                def load_g(e, i=None):
                    for ch in range(GC):
                        if i is not None:
                            sp.wait_ge(s_ghi, (i - 1) * GC + (ch + 1))
                            sp.wait_ge(s_glo, (i - 1) * GC + (ch + 1))
                        for m, w in enumerate((wg_d, wu_d)):
                            src = w[bass.ds(e, 1), ch * P:(ch + 1) * P, :].rearrange("a p n -> p (a n)")
                            sp.dma_start(g_raw[:, ch, m, :], src).then_inc(g_in[ch], 16)

                def load_d(e, i=None):
                    for ch in range(DC):
                        if i is not None:
                            sp.wait_ge(s_dhi, (i - 1) * DC + (ch + 1))
                            sp.wait_ge(s_dlo, (i - 1) * DC + (ch + 1))
                        src = wd_d[bass.ds(e, 1), ch * P:(ch + 1) * P, :].rearrange("a p n -> p (a n)")
                        sp.dma_start(d_raw[:, ch, :], src).then_inc(d_in[ch], 16)

                def same_g(i):
                    for ch in range(GC):
                        sp.wait_ge(s_ghi, (i - 1) * GC + (ch + 1))
                        sp.sem_inc(g_in[ch], 32)

                def same_d(i):
                    for ch in range(DC):
                        sp.wait_ge(s_dhi, (i - 1) * DC + (ch + 1))
                        sp.sem_inc(d_in[ch], 16)

                e0 = sp.value_load(K["texp"][0:1, 0:1], min_val=0, max_val=NE - 1)
                load_g(e0)
                load_d(e0)
                with sp.Fori(1, TILES) as i:
                    new = sp.value_load(K["tnew"][0:1, bass.ds(i, 1)], min_val=0, max_val=1)
                    with sp.If(new != 0):
                        e = sp.value_load(K["texp"][0:1, bass.ds(i, 1)], min_val=0, max_val=NE - 1)
                        load_g(e, i)
                        load_d(e, i)
                    with sp.Else():
                        same_g(i)
                        same_d(i)

            @block.gpsimd
            def _(pool):
                def gather(i):
                    nc.gpsimd.tensor_copy(idx[:], K["stok"][:, bass.ds(i, 1)]).then_inc(idx_set, 1)
                    wait_alone(pool, idx_set, i + 1, passed)
                    pool.indirect_dma_start(xg[:], None, T["u"],
                                            bass.IndirectOffsetOnAxis(ap=idx[:, 0:1], axis=0)).then_inc(x_in, 16)

                gather(0)
                with pool.Fori(1, TILES + 1) as i:
                    wait_alone(pool, x_turned, i * 2, passed)
                    gather(i)
                pool.wait_ge(x_in, 16 * (TILES + 1))

            @block.scalar
            def _(act):
                def split_g(i, ch, room=True):
                    act.wait_ge(g_in[ch], i * 32 + 32)
                    if room:
                        act.wait_ge(g_used, i * GC + (ch + 1 - GR))
                    nc.scalar.activation(g_hi[:, ch % GR], g_raw[:, ch], ACT.Copy).then_inc(s_ghi, 1)

                def split_d(i, ch, room=True):
                    act.wait_ge(d_in[ch], i * 16 + 16)
                    if room:
                        act.wait_ge(d_used, i * DC + (ch + 1 - DR))
                    nc.scalar.activation(d_hi[:, ch % DR], d_raw[:, ch], ACT.Copy).then_inc(s_dhi, 1)

                def x_part(i):
                    for h in range(2):
                        act.wait_ge(x_turned, i * 2 + (h + 1))
                        nc.scalar.activation(xT_hi[:, 4 * h:4 * h + 4, :],
                                             ps_x[:, h, :].rearrange("p (k n) -> p k n", k=4),
                                             ACT.Copy).then_inc(x_hi, 1)

                def silu(i):
                    act.wait_ge(g_used, i * GC + GC)
                    nc.scalar.activation(act_g[:], ps_g[:, 0, :], ACT.Silu).then_inc(silu_made, 1)

                def h_part(i):
                    act.wait_ge(h_turned, i + 1)
                    nc.scalar.activation(hT_hi[:], ps_h[:].rearrange("p (k n) -> p k n", k=KF),
                                         ACT.Copy).then_inc(h_hi, 1)

                def y_copy(i, first=False):
                    act.wait_ge(d_used, i * DC + DC)
                    if not first:
                        act.wait_ge(y_out, i * 16)
                    nc.scalar.activation(y[:], ps_y[:].rearrange("p a n -> p (a n)"), ACT.Copy).then_inc(y_made, 1)
                    act.wait_ge(y_made, i + 1)
                    act.dma_start(T["y"][bass.ds(i * P, P), :], y[:]).then_inc(y_out, 16)

                x_part(0)
                for ch in range(GC):
                    split_g(0, ch, False)
                silu(0)
                x_part(1)
                for ch in range(EARLY):
                    split_g(1, ch)
                h_part(0)

                def turn(i, first=False, last=False):
                    for ch in range(EARLY, GC):
                        split_g(i, ch)
                    for ch in range(DC):
                        split_d(i - 1, ch, not first)
                    silu(i)
                    x_part(i + 1)
                    if not last:
                        for ch in range(EARLY):
                            split_g(i + 1, ch)
                    y_copy(i - 1, first)
                    h_part(i)

                turn(1, first=True)
                with act.Fori(2, LAST) as i:
                    turn(i)
                turn(LAST, last=True)
                for ch in range(DC):
                    split_d(LAST, ch)
                y_copy(LAST)
                act.wait_ge(y_out, 16 * TILES)

            @block.vector
            def _(dve):
                def split_g(i, ch):
                    dve.wait_ge(s_ghi, i * GC + (ch + 1))
                    nc.vector.tensor_tensor(g_lo[:, ch % GR], g_raw[:, ch], g_hi[:, ch % GR].bitcast(F32),
                                            ALU.subtract).then_inc(s_glo, 1)

                def split_d(i, ch):
                    dve.wait_ge(s_dhi, i * DC + (ch + 1))
                    nc.vector.tensor_tensor(d_lo[:, ch % DR], d_raw[:, ch], d_hi[:, ch % DR].bitcast(F32),
                                            ALU.subtract).then_inc(s_dlo, 1)

                def x_part(i):
                    for h in range(2):
                        dve.wait_ge(x_hi, i * 2 + (h + 1))
                        nc.vector.tensor_tensor(xT_lo[:, 4 * h:4 * h + 4, :],
                                                ps_x[:, h, :].rearrange("p (k n) -> p k n", k=4),
                                                xT_hi[:, 4 * h:4 * h + 4, :].bitcast(F32),
                                                ALU.subtract).then_inc(x_lo, 1)

                def hidden(i):
                    dve.wait_ge(silu_made, i + 1)
                    nc.vector.tensor_tensor(hid[:], act_g[:], ps_g[:, 1, :], ALU.mult).then_inc(h_made, 1)

                def h_part(i):
                    dve.wait_ge(h_hi, i + 1)
                    nc.vector.tensor_tensor(hT_lo[:], ps_h[:].rearrange("p (k n) -> p k n", k=KF),
                                            hT_hi[:].bitcast(F32), ALU.subtract).then_inc(h_lo, 1)

                x_part(0)
                for ch in range(GC):
                    split_g(0, ch)
                hidden(0)
                x_part(1)
                for ch in range(EARLY):
                    split_g(1, ch)
                h_part(0)

                def turn(i, last=False):
                    for ch in range(EARLY, GC):
                        split_g(i, ch)
                    for ch in range(DC):
                        split_d(i - 1, ch)
                    hidden(i)
                    x_part(i + 1)
                    if not last:
                        for ch in range(EARLY):
                            split_g(i + 1, ch)
                    h_part(i)

                with dve.Fori(1, LAST) as i:
                    turn(i)
                turn(LAST, last=True)
                for ch in range(DC):
                    split_d(LAST, ch)

            @block.tensor
            def _(pe):
                ident = c[:, K_ID:K_ID + P]

                def turn_x(i, first=False):
                    pe.wait_ge(x_in, i * 16 + 16)
                    for h in range(2):
                        if not first:
                            pe.wait_ge(x_lo, i * 2 + (h - 1))
                        for j in range(4):
                            k = 4 * h + j
                            last = nc.tensor.transpose(ps_x[:, h, j * P:(j + 1) * P], xg[:, k * P:(k + 1) * P], ident)
                        last.then_inc(x_turned, 1)

                def gate_up(i, first=False):
                    pe.wait_ge(x_lo, i * 2 + 2)
                    if not first:
                        pe.wait_ge(h_made, i)
                    for ch in range(GC):
                        pe.wait_ge(s_glo, i * GC + (ch + 1))
                        for m in range(2):
                            last = mm3(nc, ps_g[:, m, :], xT_hi[:, ch, :], xT_lo[:, ch, :],
                                       g_hi[:, ch % GR, m, :], g_lo[:, ch % GR, m, :], ch == 0, ch == GC - 1)
                        last.then_inc(g_used, 1)

                def turn_h(i):
                    pe.wait_ge(h_made, i + 1)
                    for j in range(KF):
                        last = nc.tensor.transpose(ps_h[:, j * P:(j + 1) * P], hid[:, j * P:(j + 1) * P], ident)
                    last.then_inc(h_turned, 1)

                def down(i, first=False):
                    pe.wait_ge(h_lo, i + 1)
                    if not first:
                        pe.wait_ge(y_made, i)
                    for ch in range(DC):
                        pe.wait_ge(s_dlo, i * DC + (ch + 1))
                        for m in range(2):
                            r = slice(m * 512, (m + 1) * 512)
                            last = mm3(nc, ps_y[:, m, :], hT_hi[:, ch, :], hT_lo[:, ch, :],
                                       d_hi[:, ch % DR, r], d_lo[:, ch % DR, r], ch == 0, ch == DC - 1)
                        last.then_inc(d_used, 1)

                turn_x(0, True)
                gate_up(0, True)
                turn_x(1)
                turn_h(0)
                gate_up(1)
                turn_x(2)
                down(0, True)
                turn_h(1)
                with pe.Fori(2, TILES) as i:
                    gate_up(i)
                    turn_x(i + 1)
                    down(i - 1)
                    turn_h(i)
                down(LAST)


def stage_finish(nc, a, K, T, out):
    with Scope(nc, "fin") as sc:
        WR, HB = 4, 4
        w_raw = sc.sb("w_raw", [P, WR, D])
        w_hi = sc.sb("w_hi", [P, KD + KP, D], F32R)
        w_lo = sc.sb("w_lo", [P, KD + KP, D], F32R)
        gain = sc.sb("gain", [P, D])
        gfin = sc.sb("gfin", [P, D])
        bgate = sc.sb("bgate", [1, D])
        junk = sc.sb("junk", [P, D], BF16)
        ss = sc.sb("ss", [P, NT, 2])
        rt = sc.sb("rt", [P, NT, 2])
        rs = sc.sb("rs", [P, NT, 2])
        ht = sc.sb("h", [P, HB, D])
        ys = sc.sb("y", [P, 2, 2, D])
        pt = sc.sb("p", [P, HB, PLE])
        vt = sc.sb("v", [P, D])
        vT_hi = sc.sb("vT_hi", [P, 2, KD + KP, P], F32R)
        vT_lo = sc.sb("vT_lo", [P, 2, KD + KP, P], F32R)
        gate = sc.sb("gate", [P, D])
        ot = sc.sb("o", [P, D])
        ps_x = sc.ps("ps_x", [P, 3, 512])
        ps_g = sc.ps("ps_g", [P, 2, 512])
        ps_p = sc.ps("ps_p", [P, 2, 512])
        w_in = [sc.sem(f"w_in{i}") for i in range(WR)]
        h_in = [sc.sem(f"h_in{i}") for i in range(HB)]
        y_in = T["y_in"]
        (mixed, vec_in, split_hi, split_lo, summed, sq, var, root, v_made, turned, v_hi, v_lo, gated, projected,
         sig, added, f_var, f_root, o_made, o_out, own_dve) = (
            sc.sem(n) for n in ("mixed", "vec_in", "split_hi", "split_lo", "summed", "sq", "var", "root",
                                "v_made", "turned", "v_hi", "v_lo", "gated", "projected", "sig", "added", "f_var",
                                "f_root", "o_made", "o_out", "own_dve"))
        f_sq = sc.sem("f_sq")
        wg_d = a["w_ple_gate"].rearrange("l (k p) n -> (l k) p n", p=P)
        wp_d = a["w_ple_proj"].rearrange("l (k p) n -> (l k) p n", p=P)
        p_d = a["p"].rearrange("l b (t p) d -> (l b t) p d", p=P)
        out_d = out.rearrange("b (t p) d -> (b t) p d", p=P)
        with sc.block() as block:
            @block.sync
            def _(sp):
                sp.dma_start(gain[:], a["g_ple"].to_broadcast((P, D))).then_inc(vec_in, 16)
                sp.dma_start(gfin[:], a["g_final"].rearrange("(a n) -> a n", a=1).to_broadcast((P, D))).then_inc(vec_in, 16)
                sp.dma_start(bgate[:], a["b_ple_gate"]).then_inc(vec_in, 16)
                def rows(t):
                    sp.dma_start(ht[:, t % HB, :], T["h"][t]).then_inc(h_in[t % HB], 16)
                    sp.dma_start(pt[:, t % HB, :], p_d[t]).then_inc(h_in[t % HB], 16)

                rows(0)
                for k in range(KD + KP):
                    if k >= WR:
                        sp.wait_ge(split_lo, k - WR + 1)
                    sp.dma_start(w_raw[:, k % WR, :], wg_d[k] if k < KD else wp_d[k - KD]).then_inc(w_in[k % WR], 16)
                    if k < HB - 1:
                        rows(k + 1)
                for t in range(NT):
                    sp.wait_ge(o_made, t + 1)
                    sp.dma_start(out_d[t], ot[:]).then_inc(o_out, 16)
                    if t + HB < NT:
                        rows(t + HB)
                sp.wait_ge(o_out, 16 * NT)

            @block.gpsimd
            def _(pool):
                for t in range(NT):
                    if t >= 2:
                        pool.wait_ge(summed, 2 * t - 2)
                    for k in range(2):
                        pool.indirect_dma_start(ys[:, t % 2, k, :], None, T["y"],
                                                bass.IndirectOffsetOnAxis(ap=K["slot"][:, k, t:t + 1], axis=0)
                                                ).then_inc(y_in[t % 2], 16)

            def tiles(head, turn, weigh, tail, split):
                head(0)
                turn(0)
                head(1)
                split()
                for i in range(NT + 1):
                    if i:
                        weigh(i - 1)
                    if i + 1 < NT:
                        turn(i + 1)
                    if i + 2 < NT:
                        head(i + 2)
                    if i:
                        tail(i - 1)

            @block.scalar
            def _(act):
                def split():
                    for k in range(KD + KP):
                        act.wait_ge(w_in[k % WR], 16 * (k // WR + 1))
                        nc.scalar.activation(w_hi[:, k, :], w_raw[:, k % WR, :], ACT.Copy).then_inc(split_hi, 1)

                def head(t):
                    act.wait_ge(summed, 2 * t + 2)
                    nc.scalar.activation(junk[:], ht[:, t % HB, :], ACT.Square,
                                         accum_out=ss[:, t, 0:1]).then_inc(sq, 1)
                    act.wait_ge(var, t + 1)
                    nc.scalar.activation(rt[:, t, 0:1], rt[:, t, 0:1], ACT.Sqrt).then_inc(root, 1)

                def turn(t):
                    for h in range(3):
                        act.wait_ge(turned, 3 * t + h + 1)
                        if t >= 2:
                            act.wait_ge(projected, t - 1)
                        n = 4 if h < 2 else KP
                        nc.scalar.activation(vT_hi[:, t % 2, 4 * h:4 * h + n, :],
                                             ps_x[:, h, 0:n * P].rearrange("p (k n) -> p k n", k=n),
                                             ACT.Copy).then_inc(v_hi, 1)

                def weigh(t):
                    act.wait_ge(gated, t + 1)
                    if t:
                        act.wait_ge(added, t)
                    nc.scalar.activation(gate[:], ps_g[:].rearrange("p a n -> p (a n)"), ACT.Sigmoid).then_inc(sig, 1)

                def tail(t):
                    act.wait_ge(added, t + 1)
                    nc.scalar.activation(junk[:], ht[:, t % HB, :], ACT.Square,
                                         accum_out=ss[:, t, 1:2]).then_inc(f_sq, 1)
                    act.wait_ge(f_var, t + 1)
                    nc.scalar.activation(rt[:, t, 1:2], rt[:, t, 1:2], ACT.Sqrt).then_inc(f_root, 1)

                tiles(head, turn, weigh, tail, split)

            @block.vector
            def _(dve):
                own = Tally(own_dve)

                def split():
                    for k in range(KD + KP):
                        dve.wait_ge(split_hi, k + 1)
                        nc.vector.tensor_tensor(w_lo[:, k, :], w_raw[:, k % WR, :], w_hi[:, k, :].bitcast(F32),
                                                ALU.subtract).then_inc(split_lo, 1)

                dve.wait_ge(vec_in, 48)

                def head(t):
                    h = ht[:, t % HB, :]
                    dve.wait_ge(h_in[t % HB], 32 * (t // HB + 1))
                    dve.wait_ge(y_in[t % 2], 32 * (t // 2 + 1))
                    for k in range(2):
                        nc.vector.scalar_tensor_tensor(h, ys[:, t % 2, k, :], K["cw"][:, k, t:t + 1], h, ALU.mult,
                                                       ALU.add).then_inc(summed, 1)
                        dve.wait_ge(summed, 2 * t + k + 1)
                    dve.wait_ge(sq, t + 1)
                    nc.vector.tensor_scalar(rt[:, t, 0:1], ss[:, t, 0:1], 1.0 / D, EPS, ALU.mult,
                                            ALU.add).then_inc(var, 1)
                    dve.wait_ge(root, t + 1)
                    own.inc(nc.vector.reciprocal(rs[:, t, 0:1], rt[:, t, 0:1]))
                    own.wait(dve)
                    if t:
                        dve.wait_ge(turned, 3 * t)
                    nc.vector.scalar_tensor_tensor(vt[:], h, rs[:, t, 0:1], gain[:], ALU.mult,
                                                   ALU.mult).then_inc(v_made, 1)

                def turn(t):
                    for h in range(3):
                        dve.wait_ge(v_hi, 3 * t + h + 1)
                        n = 4 if h < 2 else KP
                        nc.vector.tensor_tensor(vT_lo[:, t % 2, 4 * h:4 * h + n, :],
                                                ps_x[:, h, 0:n * P].rearrange("p (k n) -> p k n", k=n),
                                                vT_hi[:, t % 2, 4 * h:4 * h + n, :].bitcast(F32),
                                                ALU.subtract).then_inc(v_lo, 1)

                def weigh(t):
                    dve.wait_ge(sig, t + 1)
                    dve.wait_ge(projected, t + 1)
                    nc.vector.tensor_tensor(gate[:], gate[:], ps_p[:].rearrange("p a n -> p (a n)"),
                                            ALU.mult).then_inc(mixed, 1)

                def tail(t):
                    h = ht[:, t % HB, :]
                    dve.wait_ge(mixed, t + 1)
                    nc.vector.tensor_tensor(h, h, gate[:], ALU.add).then_inc(added, 1)
                    dve.wait_ge(f_sq, t + 1)
                    nc.vector.tensor_scalar(rt[:, t, 1:2], ss[:, t, 1:2], 1.0 / D, EPS, ALU.mult,
                                            ALU.add).then_inc(f_var, 1)
                    dve.wait_ge(f_root, t + 1)
                    own.inc(nc.vector.reciprocal(rs[:, t, 1:2], rt[:, t, 1:2]))
                    own.wait(dve)
                    if t:
                        dve.wait_ge(o_out, 16 * t)
                    nc.vector.scalar_tensor_tensor(ot[:], h, rs[:, t, 1:2], gfin[:], ALU.mult,
                                                   ALU.mult).then_inc(o_made, 1)

                tiles(head, turn, weigh, tail, split)

            @block.tensor
            def _(pe):
                ident = K["c"][:, K_ID:K_ID + P]

                def turn(t):
                    pe.wait_ge(v_made, t + 1)
                    pe.wait_ge(h_in[t % HB], 32 * (t // HB + 1))
                    for h in range(3):
                        if t:
                            pe.wait_ge(v_lo, 3 * t + h - 2)
                        for j in range(4 if h < 2 else KP):
                            src = vt[:, (4 * h + j) * P:(4 * h + j + 1) * P] if h < 2 else pt[:, t % HB, j * P:(j + 1) * P]
                            last = nc.tensor.transpose(ps_x[:, h, j * P:(j + 1) * P], src, ident)
                        last.then_inc(turned, 1)

                turn(0)
                for t in range(NT):
                    if t + 1 < NT:
                        turn(t + 1)
                    pe.wait_ge(v_lo, 3 * t + 3)
                    if t:
                        pe.wait_ge(sig, t)
                    for out_, ks, sem in ((ps_g, range(KD), gated), (ps_p, range(KD, KD + KP), projected)):
                        if t and ks[0]:
                            pe.wait_ge(mixed, t)
                        for h in range(2):
                            r = slice(h * 512, (h + 1) * 512)
                            for k in ks:
                                if t == 0 and h == 0:
                                    pe.wait_ge(split_lo, k + 1)
                                last = mm3(nc, out_[:, h, :], vT_hi[:, t % 2, k, :], vT_lo[:, t % 2, k, :], w_hi[:, k, r],
                                           w_lo[:, k, r], k == ks[0], k == ks[-1] and ks[0] > 0)
                            if ks[0] == 0:
                                last = nc.tensor.matmul(out_[:, h, :], K["c"][0:1, K_ONE:K_ONE + P], bgate[:, r],
                                                        start=False, stop=True)
                        last.then_inc(sem, 1)


def build(nc, a, out):
    T = {
        "feat": nc.dram_tensor("feat", [16, P, S], F32).ap(),
        "cum": nc.dram_tensor("cum", [NH, 2, S], F32).ap(),
        "h": nc.dram_tensor("h_rows", [NT, P, D], F32).ap(),
        "u": nc.dram_tensor("u_rows", [S, D], F32).ap(),
        "slots": nc.dram_tensor("slots", [SLOTS, 1], U32).ap(),
        "y": nc.dram_tensor("y_rows", [TILES * P, D], F32).ap(),
    }
    K = {}
    with Scope(nc, "all") as outer:
        T["stored"] = [outer.sem(f"stored{i}") for i in range(2)]
        T["y_in"] = [outer.sem(f"y_in{i}") for i in range(2)]
        for name in ("zero_out", "scattered", "back", "xg_in"):
            T[name] = outer.sem(name)
        for name, shape, dt in (("c", [P, K_COLS], F32), ("lg", [P, NT, NG + NE], F32), ("cw", [P, 2, NT], F32),
                                ("slot", [P, 2, NT], U32), ("texp", [P, 32], I32),
                                ("tnew", [P, 32], I32), ("stok", [P, SLOTS // P], U32)):
            K[name] = outer.sb(name, shape, dt)
        with Scope(nc, "att") as inner:
            for name, shape, dt in (("o", [P, NT, D], F32),):
                K[name] = inner.sb(name, shape, dt)
            with Scope(nc, "tok") as tok:
                for name, shape, dt in (
                        ("maskb", [P, (2 + NT) * P], BF16), ("identb", [P, P], BF16), ("cos", [P, S], F32),
                        ("sin", [P, S], F32), ("vb", [P, NT, NH * HD], F32), ("vsw", [P, NT, 288], F32),
                        ("gate", [P, NT, 3 * NH], F32), ("vc", [P, GROUPS, HD], F32),
                        ("kc_raw", [P, GROUPS, P], F32), ("kc_hi", [P, GROUPS, P], F32R),
                        ("kc_lo", [P, GROUPS, P], F32R)):
                    K[name] = tok.sb(name, shape, dt)
                K["tokT"] = K["o"][:, 0:2, :]
                stage_load(nc, a, K)
                stage_project(nc, a, K, T)
                stage_compress(nc, a, K, T)
                stage_attention(nc, K, T, sparse=True)
                stage_attention(nc, K, T, sparse=False)
            stage_mix(nc, a, K, T)
        stage_route(nc, K, T)
        stage_moe(nc, a, K, T)
        stage_finish(nc, a, K, T, out)


_INS = ["x", "p", "positions", "g_mix", "w_in", "b_nsa_gate", "b_forget", "pe_cmp_k", "w_cmp_k1", "w_cmp_k2",
        "pe_cmp_v", "w_cmp_v1", "w_cmp_v2", "beta_nsa", "beta_fox", "w_out", "g_ffn", "w_group", "b_group",
        "w_router", "b_router", "w_gate_e", "w_up_e", "w_down_e", "g_ple", "w_ple_gate", "b_ple_gate",
        "w_ple_proj", "g_final"]


def kernel(**inputs):
    import concourse.bacc as bacc
    from concourse.bass_utils import run_bass_kernel_spmd as run

    nc = bacc.Bacc("TRN2", target_bir_lowering=False, num_devices=1)
    arrays, a = {}, {}
    for name in _INS:
        v = np.ascontiguousarray(inputs[name])
        arrays[f"in_{name}"] = v
        a[name] = nc.dram_tensor(f"in_{name}", v.shape, mybir.dt.from_np(v.dtype), kind="ExternalInput").ap()
    c = constants()
    arrays["in_consts"] = c
    a["consts"] = nc.dram_tensor("in_consts", c.shape, F32, kind="ExternalInput").ap()
    out = nc.dram_tensor("out", (1, S, D), F32, kind="ExternalOutput").ap()
    build(nc, a, out)
    r = run(nc, [arrays], core_ids=[0])
    return r.results[0]["out"]
```

```python
from contextlib import ExitStack

import numpy as np

import concourse.bass as bass
from concourse import mybir

F32 = mybir.dt.float32
F32R = mybir.dt.float32r
BF16 = mybir.dt.bfloat16
I32 = mybir.dt.int32
U32 = mybir.dt.uint32
ALU = mybir.AluOpType
ACT = mybir.ActivationFunctionType
X = mybir.AxisListType.X

P = 128
D = 1024
S = 1024
KD = D // P
NT = S // P
HD = 64
NH = 8
GROUPS = 2
SCALE = HD ** -0.5
CMP_BLOCK, CMP_STRIDE = 32, 16
N_CMP = (S - CMP_BLOCK) // CMP_STRIDE + 1
WINDOW = 512
WB = WINDOW // P
NG, EPG = 4, 4
NE = NG * EPG
FE = D // 2
KF = FE // P
PLE = 256
KP = PLE // P
EPS = 1e-6
NEG = -1e30
TILES = (2 * S) // P + NE - 1
FEWEST = (2 * S) // P
SLOTS = (TILES + 1) * P
ROPE_HALF = HD // 8

C_Q, C_KC, C_VC, C_KS, C_VS, C_KW, C_VW, C_GATE = 0, 512, 640, 768, 896, 1024, 1152, 1280
C_QB, C_KB, C_VB, C_F = 1304, 1816, 2328, 2840

K_ID, K_ROT, K_LT, K_ONE, K_DIAG, K_FAR, K_CMP = 0, 128, 256, 384, 512, 640, 768
K_FREQ = K_CMP + NT * P
K_ISROPE, K_NOROPE, K_VALID, K_PRI, K_TILE, K_COLS = (
    K_FREQ + 1, K_FREQ + 2, K_FREQ + 3, K_FREQ + 4, K_FREQ + 8, K_FREQ + 8 + 32)
K_TOK = K_COLS
K_COLS = K_TOK + NT


def constants():
    c = np.zeros((P, K_COLS), np.float32)
    a = np.arange(P)
    c[:, K_ID:K_ID + P] = np.eye(P)
    rot = np.zeros((P, P), np.float32)
    for h in (0, HD):
        for d in range(ROPE_HALF):
            rot[h + d + ROPE_HALF, h + d] = -1.0
            rot[h + d, h + d + ROPE_HALF] = 1.0
    c[:, K_ROT:K_ROT + P] = rot
    c[:, K_LT:K_LT + P] = (a[:, None] < a[None, :])
    c[:, K_ONE:K_ONE + P] = 1.0
    c[:, K_DIAG:K_DIAG + P] = np.where(a[None, :] <= a[:, None], 0.0, -NEG)
    c[:, K_FAR:K_FAR + P] = np.where(a[None, :] > a[:, None], 0.0, -NEG)
    for qt in range(NT):
        t = qt * P + a
        end = a * CMP_STRIDE + CMP_BLOCK - 1
        c[:, K_CMP + qt * P:K_CMP + (qt + 1) * P] = np.where(
            (end[None, :] <= t[:, None]) & (a[None, :] < N_CMP), 0.0, -NEG)
    inv = np.power(np.float32(500000.0), -np.arange(ROPE_HALF, dtype=np.float32) / np.float32(ROPE_HALF))
    rope = (a % HD) < 2 * ROPE_HALF
    c[:, K_FREQ] = np.where(rope, inv[a % ROPE_HALF], 0.0)
    c[:, K_ISROPE] = rope
    c[:, K_NOROPE] = ~rope
    c[:, K_VALID] = (a >= CMP_BLOCK - 1)
    c[:, K_PRI:K_PRI + 4] = np.arange(4, 0, -1)[None, :]
    c[:, K_TILE:K_TILE + 32] = np.arange(32)[None, :]
    c[:, K_TOK:K_TOK + NT] = a[:, None] + P * np.arange(NT)[None, :]
    return c


class Tally:

    def __init__(self, sem, base=0):
        self.sem, self.base, self.n = sem, base, 0

    def inc(self, ins):
        ins.then_inc(self.sem, 1)
        self.n += 1

    def wait(self, eng):
        eng.wait_ge(self.sem, self.base + self.n)


def mm3(nc, out, a_hi, a_lo, b_hi, b_lo, first, last):
    nc.tensor.matmul(out, a_hi, b_hi, start=first, stop=False)
    nc.tensor.matmul(out, a_hi, b_lo, start=False, stop=False)
    return nc.tensor.matmul(out, a_lo, b_hi, start=False, stop=last)


def wait_alone(eng, sem, value, passed):
    eng.wait_ge(sem, value)
    eng.sem_inc(passed, 1)


class Scope:

    def __init__(self, nc, name):
        self.nc, self.name, self.ctx, self.sems = nc, name, ExitStack(), []

    def __enter__(self):
        self.ctx.__enter__()
        return self

    def __exit__(self, *a):
        if self.sems:
            self.nc.all_engine_barrier()
            self.nc.clear_and_free_semaphores(self.sems)
            self.nc.all_engine_barrier()
        return self.ctx.__exit__(*a)

    def sb(self, name, shape, dt=F32):
        return self.ctx.enter_context(self.nc.sbuf_tensor(f"{self.name}_{name}", shape, dt))

    def ps(self, name, shape, dt=F32):
        return self.ctx.enter_context(self.nc.psum_tensor(f"{self.name}_{name}", shape, dt))

    def sem(self, name):
        self.sems.append(self.nc.alloc_semaphore(f"{self.name}_{name}"))
        return self.sems[-1]

    def block(self):
        return self.nc.Block()


def stage_load(nc, a, K):
    PI = float(np.pi)
    TWO_PI_HI = 6.28125
    TWO_PI_LO = float(2 * np.pi - TWO_PI_HI)
    with Scope(nc, "load") as sc:
        pos = sc.sb("pos", [P, S], I32)
        turns = sc.sb("turns", [P, S], I32)
        ang = sc.sb("ang", [P, S])
        whole = sc.sb("whole", [P, S])
        over = sc.sb("over", [P, S])
        ang_c = sc.sb("ang_c", [P, S])
        loaded, made, reduced, looked = (sc.sem(n) for n in ("loaded", "made", "reduced", "looked"))
        c = K["c"]
        with sc.block() as block:
            @block.sync
            def _(sp):
                sp.dma_start(c[:], a["consts"]).then_inc(loaded, 16)
                sp.dma_start(pos[:], a["positions"].to_broadcast((P, S))).then_inc(loaded, 16)
                sp.wait_ge(loaded, 32)

            @block.vector
            def _(dve):
                dve.wait_ge(loaded, 32)
                own = Tally(made)

                def step(ins):
                    own.inc(ins)
                    own.wait(dve)

                def wrap(x):
                    step(nc.vector.tensor_scalar(over[:], x[:], PI, -2 * PI, ALU.is_gt, ALU.mult))
                    step(nc.vector.tensor_tensor(x[:], x[:], over[:], ALU.add))
                    step(nc.vector.tensor_scalar(over[:], x[:], -PI, 2 * PI, ALU.is_lt, ALU.mult))
                    step(nc.vector.tensor_tensor(x[:], x[:], over[:], ALU.add))
                    step(nc.vector.tensor_scalar(x[:], x[:], 3.1415925, -3.1415925, ALU.min, ALU.max))

                own.inc(nc.vector.tensor_copy(K["maskb"][:], c[:, K_DIAG:K_DIAG + (2 + NT) * P]))
                own.inc(nc.vector.tensor_copy(K["identb"][:], c[:, K_ID:K_ID + P]))
                step(nc.vector.tensor_copy(ang[:], pos[:]))
                step(nc.vector.tensor_scalar(ang[:], ang[:], c[:, K_FREQ:K_FREQ + 1], None, ALU.mult))
                step(nc.vector.tensor_scalar(whole[:], ang[:], 1.0 / (2 * PI), None, ALU.mult))
                step(nc.vector.tensor_copy(turns[:], whole[:]))
                step(nc.vector.tensor_copy(whole[:], turns[:]))
                step(nc.vector.scalar_tensor_tensor(ang[:], whole[:], -TWO_PI_HI, ang[:], ALU.mult, ALU.add))
                step(nc.vector.scalar_tensor_tensor(ang[:], whole[:], -TWO_PI_LO, ang[:], ALU.mult, ALU.add))
                wrap(ang)
                step(nc.vector.tensor_scalar(ang_c[:], ang[:], PI / 2, None, ALU.add))
                wrap(ang_c)
                nc.vector.tensor_copy(over[:, 0:1], ang_c[:, 0:1]).then_inc(reduced, 1)
                dve.wait_ge(looked, 2)
                step(nc.vector.tensor_scalar(K["sin"][:], K["sin"][:], c[:, K_ISROPE:K_ISROPE + 1], None, ALU.mult))
                step(nc.vector.tensor_scalar(K["cos"][:], K["cos"][:], c[:, K_ISROPE:K_ISROPE + 1],
                                             c[:, K_NOROPE:K_NOROPE + 1], ALU.mult, ALU.add))

            @block.scalar
            def _(act):
                act.wait_ge(reduced, 1)
                nc.scalar.activation(K["sin"][:], ang[:], ACT.Sin).then_inc(looked, 1)
                nc.scalar.activation(K["cos"][:], ang_c[:], ACT.Sin).then_inc(looked, 1)


def stage_project(nc, a, K, T):
    with Scope(nc, "prj") as sc:
        XR = 3
        ss = sc.sb("ss", [P, NT])
        rstd = sc.sb("rstd", [P, 2 * NT])
        hT_hi = sc.sb("hT_hi", [P, KD, S], F32R)
        hT_lo = sc.sb("hT_lo", [P, KD, S], F32R)
        w_raw = sc.sb("w_raw", [P, 2, KD, P])
        w_hi = sc.sb("w_hi", [P, 2, KD, P], F32R)
        w_lo = sc.sb("w_lo", [P, 2, KD, P], F32R)
        feat = sc.sb("feat", [P, 2, S])
        turn = sc.sb("turn", [P, S // 2])
        cos_t = K["cos"]
        sin_t = K["sin"]
        VW = 256 + 24 + 8
        v_raw = K["o"][:, 2:5, :].rearrange("p a n -> p (a n)")[:, 0:KD * VW].rearrange("p (k n) -> p k n", k=KD)
        with Scope(nc, "prj_x") as early:
            xt = early.sb("x", [P, XR, D])
            xn = early.sb("xn", [P, 2, D])
            gain = early.sb("gain", [P, D])
            sq = early.sb("sq", [P, D], BF16)
        v_hi = sc.sb("v_hi", [P, KD, VW], F32R)
        v_lo = sc.sb("v_lo", [P, KD, VW], F32R)
        ps_x = sc.ps("ps_x", [P, 2, 512])
        ps_w = sc.ps("ps_w", [P, 2, 512])
        ps_r = sc.ps("ps_r", [P, 512])

        x_in = [sc.sem(f"x_in{i}") for i in range(XR)]
        gain_in, normed, scaled, turned, up_hi, up_lo, own_act, own_dve = (
            sc.sem(n) for n in ("gain_in", "normed", "scaled", "turned", "up_hi", "up_lo", "own_act", "own_dve"))
        squared = sc.sem("squared")
        rooted = sc.sem("rooted")
        var = sc.sem("var")
        w_in_ = [sc.sem(f"w_in{i}") for i in range(2)]
        split_hi, split_lo, product, evac, rotated, turn_made = (
            sc.sem(n) for n in ("split_hi", "split_lo", "product", "evac", "rotated", "turn_made"))
        roped = sc.sem("roped")
        stored = T["stored"]
        v_in = sc.sem("v_in")
        vs_hi, vs_lo, v_product, v_evac = (sc.sem(n) for n in ("vs_hi", "vs_lo", "v_product", "v_evac"))

        x_d = a["x"].rearrange("b (t p) d -> (b t) p d", p=P)
        w_d = a["w_in"].rearrange("l (k p) n -> (l p) k n", p=P)
        FIXED = [(C_Q + P * j, j, True) for j in range(4)] + [
            (C_KC, None, False), (C_VC, None, False), (C_KS, 6, True), (C_KW, 7, True)]
        NFIX = len(FIXED)

        def stores_before(n):
            return sum(1 for m in range(n % 2, n, 2) if FIXED[m][1] is not None)

        VCH = [[(C_VB, 256)], [(C_VB + 256, 256)], [(C_VS, 128), (C_VW, 128), (C_GATE, 24), (C_F, 8)]]

        with sc.block() as block:
            @block.sync
            def _(sp):
                sp.dma_start(gain[:], a["g_mix"].to_broadcast((P, D))).then_inc(gain_in, 16)
                for t in range(NT):
                    if t >= XR:
                        sp.wait_ge(scaled, t - XR + 1)
                    sp.dma_start(xt[:, t % XR, :], x_d[t]).then_inc(x_in[t % XR], 16)
                    if t < 2:
                        c = FIXED[t][0]
                        sp.dma_start(w_raw[:, t, :, :], w_d[:, :, c:c + P]).then_inc(w_in_[t], 16)
                for n in range(2, NFIX):
                    sp.wait_ge(split_hi, n - 1)
                    sp.wait_ge(split_lo, n - 1)
                    c = FIXED[n][0]
                    sp.dma_start(w_raw[:, n % 2, :, :], w_d[:, :, c:c + P]).then_inc(w_in_[n % 2], 16)
                with sp.Fori(0, NFIX // 2) as i:
                    for s in range(2):
                        sp.wait_ge(split_hi, i * 2 + (NFIX + s - 1))
                        sp.wait_ge(split_lo, i * 2 + (NFIX + s - 1))
                        sp.dma_start(w_raw[:, s, :, :],
                                     w_d[:, :, bass.ds(i * (2 * P) + (C_QB + s * P), P)]).then_inc(w_in_[s], 16)
                for n, cols in enumerate(VCH):
                    if n:
                        sp.wait_ge(vs_hi, n)
                        sp.wait_ge(vs_lo, n)
                    o = 0
                    for c, w in cols:
                        sp.dma_start(v_raw[:, :, o:o + w], w_d[:, :, c:c + w]).then_inc(v_in, 16)
                        o += w

            @block.gpsimd
            def _(pool):
                halves = 0
                for n, (_, row, rope) in enumerate(FIXED):
                    if row is None:
                        continue
                    if rope:
                        halves += 2
                        pool.wait_ge(roped, halves)
                    pool.dma_start(T["feat"][row], feat[:, n % 2, :]).then_inc(stored[n % 2], 16)
                with pool.Fori(0, NFIX // 2) as i:
                    for s in range(2):
                        pool.wait_ge(evac, i * 4 + (2 * NFIX + 2 * s + 2))
                        pool.dma_start(T["feat"][bass.ds(i * 2 + (NFIX + s), 1)].rearrange("a p n -> p (a n)"),
                                       feat[:, s, :]).then_inc(stored[s], 16)
                for s in range(2):
                    pool.wait_ge(stored[s], 16 * (stores_before(NFIX + s) + NFIX // 2))

            @block.scalar
            def _(act):
                for t in range(NT):
                    act.wait_ge(x_in[t % XR], 16 * (t // XR + 1))
                    if t:
                        act.wait_ge(squared, t)
                    nc.scalar.activation(sq[:], xt[:, t % XR, :], ACT.Square,
                                         accum_out=ss[:, t:t + 1]).then_inc(squared, 1)
                    act.wait_ge(var, t + 1)
                    nc.scalar.activation(rstd[:, NT + t:NT + t + 1], rstd[:, t:t + 1], ACT.Sqrt).then_inc(rooted, 1)
                    for h in range(2):
                        act.wait_ge(turned, 2 * t + h + 1)
                        nc.scalar.activation(hT_hi[:, 4 * h:4 * h + 4, t * P:(t + 1) * P],
                                             ps_x[:, h, :].rearrange("p (k n) -> p k n", k=4),
                                             ACT.Copy).then_inc(up_hi, 1)

                def split(n, s):
                    act.wait_ge(w_in_[s], n[0])
                    act.wait_ge(product, n[1])
                    nc.scalar.activation(w_hi[:, s], w_raw[:, s], ACT.Copy).then_inc(split_hi, 1)

                def copy_out(s, h, product_at, stored_at, kept=None, scale=1.0):
                    act.wait_ge(product, product_at)
                    if stored_at is not None:
                        act.wait_ge(stored[s], stored_at)
                    out = feat[:, s, :] if kept is None else K["tokT"][:, kept, :]
                    nc.scalar.activation(out[:, h * 512:(h + 1) * 512], ps_w[:, h, :], ACT.Copy,
                                         scale=scale).then_inc(evac, 1)

                for s in range(2):
                    act.wait_ge(w_in_[s], 16)
                    nc.scalar.activation(w_hi[:, s], w_raw[:, s], ACT.Copy).then_inc(split_hi, 1)
                for n in range(NFIX):
                    kept = n - 4 if FIXED[n][1] is None else None
                    for h in range(2):
                        copy_out(n % 2, h, 2 * n + h + 1, 16 * stores_before(n) or None, kept,
                                 -SCALE if n < 4 else 1.0)
                    split((16 * (n // 2 + 2), 2 * n + 2), n % 2)
                SB = [stores_before(NFIX + s) for s in range(2)]
                for first, end, scale in ((0, NFIX // 4, -SCALE), (NFIX // 4, NFIX // 2 - 1, 1.0)):
                    with act.Fori(first, end) as i:
                        for s in range(2):
                            for h in range(2):
                                copy_out(s, h, i * 4 + (2 * NFIX + 2 * s + h + 1), i * 16 + 16 * SB[s], scale=scale)
                            split((i * 16 + 16 * (NFIX // 2 + 2), i * 4 + (2 * NFIX + 2 * s + 2)), s)
                for s in range(2):
                    for h in range(2):
                        copy_out(s, h, 4 * NFIX - 4 + 2 * s + h + 1, 16 * (SB[s] + NFIX // 2 - 1))

                for n in range(3):
                    act.wait_ge(v_in, 16 * (6 if n == 2 else n + 1))
                    if n:
                        act.wait_ge(v_product, NT * n)
                    w = sum(x[1] for x in VCH[n])
                    nc.scalar.activation(v_hi[:, :, 0:w], v_raw[:, :, 0:w], ACT.Copy).then_inc(vs_hi, 1)

            @block.vector
            def _(dve):
                own = Tally(own_dve)
                dve.wait_ge(gain_in, 16)
                for t in range(NT):
                    dve.wait_ge(squared, t + 1)
                    nc.vector.tensor_scalar(rstd[:, t:t + 1], ss[:, t:t + 1], 1.0 / D, EPS, ALU.mult,
                                            ALU.add).then_inc(var, 1)
                    dve.wait_ge(rooted, t + 1)
                    own.inc(nc.vector.reciprocal(rstd[:, t:t + 1], rstd[:, NT + t:NT + t + 1]))
                    own.wait(dve)
                    if t >= 2:
                        dve.wait_ge(turned, 2 * (t - 1))
                    nc.vector.scalar_tensor_tensor(xn[:, t % 2, :], xt[:, t % XR, :], rstd[:, t:t + 1], gain[:],
                                                   ALU.mult, ALU.mult).then_inc(scaled, 1)
                    for h in range(2):
                        dve.wait_ge(up_hi, 2 * t + h + 1)
                        nc.vector.tensor_tensor(hT_lo[:, 4 * h:4 * h + 4, t * P:(t + 1) * P],
                                                ps_x[:, h, :].rearrange("p (k n) -> p k n", k=4),
                                                hT_hi[:, 4 * h:4 * h + 4, t * P:(t + 1) * P].bitcast(F32),
                                                ALU.subtract).then_inc(up_lo, 1)

                def split(s, at):
                    dve.wait_ge(split_hi, at)
                    nc.vector.tensor_tensor(w_lo[:, s], w_raw[:, s], w_hi[:, s].bitcast(F32),
                                            ALU.subtract).then_inc(split_lo, 1)

                for s in range(2):
                    split(s, s + 1)
                halves = 0
                for n, (_, _, rope) in enumerate(FIXED):
                    if rope:
                        for h in range(2):
                            halves += 1
                            dve.wait_ge(rotated, halves)
                            f = feat[:, n % 2, h * 512:(h + 1) * 512]
                            nc.vector.tensor_tensor(turn[:], ps_r[:], sin_t[:, h * 512:(h + 1) * 512],
                                                    ALU.mult).then_inc(turn_made, 1)
                            own.inc(nc.vector.tensor_tensor(f, f, cos_t[:, h * 512:(h + 1) * 512], ALU.mult))
                            own.wait(dve)
                            dve.wait_ge(turn_made, halves)
                            nc.vector.tensor_tensor(f, f, turn[:], ALU.add).then_inc(roped, 1)
                            dve.wait_ge(roped, halves)
                    split(n % 2, n + 3)
                with dve.Fori(0, NFIX // 2 - 1) as i:
                    for s in range(2):
                        split(s, i * 2 + (NFIX + s + 3))

                def v_split(n):
                    w = sum(x[1] for x in VCH[n])
                    dve.wait_ge(vs_hi, n + 1)
                    nc.vector.tensor_tensor(v_lo[:, :, 0:w], v_raw[:, :, 0:w], v_hi[:, :, 0:w].bitcast(F32),
                                            ALU.subtract).then_inc(vs_lo, 1)

                v_split(0)
                for n in range(3):
                    w = sum(x[1] for x in VCH[n])
                    for t in range(NT):
                        dve.wait_ge(v_product, n * NT + t + 1)
                        out = K["vb"][:, t, n * 256:(n + 1) * 256] if n < 2 else K["vsw"][:, t, 0:w]
                        nc.vector.tensor_copy(out, ps_w[:, t % 2, 0:w]).then_inc(v_evac, 1)
                    if n < 2:
                        v_split(n + 1)

            @block.tensor
            def _(pe):
                ident = K["c"][:, K_ID:K_ID + P]
                for t in range(NT):
                    pe.wait_ge(scaled, t + 1)
                    for h in range(2):
                        if t:
                            pe.wait_ge(up_lo, 2 * t + h - 1)
                        for j in range(4):
                            k = 4 * h + j
                            last = nc.tensor.transpose(ps_x[:, h, j * P:(j + 1) * P],
                                                       xn[:, t % 2, k * P:(k + 1) * P], ident)
                        last.then_inc(turned, 1)
                pe.wait_ge(up_lo, 2 * NT)

                def block_of(s, split_at, evac_at):
                    pe.wait_ge(split_hi, split_at)
                    pe.wait_ge(split_lo, split_at)
                    for h in range(2):
                        if evac_at is not None:
                            pe.wait_ge(evac, evac_at + h)
                        for k in range(KD):
                            last = mm3(nc, ps_w[:, h, :], w_hi[:, s, k, :], w_lo[:, s, k, :],
                                       hT_hi[:, k, h * 512:(h + 1) * 512], hT_lo[:, k, h * 512:(h + 1) * 512],
                                       k == 0, k == KD - 1)
                        last.then_inc(product, 1)

                halves = 0
                for n, (_, _, rope) in enumerate(FIXED):
                    block_of(n % 2, n + 1, 2 * n - 1 if n else None)
                    if rope:
                        for h in range(2):
                            pe.wait_ge(evac, 2 * n + h + 1)
                            if halves:
                                pe.wait_ge(turn_made, halves)
                            nc.tensor.matmul(ps_r[:], K["c"][:, K_ROT:K_ROT + P],
                                             feat[:, n % 2, h * 512:(h + 1) * 512], start=True,
                                             stop=True).then_inc(rotated, 1)
                            halves += 1
                with pe.Fori(0, NFIX // 2) as i:
                    for s in range(2):
                        block_of(s, i * 2 + (NFIX + s + 1), i * 4 + (2 * NFIX + 2 * s - 1))
                pe.wait_ge(evac, 4 * NFIX)
                for n in range(3):
                    w = sum(x[1] for x in VCH[n])
                    pe.wait_ge(vs_hi, n + 1)
                    pe.wait_ge(vs_lo, n + 1)
                    for t in range(NT):
                        m = n * NT + t
                        if m >= 2:
                            pe.wait_ge(v_evac, m - 1)
                        for k in range(KD):
                            ts = slice(t * P, (t + 1) * P)
                            last = mm3(nc, ps_w[:, t % 2, 0:w], hT_hi[:, k, ts], hT_lo[:, k, ts],
                                       v_hi[:, k, 0:w], v_lo[:, k, 0:w], k == 0, k == KD - 1)
                        last.then_inc(v_product, 1)


def stage_compress(nc, a, K, T):
    with Scope(nc, "cmp") as sc:
        PAIRS = CMP_BLOCK // 2
        N_WIN = S // CMP_STRIDE + 1
        tok = sc.sb("tok", [P, 2, GROUPS, S + CMP_BLOCK])
        w1 = sc.sb("w1", [P, 2, PAIRS, P])
        w2 = sc.sb("w2", [P, 2, HD])
        pe_rows = sc.sb("pe_rows", [PAIRS, 2, 2 * HD])
        bias = sc.sb("bias", [P, 2])
        hid = sc.sb("hid", [P, 4, 64])
        kc = sc.sb("kc", [P, 64])
        kc_turn = sc.sb("kc_turn", [P, 64])
        kc_dup = sc.sb("kc_dup", [P, GROUPS, 64])
        fT = sc.sb("fT", [NH, S])
        fe = sc.sb("fe", [NH, S])
        ones = sc.sb("ones", [NH, S])
        cum = sc.sb("cum", [NH, S])
        bf = sc.sb("bf", [NH, 1])
        cum_hi = sc.sb("cum_hi", [NH, S], F32R)
        cum_lo = sc.sb("cum_lo", [NH, S], F32R)
        bg = sc.sb("bg", [P, 3 * NH])
        ps_h = sc.ps("ps_h", [P, 2, 512])
        ps_b = sc.ps("ps_b", [P, 512])
        ps_k = sc.ps("ps_k", [P, 512])
        ps_f = sc.ps("ps_f", [P, 1024])
        pe_in, tok_in, small_in, own_dve, own_act, dup_in, cum_out = (
            sc.sem(n) for n in ("pe_in", "tok_in", "small_in", "own_dve", "own_act", "dup_in", "cum_out"))
        f_turned, f_copied, f_exp, f_ln, cum_made, pe_turned, pe_copied, bias_copied = (
            sc.sem(n) for n in ("f_turned", "f_copied", "f_exp", "f_ln", "cum_made", "pe_turned", "pe_copied",
                                "bias_copied"))
        hid_made, hid_act, k_made, k_copied, k_rotated, k_roped, v_made, fe_made = (
            sc.sem(n) for n in ("hid_made", "hid_act", "k_made", "k_copied", "k_rotated", "k_roped", "v_made",
                                "fe_made"))
        w1_in = [sc.sem(f"w1_in{kv}") for kv in range(2)]
        g_exp, gate_in = sc.sem("g_exp"), sc.sem("gate_in")
        hid_sig = sc.sem("hid_sig")
        c = K["c"]

        def hid_of(kv):
            return ps_h[:, kv, 0:GROUPS * N_WIN].rearrange("p (g n) -> p g n", g=GROUPS)

        with sc.block() as block:
            @block.sync
            def _(sp):
                for kv, pe_ in enumerate(("pe_cmp_k", "pe_cmp_v")):
                    sp.dma_start(pe_rows[:, kv, :], a[pe_][0].rearrange("(m h) d -> m (h d)", h=2)).then_inc(pe_in, 16)
                for g in range(GROUPS):
                    for h in range(2):
                        sp.dma_start(tok[h * HD:(h + 1) * HD, :, g, 0:S - h],
                                     K["tokT"][g * HD:(g + 1) * HD, :, h:S]).then_inc(tok_in, 16)
                for kv, w in enumerate(("w_cmp_k1", "w_cmp_v1")):
                    sp.dma_start(w1[:, kv, :, :], a[w].rearrange("l (m p) n -> (l p) m n", p=P)).then_inc(w1_in[kv], 16)
                sp.wait_ge(k_roped, 1)
                for g in range(GROUPS):
                    for half in range(2):
                        sp.dma_start(kc_dup[half * HD:(half + 1) * HD, g, :],
                                     kc[g * HD:(g + 1) * HD, :]).then_inc(dup_in, 16)
                sp.wait_ge(cum_made, 1)
                sp.dma_start(T["cum"][:, 0, :], cum_hi[:].bitcast(F32)).then_inc(cum_out, 16)
                sp.dma_start(T["cum"][:, 1, :], cum_lo[:].bitcast(F32)).then_inc(cum_out, 16)
                sp.wait_ge(cum_out, 32)

            @block.tensor
            def _(pe):
                ident = c[:, K_ID:K_ID + P]
                for t in range(NT):
                    last = nc.tensor.transpose(ps_f[0:NH, t * P:(t + 1) * P], K["vsw"][:, t, 280:288], ident)
                last.then_inc(f_turned, 1)
                pe.wait_ge(pe_in, 32)
                for kv in range(2):
                    last = nc.tensor.transpose(ps_b[:, kv * PAIRS:(kv + 1) * PAIRS], pe_rows[:, kv, :],
                                               ident[0:PAIRS, 0:PAIRS])
                last.then_inc(pe_turned, 1)
                pe.wait_ge(pe_copied, 2)
                pe.wait_ge(tok_in, 64)
                for kv in range(2):
                    pe.wait_ge(w1_in[kv], 16)
                    for m in range(PAIRS):
                        win = tok[:, kv, :, 2 * m:2 * m + CMP_STRIDE * (N_WIN - 1) + 1:CMP_STRIDE]
                        last = nc.tensor.matmul(hid_of(kv), w1[:, kv, m, :], win, start=(m == 0), stop=(m == PAIRS - 1))
                    last.then_inc(hid_made, 1)
                pe.wait_ge(small_in, 48)
                pe.wait_ge(hid_act, 2)
                for g in range(GROUPS):
                    last = nc.tensor.matmul(ps_k[g * HD:(g + 1) * HD, 0:N_CMP], w2[:, 0, :], hid[:, g, 0:N_CMP],
                                            start=True, stop=True)
                last.then_inc(k_made, 1)
                for g in range(GROUPS):
                    last = nc.tensor.matmul(ps_b[0:N_CMP, 256 + g * HD:256 + (g + 1) * HD], hid[:, 2 + g, 0:N_CMP],
                                            w2[:, 1, :], start=(g == 0), stop=(g == 1), skip_group_check=True)
                last.then_inc(v_made, 1)
                pe.wait_ge(k_copied, 1)
                nc.tensor.matmul(ps_k[:, 256:256 + N_CMP], c[:, K_ROT:K_ROT + P], kc[:, 0:N_CMP], start=True,
                                 stop=True).then_inc(k_rotated, 1)

            @block.scalar
            def _(act):
                act.dma_start(bf[:], a["b_forget"].rearrange("l h -> h l")).then_inc(small_in, 16)
                act.dma_start(bg[:], a["b_nsa_gate"].to_broadcast((P, 3 * NH))).then_inc(gate_in, 16)
                act.dma_start(w2[:, 0, :], a["w_cmp_k2"][0]).then_inc(small_in, 16)
                act.dma_start(w2[:, 1, :], a["w_cmp_v2"][0]).then_inc(small_in, 16)
                act.wait_ge(fe_made, 1)
                nc.scalar.activation(fe[:], fe[:], ACT.Exp).then_inc(f_exp, 1)
                act.wait_ge(gate_in, 17)
                nc.scalar.activation(K["gate"][:], K["gate"][:], ACT.Exp, scale=-1.0).then_inc(g_exp, 1)
                act.wait_ge(f_exp, 1)
                nc.scalar.activation(fe[:], fe[:], ACT.Ln, bias=1.0).then_inc(f_ln, 1)
                act.wait_ge(bias_copied, 1)
                for kv in range(2):
                    nc.scalar.activation(hid[:, 2 * kv:2 * kv + 2, 0:N_CMP], hid_of(kv)[:, :, 0:N_CMP], ACT.Sigmoid,
                                         bias=bias[:, kv:kv + 1]).then_inc(hid_sig, 1)

            @block.vector
            def _(dve):
                own = Tally(own_dve)

                def step(ins):
                    own.inc(ins)
                    own.wait(dve)

                own.inc(nc.vector.memset(ones[:], 1.0))
                own.inc(nc.vector.memset(K["vc"][:], 0.0))
                own.inc(nc.vector.memset(K["kc_raw"][:], 0.0))
                own.inc(nc.vector.memset(kc[:], 0.0))
                dve.wait_ge(pe_turned, 1)
                for g in range(GROUPS):
                    nc.vector.tensor_copy(tok[:, :, g, S:S + CMP_BLOCK - 1:2],
                                          ps_b[:, 0:2 * PAIRS].rearrange("p (a j) -> p a j", a=2)).then_inc(pe_copied, 1)
                dve.wait_ge(small_in, 48)
                dve.wait_ge(f_turned, 1)
                step(nc.vector.tensor_scalar(fT[:], ps_f[0:NH, :], bf[:, 0:1], None, ALU.add))
                step(nc.vector.tensor_scalar(fe[:], fT[:], -1.0, None, ALU.mult))
                step(nc.vector.tensor_tensor(fe[:], fe[:], fT[:], ALU.min))
                nc.vector.tensor_scalar(fT[:], fT[:], 0.0, None, ALU.min).then_inc(fe_made, 1)
                dve.wait_ge(gate_in, 16)
                nc.vector.tensor_tensor(K["gate"][:], K["vsw"][:, :, 256:280],
                                        bg[:].unsqueeze(1).to_broadcast((P, NT, 3 * NH)),
                                        ALU.add).then_inc(gate_in, 1)
                dve.wait_ge(g_exp, 1)
                step(nc.vector.tensor_scalar(K["gate"][:], K["gate"][:], 1.0, None, ALU.add))
                step(nc.vector.reciprocal(K["gate"][:], K["gate"][:]))
                dve.wait_ge(f_ln, 1)
                dve.wait_ge(fe_made, 1)
                step(nc.vector.tensor_tensor(fT[:], fT[:], fe[:], ALU.subtract))
                step(nc.vector.tensor_tensor_scan(cum[:], ones[:], fT[:], 0.0, ALU.mult, ALU.add))
                step(nc.vector.tensor_copy(cum_hi[:], cum[:]))
                nc.vector.tensor_tensor(cum_lo[:], cum[:], cum_hi[:].bitcast(F32), ALU.subtract).then_inc(cum_made, 1)
                dve.wait_ge(hid_made, 2)
                nc.vector.tensor_copy(bias[:], ps_h[:, :, N_WIN - 1]).then_inc(bias_copied, 1)
                dve.wait_ge(bias_copied, 1)
                for kv in range(2):
                    dve.wait_ge(hid_sig, kv + 1)
                    h = hid[:, 2 * kv:2 * kv + 2, 0:N_CMP]
                    nc.vector.scalar_tensor_tensor(h, hid_of(kv)[:, :, 0:N_CMP], bias[:, kv:kv + 1], h, ALU.add,
                                                   ALU.mult).then_inc(hid_act, 1)
                dve.wait_ge(k_made, 1)
                nc.vector.tensor_copy(kc[:, 0:N_CMP], ps_k[:, 0:N_CMP]).then_inc(k_copied, 1)
                dve.wait_ge(k_copied, 1)
                dve.wait_ge(v_made, 1)
                step(nc.vector.tensor_copy(K["vc"][0:N_CMP, :, :],
                                           ps_b[0:N_CMP, 256:384].rearrange("p (g d) -> p g d", g=GROUPS)))
                dve.wait_ge(k_rotated, 1)
                ends = slice(CMP_BLOCK - 1, CMP_BLOCK + CMP_STRIDE * (N_CMP - 1), CMP_STRIDE)
                step(nc.vector.tensor_tensor(kc_turn[:, 0:N_CMP], ps_k[:, 256:256 + N_CMP], K["sin"][:, ends], ALU.mult))
                step(nc.vector.tensor_tensor(kc[:, 0:N_CMP], kc[:, 0:N_CMP], K["cos"][:, ends], ALU.mult))
                nc.vector.tensor_tensor(kc[:, 0:N_CMP], kc[:, 0:N_CMP], kc_turn[:, 0:N_CMP], ALU.add
                                        ).then_inc(k_roped, 1)
                dve.wait_ge(dup_in, 64)
                step(nc.vector.tensor_copy(K["kc_raw"][:, :, 0:64], kc_dup[:]))
                step(nc.vector.tensor_copy(K["kc_hi"][:], K["kc_raw"][:]))
                step(nc.vector.tensor_tensor(K["kc_lo"][:], K["kc_raw"][:], K["kc_hi"][:].bitcast(F32), ALU.subtract))


class Soft:

    def __init__(self, at, blocks, gate):
        self.at, self.blocks, self.gate = at, blocks, gate


def attention_steps(sparse):
    steps = []
    for qt in range(NT):
        full = [("k", kt, "diag" if kt == qt else None) for kt in range(qt + 1)]
        steps.append((qt, full, [Soft(0, [("v", kt) for kt in range(qt + 1)], 1)]))
        if sparse:
            lo = max(0, qt - WB)
            near = [("w", kt, "diag" if kt == qt else "far" if kt == qt - WB else None) for kt in range(lo, qt + 1)]
            steps.append((qt, near + [("c", 0, ("cmp", qt))],
                          [Soft(0, [("vw", kt) for kt in range(lo, qt + 1)], 2), Soft(len(near), [("vc", 0)], 0)]))
    return steps


def stage_attention(nc, K, T, sparse):
    name = "nsa" if sparse else "fox"
    with Scope(nc, name) as sc:
        q_raw = [sc.sb(f"q_raw{s}", [P, S]) for s in range(2)]
        q_st = [sc.sb(f"q_st{s}", [P, S], F32R) for s in range(2)]
        q_tmp = sc.sb("q_tmp", [P, S], F32R)
        NK = GROUPS if sparse else 2
        k_raw = [sc.sb(f"k_raw{s}", [P, S]) for s in range(NK)]
        k_hi = [sc.sb(f"k_hi{s}", [P, S], F32R) for s in range(NK)]
        k_lo = [sc.sb(f"k_lo{s}", [P, S], F32R) for s in range(NK)]
        if sparse:
            w_hi = [sc.sb(f"w_hi{s}", [P, S], F32R) for s in range(NK)]
            w_lo = [sc.sb(f"w_lo{s}", [P, S], F32R) for s in range(NK)]
            gate_h = [sc.sb(f"gate_h{s}", [P, NT, 3]) for s in range(2)]
        else:
            v_h = [sc.sb(f"v_h{s}", [P, NT, HD]) for s in range(2)]
            cum_k = [sc.sb(f"cum_k{s}", [P, S], F32R) for s in range(2)]
            sel2 = sc.sb("sel2", [P, P], F32R)
        prob = sc.sb("prob", [P, 2, S])
        probT = sc.sb("probT", [P, 4, 4, P])
        o_h = [sc.sb(f"o_h{s}", [P, NT, HD]) for s in range(2)]
        mx = sc.sb("mx", [P, 2, 2])
        sums = sc.sb("sums", [P, 4, 2])
        wt = sc.sb("wt", [P, 4, 2])
        ps_s = sc.ps("ps_s", [P, 2, 1024])
        ps_t = sc.ps("ps_t", [P, 2, 512])
        ps_o = sc.ps("ps_o", [P, 2, 512])

        q_in = [sc.sem(f"q_in{s}") for s in range(2)]
        k_in = [sc.sem(f"k_in{s}") for s in range(2)]
        head_ready, head_done, o_kept, o_made = (
            [sc.sem(f"{n}{s}") for s in range(2)] for n in ("head_ready", "head_done", "o_kept", "o_made"))
        scored, maxed, expd, turned, weighed = (
            sc.sem(n) for n in ("scored", "maxed", "expd", "turned", "weighed"))
        evac = [sc.sem(f"evac{b}") for b in range(2)]
        passed, q_rounded, head_part = sc.sem("passed"), sc.sem("q_rounded"), sc.sem("head_part")
        q_bytes = 32 if sparse else 64
        pv_group, own_pool, own_dve, k_rounded = (
            sc.sem(n) for n in ("pv_group", "own_pool", "own_dve", "k_rounded"))
        k_ready = [sc.sem(f"k_ready{g}") for g in range(GROUPS)]
        k_rounded1 = sc.sem("k_rounded1")

        def at(softs, i):
            return slice(len(softs) - 1 - i, len(softs) - i)

        one = attention_steps(sparse)
        steps = [(s, *x) for s in range(2) for x in one]
        N = len(steps)
        groups = []
        for n, (s, qt, cols, softs) in enumerate(steps):
            for b in range(0, len(cols), 4):
                groups.append((n, b, min(4, len(cols) - b)))
        NGR = len(groups)
        assert NGR % 2 == 0
        first_group = [min(i for i, g in enumerate(groups) if g[0] == n) for n in range(N)] + [NGR]
        TURNS = NH // 2
        runs = [(0, 0, 2), (1, 2, 4)] if sparse else [(None, 0, TURNS)]
        head0 = 0 if sparse else NH

        def feat_rows(row, half):
            return T["feat"][row, half * HD:(half + 1) * HD, :]

        with sc.block() as block:
            @block.sync
            def _(sp):
                def load_raw(s, it):
                    for row0, dst in ((0 if sparse else 8, q_raw[s]),) + (() if sparse else ((12, k_raw[s]),)):
                        row = T["feat"][bass.ds(it + row0, 1)].rearrange("a p n -> p (a n)")
                        for half in range(2):
                            sp.dma_start(dst[half * HD:(half + 1) * HD, :],
                                         row[s * HD:(s + 1) * HD, :]).then_inc(q_in[s], 16)

                def load_cum(s, it):
                    sp.dma_start(cum_k[s][0:2, :].bitcast(F32),
                                 T["cum"][bass.ds(it * 2 + s, 1)].rearrange("a b n -> (a b) n")).then_inc(k_in[s], 16)

                def load_keys(w, g):
                    if w:
                        sp.wait_ge(k_ready[g], 1)
                    for half in range(2):
                        sp.dma_start(k_raw[g][half * HD:(half + 1) * HD, :], feat_rows(6 + w, g)).then_inc(k_in[g], 16)

                if sparse:
                    load_keys(0, 0)
                for s in range(2):
                    load_raw(s, 0)
                if sparse:
                    for w, g in ((1, 0), (0, 1), (1, 1)):
                        load_keys(w, g)
                if not sparse:
                    sp.wait_ge(own_dve, 3)
                    for s in range(2):
                        load_cum(s, 0)
                with sp.Fori(1, TURNS) as it:
                    for s in range(2):
                        sp.wait_ge(head_ready[s], it)
                        load_raw(s, it)
                    if not sparse:
                        for s in range(2):
                            sp.wait_ge(head_done[s], it)
                            load_cum(s, it)

            @block.gpsimd
            def _(pool):
                for s in range(2):
                    pool.sem_inc(o_kept[s], 1)
                PER = 3 if sparse else 5

                def prepare(s, it, before):
                    own = Tally(own_pool, before * (2 * PER) + s * PER)
                    wait_alone(pool, q_in[s], it * q_bytes + q_bytes, passed)
                    own.inc(nc.gpsimd.tensor_copy(q_tmp[:], q_raw[s][:]))
                    wait_alone(pool, own.sem, own.base + own.n, passed)
                    own.inc(nc.gpsimd.tensor_copy(q_st[s][0:HD, :], q_tmp[0:HD, :].bitcast(F32)))
                    if sparse:
                        own.inc(nc.gpsimd.tensor_copy(gate_h[s][:], K["gate"][:, :, bass.ds(it * 6 + s * 3, 3)]))
                    else:
                        own.inc(nc.gpsimd.tensor_copy(k_hi[s][:], k_raw[s][:]))
                        wait_alone(pool, own.sem, own.base + own.n, passed)
                        own.inc(nc.gpsimd.tensor_tensor(k_lo[s][:], k_raw[s][:], k_hi[s][:].bitcast(F32),
                                                        ALU.subtract))
                        own.inc(nc.gpsimd.tensor_copy(v_h[s][:], K["vb"][:, :, bass.ds(it * (2 * HD) + s * HD, HD)]))
                    wait_alone(pool, own.sem, own.base + own.n, passed)
                    nc.gpsimd.tensor_tensor(q_st[s][HD:P, :], q_raw[s][HD:P, :], q_tmp[HD:P, :].bitcast(F32),
                                            ALU.subtract).then_inc(head_ready[s], 1)
                    wait_alone(pool, head_ready[s], it + 1, passed)

                def keep(s, it):
                    wait_alone(pool, o_made[s], it + 1, passed)
                    nc.gpsimd.tensor_copy(K["o"][:, :, bass.ds(it * (2 * HD) + (head0 * HD + s * HD), HD)],
                                          o_h[s][:]).then_inc(o_kept[s], 1)

                if sparse:
                    for w, (hi, lo) in enumerate(((k_hi, k_lo), (w_hi, w_lo))):
                        pool.wait_ge(k_in[1], 32 * (w + 1))
                        nc.gpsimd.tensor_copy(hi[1][:], k_raw[1][:]).then_inc(k_rounded1, 1)
                        pool.wait_ge(k_rounded1, w + 1)
                        nc.gpsimd.tensor_tensor(lo[1][:], k_raw[1][:], hi[1][:].bitcast(F32),
                                                ALU.subtract).then_inc(k_ready[1], 1)
                with pool.Fori(0, TURNS - 1) as it:
                    for s in range(2):
                        keep(s, it)
                        wait_alone(pool, head_done[s], it + 1, passed)
                        prepare(s, it + 1, it)
                for s in range(2):
                    keep(s, TURNS - 1)
                    pool.wait_ge(o_kept[s], TURNS + 1)

            def turns(eng, body):
                for g, a0, a1 in runs:
                    with eng.Fori(a0, a1) as it:
                        body(g, it)

            @block.tensor
            def _(pe):
                ident = K["c"][:, K_ID:K_ID + P]
                if not sparse:
                    pe.wait_ge(own_dve, 3)

                def scores(g, it, n):
                    s, qt, cols, softs = steps[n]
                    if n % len(one) == 0:
                        pe.wait_ge(head_ready[s], it + 1)
                        if sparse:
                            pe.wait_ge(k_ready[g], 1)
                        else:
                            pe.wait_ge(k_in[s], it * 16 + 16)
                    if sparse and n == 1:
                        pe.wait_ge(k_ready[g], 2)
                    pe.wait_ge(expd, it * N + (n - 1 if n >= 2 else 0) + 1)
                    q = q_st[s][:, qt * P:(qt + 1) * P]
                    pieces, b = [], 0
                    while b < len(cols):
                        e = b + 1
                        while e < len(cols) and e % 4 and cols[e][0] == cols[b][0]:
                            e += 1
                        pieces.append((b, e))
                        b = e
                    started = set()
                    for i, (b, e) in enumerate(pieces):
                        src, kt, _ = cols[b]
                        out = ps_s[:, n % 2, b * P:e * P]
                        ks = slice(kt * P, (kt + e - b) * P)
                        kk = g if sparse else s
                        if src == "k":
                            parts = (k_hi[kk][:, ks], k_lo[kk][:, ks])
                        elif src == "w":
                            parts = (w_hi[kk][:, ks], w_lo[kk][:, ks])
                        else:
                            parts = (K["kc_hi"][:, kk, :], K["kc_lo"][:, kk, :])
                        bank = b // 4
                        masks = [(j, cols[j][2]) for j in range(b, e) if cols[j][2]]
                        lastpiece = i + 1 == len(pieces) or pieces[i + 1][0] // 4 != bank
                        last = nc.tensor.matmul(out, q, parts[0], start=bank not in started, stop=False,
                                                skip_group_check=True)
                        started.add(bank)
                        last = nc.tensor.matmul(out, q, parts[1], start=False,
                                                stop=lastpiece and not masks and sparse, skip_group_check=True)
                        if not sparse:
                            last = nc.tensor.matmul(out, sel2[:], cum_k[s][:, ks], start=False,
                                                    stop=lastpiece and not masks, skip_group_check=True)
                        for m, (j, kind) in enumerate(masks):
                            col = 0 if kind == "diag" else P if kind == "far" else (2 + kind[1]) * P
                            last = nc.tensor.matmul(ps_s[:, n % 2, j * P:(j + 1) * P], K["identb"][:],
                                                    K["maskb"][:, col:col + P], start=False,
                                                    stop=lastpiece and m == len(masks) - 1, skip_group_check=True)
                    last.then_inc(scored, 1)

                def turn_group(g, it, gr):
                    n, b, w = groups[gr]
                    pe.wait_ge(evac[gr % 2], it * (NGR // 2) + (gr // 2) + 1)
                    for j in range(w):
                        last = nc.tensor.transpose(ps_t[:, gr % 2, j * P:(j + 1) * P],
                                                   prob[:, n % 2, (b + j) * P:(b + j + 1) * P], ident)
                    last.then_inc(turned, 1)

                def values(g, it, gr):
                    n, b, w = groups[gr]
                    s, qt, cols, softs = steps[n]
                    pe.wait_ge(evac[gr % 2], it * (NGR // 2) + (gr // 2) + 2)
                    if gr == first_group[n]:
                        pe.wait_ge(weighed, it * N + (n - 1 if n >= 2 else 0) + 1)
                    for j in range(w):
                        blk = b + j
                        i = max(k for k, so in enumerate(softs) if so.at <= blk)
                        src, kt = softs[i].blocks[blk - softs[i].at]
                        if src == "v":
                            val = K["vsw"][:, kt, g * HD:(g + 1) * HD] if sparse else v_h[s][:, kt, :]
                        elif src == "vw":
                            val = K["vsw"][:, kt, 128 + g * HD:128 + (g + 1) * HD]
                        else:
                            val = K["vc"][:, g, :]
                        last = nc.tensor.matmul(ps_o[:, n % 2, i * HD:(i + 1) * HD], probT[:, gr % 4, j, :], val,
                                                start=(blk == 0), stop=(blk == softs[i].at + len(softs[i].blocks) - 1),
                                                skip_group_check=True)
                    last.then_inc(pv_group, 1)

                def body(g, it):
                    scores(g, it, 0)
                    scores(g, it, 1)
                    for n in range(N + 1):
                        if n < N:
                            pe.wait_ge(expd, it * N + (n + 2))
                            for gr in range(first_group[n], first_group[n + 1]):
                                turn_group(g, it, gr)
                        if n + 2 < N:
                            scores(g, it, n + 2)
                        if n:
                            for gr in range(first_group[n - 1], first_group[n]):
                                values(g, it, gr)
                        if n and n % len(one) == 0:
                            pe.wait_ge(pv_group, it * NGR + first_group[n])
                            pe.sem_inc(head_done[steps[n - 1][0]], 1)

                turns(pe, body)

            def copy_group(eng, it, gr, copy):
                n, b, w = groups[gr]
                eng.wait_ge(turned, it * NGR + (gr + 1))
                if gr >= 4:
                    eng.wait_ge(pv_group, it * NGR + (gr - 3))
                copy(probT[:, gr % 4, 0:w, :], ps_t[:, gr % 2, 0:w * P].rearrange("p (j n) -> p j n", n=P)
                     ).then_inc(evac[gr % 2], 1)

            @block.scalar
            def _(act):
                act.sem_inc(expd, 1)
                act.sem_inc(evac[1], 1)
                def keys(w):
                    act.wait_ge(k_in[0], 32 * (w + 1))
                    nc.scalar.activation((w_hi if w else k_hi)[0][:], k_raw[0][:], ACT.Copy).then_inc(k_rounded, 1)

                def first_head(s):
                    act.wait_ge(q_in[s], q_bytes)
                    if not sparse:
                        nc.scalar.activation(k_hi[s][:], k_raw[s][:], ACT.Copy).then_inc(k_rounded, 1)
                    if s:
                        act.wait_ge(head_ready[0], 1)
                    nc.scalar.activation(q_tmp[HD:P, :], q_raw[s][HD:P, :], ACT.Copy).then_inc(q_rounded, 1)
                    nc.scalar.activation(q_st[s][0:HD, :], q_raw[s][0:HD, :], ACT.Copy).then_inc(q_rounded, 1)

                if sparse:
                    keys(0)
                    first_head(0)
                    keys(1)
                    first_head(1)
                else:
                    first_head(0)
                    first_head(1)

                def exps(it, n):
                    s, qt, cols, softs = steps[n]
                    act.wait_ge(maxed, it * N + (n + 1))
                    if n >= 2:
                        act.wait_ge(turned, it * NGR + first_group[n - 1])
                    for i, so in enumerate(softs):
                        r = slice(so.at * P, (so.at + len(so.blocks)) * P)
                        last = nc.scalar.activation(prob[:, n % 2, r], ps_s[:, n % 2, r], ACT.Exp,
                                                    bias=mx[:, n % 2, i:i + 1], scale=-1.0,
                                                    accum_out=sums[:, n % 4, at(softs, i)])
                    last.then_inc(expd, 1)

                def body(g, it):
                    exps(it, 0)
                    exps(it, 1)
                    for n in range(N):
                        for gr in range(first_group[n], first_group[n + 1]):
                            if gr % 2 == 1:
                                copy_group(act, it, gr, lambda o, x: nc.scalar.activation(o, x, ACT.Copy))
                        if n + 2 < N:
                            exps(it, n + 2)

                turns(act, body)

            @block.vector
            def _(dve):
                dve.sem_inc(evac[0], 1)
                dve.sem_inc(weighed, 1)
                def keys(w):
                    hi, lo = (w_hi, w_lo) if w else (k_hi, k_lo)
                    dve.wait_ge(k_rounded, w + 1)
                    nc.vector.tensor_tensor(lo[0][:], k_raw[0][:], hi[0][:].bitcast(F32),
                                            ALU.subtract).then_inc(k_ready[0], 1)

                def first_head(s):
                    dve.wait_ge(q_in[s], q_bytes)
                    if sparse:
                        nc.vector.tensor_copy(gate_h[s][:], K["gate"][:, :, 3 * s:3 * s + 3]).then_inc(head_part, 1)
                    else:
                        nc.vector.tensor_copy(v_h[s][:], K["vb"][:, :, s * HD:(s + 1) * HD]).then_inc(head_part, 1)
                        dve.wait_ge(k_rounded, s + 1)
                        nc.vector.tensor_tensor(k_lo[s][:], k_raw[s][:], k_hi[s][:].bitcast(F32),
                                                ALU.subtract).then_inc(head_part, 1)
                    dve.wait_ge(q_rounded, 2 * s + 2)
                    dve.wait_ge(head_part, (s + 1) * (1 if sparse else 2))
                    nc.vector.tensor_tensor(q_st[s][HD:P, :], q_raw[s][HD:P, :], q_tmp[HD:P, :].bitcast(F32),
                                            ALU.subtract).then_inc(head_ready[s], 1)

                if sparse:
                    keys(0)
                    first_head(0)
                    keys(1)
                    first_head(1)
                else:
                    nc.vector.tensor_copy(sel2[:], K["c"][:, K_ONE:K_ONE + P]).then_inc(own_dve, 1)
                    for s in range(2):
                        nc.vector.tensor_scalar(cum_k[s][:], K["cos"][:], 0.0, None, ALU.mult).then_inc(own_dve, 1)
                    first_head(0)
                    first_head(1)

                OWN0 = 0 if sparse else 3

                def max_of(it, n):
                    s, qt, cols, softs = steps[n]
                    dve.wait_ge(scored, it * N + (n + 1))
                    if n >= 2:
                        dve.wait_ge(expd, it * N + n)
                    else:
                        dve.wait_ge(expd, it * N + 1)
                    for i, so in enumerate(softs):
                        r = slice(so.at * P, (so.at + len(so.blocks)) * P)
                        last = nc.vector.tensor_reduce(mx[:, n % 2, i:i + 1], ps_s[:, n % 2, r], X, ALU.min)
                    last.then_inc(maxed, 1)

                def weigh(it, n, own):
                    s, qt, cols, softs = steps[n]
                    k = len(softs)
                    dve.wait_ge(pv_group, it * NGR + first_group[n + 1])
                    w = wt[:, n % 4, 0:k]
                    own.inc(nc.vector.reciprocal(w, sums[:, n % 4, 0:k]))
                    own.wait(dve)
                    o = o_h[s][:, qt, :]
                    if n % len(one) == 0:
                        dve.wait_ge(o_kept[s], it + 1)
                    if not sparse:
                        nc.vector.tensor_scalar(o, ps_o[:, n % 2, 0:HD], w, None,
                                                ALU.mult).then_inc(weighed, 1)
                    elif k == 1:
                        nc.vector.tensor_scalar(o, ps_o[:, n % 2, 0:HD], w, gate_h[s][:, qt, 1:2],
                                                ALU.mult, ALU.mult).then_inc(weighed, 1)
                    else:
                        own.inc(nc.vector.tensor_tensor(w, w, gate_h[s][:, qt, 0:3:2], ALU.mult))
                        own.wait(dve)
                        if qt == 0:
                            own.inc(nc.vector.tensor_tensor(wt[:, n % 4, 0:1], wt[:, n % 4, 0:1],
                                                            K["c"][:, K_VALID:K_VALID + 1], ALU.mult))
                            own.wait(dve)
                        dve.wait_ge(weighed, it * N + (n + 1))
                        own.inc(nc.vector.scalar_tensor_tensor(o, ps_o[:, n % 2, 0:HD], wt[:, n % 4, 1:2], o,
                                                               ALU.mult, ALU.add))
                        own.wait(dve)
                        nc.vector.scalar_tensor_tensor(o, ps_o[:, n % 2, HD:2 * HD], wt[:, n % 4, 0:1], o,
                                                       ALU.mult, ALU.add).then_inc(weighed, 1)
                    if n % len(one) == len(one) - 1:
                        dve.wait_ge(weighed, it * N + (n + 2))
                        dve.sem_inc(o_made[s], 1)

                def plan(own, it):
                    max_of(it, 0)
                    max_of(it, 1)
                    for n in range(N):
                        for gr in range(first_group[n], first_group[n + 1]):
                            if gr % 2 == 0:
                                copy_group(dve, it, gr, nc.vector.tensor_copy)
                        if n >= 2:
                            weigh(it, n - 2, own)
                        if n + 2 < N:
                            max_of(it, n + 2)
                    weigh(it, N - 2, own)
                    weigh(it, N - 1, own)

                OWN = 2 * N + 2 if sparse else N

                def body(g, it):
                    own = Tally(own_dve, it * OWN + OWN0)
                    plan(own, it)
                    assert own.n == OWN, (own.n, OWN)

                turns(dve, body)


def stage_mix(nc, a, K, T):
    with Scope(nc, "mix") as sc:
        HALF = NH * HD
        w_raw = sc.sb("w_raw", [P, 2, D])
        w_hi = sc.sb("w_hi", [P, KD, D], F32R)
        w_lo = sc.sb("w_lo", [P, KD, D], F32R)
        beta = sc.sb("beta", [P, D])
        gain = sc.sb("gain", [P, D])
        w_rt = sc.sb("w_rt", [P, KD, NG + NE])
        b_rt = sc.sb("b_rt", [1, NG + NE])
        junk = sc.sb("junk", [P, D], BF16)
        ss = sc.sb("ss", [P, NT, 3])
        rt = sc.sb("rt", [P, NT, 3])
        rs = sc.sb("rs", [P, NT, 3])
        xt = sc.sb("x", [P, 2, D])
        mT_hi = sc.sb("mT_hi", [P, 2, KD, P], F32R)
        mT_lo = sc.sb("mT_lo", [P, 2, KD, P], F32R)
        ht = sc.sb("h", [P, 2, D])
        ut = sc.sb("u", [P, 2, D])
        uT = sc.sb("uT", [P, KD, P])
        ps_x = sc.ps("ps_x", [P, 2, 512])
        ps_y = sc.ps("ps_y", [P, 2, 512])
        ps_u = sc.ps("ps_u", [P, 2, 512])
        ps_l = sc.ps("ps_l", [P, 512])
        w_in = [sc.sem(f"w_in{i}") for i in range(2)]
        x_in = [sc.sem(f"x_in{i}") for i in range(2)]
        h_out = [sc.sem(f"h_out{i}") for i in range(2)]
        u_out = [sc.sem(f"u_out{i}") for i in range(2)]
        (vec_in, rt_in, split_hi, split_lo, o_sq, o_var, o_root, o_norm, turned, m_hi, m_lo, product, h_made, h_sq,
         h_var, h_root, u_made, u_turned, u_copied, logits, own_dve) = (
            sc.sem(n) for n in ("vec_in", "rt_in", "split_hi", "split_lo", "o_sq", "o_var", "o_root", "o_norm",
                                "turned", "m_hi", "m_lo", "product", "h_made", "h_sq", "h_var", "h_root", "u_made",
                                "u_turned", "u_copied", "logits", "own_dve"))
        x_d = a["x"].rearrange("b (t p) d -> (b t) p d", p=P)
        w_d = a["w_out"].rearrange("l (k p) n -> (l k) p n", p=P)
        with sc.block() as block:
            @block.sync
            def _(sp):
                sp.dma_start(beta[:, 0:HALF], a["beta_nsa"].to_broadcast((P, HALF))).then_inc(vec_in, 16)
                sp.dma_start(beta[:, HALF:D], a["beta_fox"].to_broadcast((P, HALF))).then_inc(vec_in, 16)
                sp.dma_start(gain[:], a["g_ffn"].to_broadcast((P, D))).then_inc(vec_in, 16)
                for k in range(KD):
                    if k >= 2:
                        sp.wait_ge(split_hi, k - 1)
                        sp.wait_ge(split_lo, k - 1)
                    sp.dma_start(w_raw[:, k % 2, :], w_d[k]).then_inc(w_in[k % 2], 16)
                    if k < 2:
                        sp.dma_start(xt[:, k, :], x_d[k]).then_inc(x_in[k], 16)
                sp.dma_start(w_rt[:, :, 0:NG], a["w_group"].rearrange("l (k p) n -> (l p) k n", p=P)).then_inc(rt_in, 16)
                sp.dma_start(w_rt[:, :, NG:], a["w_router"].rearrange("l (k p) n -> (l p) k n", p=P)).then_inc(rt_in, 16)
                sp.dma_start(b_rt[:, 0:NG], a["b_group"]).then_inc(rt_in, 16)
                sp.dma_start(b_rt[:, NG:], a["b_router"]).then_inc(rt_in, 16)
                for t in range(NT):
                    sp.wait_ge(h_made, 2 * t + 2)
                    sp.dma_start(T["h"][t], ht[:, t % 2, :]).then_inc(h_out[t % 2], 16)
                    if t + 2 < NT:
                        sp.dma_start(xt[:, t % 2, :], x_d[t + 2]).then_inc(x_in[t % 2], 16)
                    sp.wait_ge(u_made, t + 1)
                    sp.dma_start(T["u"][t * P:(t + 1) * P, :], ut[:, t % 2, :]).then_inc(u_out[t % 2], 16)
                for s in range(2):
                    sp.wait_ge(h_out[s], 16 * (NT // 2))
                    sp.wait_ge(u_out[s], 16 * (NT // 2))

            def tiles(norm, turn, leave, mix, route, split):
                norm(0)
                turn(0)
                norm(1)
                split()
                for i in range(NT + 2):
                    if i >= 2:
                        route(i - 2)
                    if 1 <= i <= NT:
                        leave(i - 1)
                    if i + 1 < NT:
                        turn(i + 1)
                    if 1 <= i <= NT:
                        mix(i - 1)
                    if i + 2 < NT:
                        norm(i + 2)

            @block.scalar
            def _(act):
                def split():
                    for k in range(KD):
                        act.wait_ge(w_in[k % 2], 16 * (k // 2 + 1))
                        nc.scalar.activation(w_hi[:, k, :], w_raw[:, k % 2, :], ACT.Copy).then_inc(split_hi, 1)

                def norm(t):
                    for g in range(2):
                        nc.scalar.activation(junk[:, g * HALF:(g + 1) * HALF],
                                             K["o"][:, t, g * HALF:(g + 1) * HALF], ACT.Square,
                                             accum_out=ss[:, t, g:g + 1]).then_inc(o_sq, 1)
                    act.wait_ge(o_var, t + 1)
                    nc.scalar.activation(rt[:, t, 0:2], rt[:, t, 0:2], ACT.Sqrt).then_inc(o_root, 1)

                def turn(t):
                    for h in range(2):
                        act.wait_ge(turned, 2 * t + h + 1)
                        if t >= 2:
                            act.wait_ge(product, t - 1)
                        nc.scalar.activation(mT_hi[:, t % 2, 4 * h:4 * h + 4, :],
                                             ps_x[:, h, :].rearrange("p (k n) -> p k n", k=4),
                                             ACT.Copy).then_inc(m_hi, 1)

                def leave(t):
                    pass

                def mix(t):
                    act.wait_ge(h_made, 2 * t + 2)
                    nc.scalar.activation(junk[:], ht[:, t % 2, :], ACT.Square,
                                         accum_out=ss[:, t, 2:3]).then_inc(h_sq, 1)
                    act.wait_ge(h_var, t + 1)
                    nc.scalar.activation(rt[:, t, 2:3], rt[:, t, 2:3], ACT.Sqrt).then_inc(h_root, 1)

                def route(t):
                    for h in range(2):
                        act.wait_ge(u_turned, 2 * t + h + 1)
                        if t:
                            act.wait_ge(logits, t)
                        nc.scalar.activation(uT[:, 4 * h:4 * h + 4, :],
                                             ps_u[:, h, :].rearrange("p (k n) -> p k n", k=4),
                                             ACT.Copy).then_inc(u_copied, 1)

                tiles(norm, turn, leave, mix, route, split)

            @block.vector
            def _(dve):
                own = Tally(own_dve)

                def split():
                    for k in range(KD):
                        dve.wait_ge(split_hi, k + 1)
                        nc.vector.tensor_tensor(w_lo[:, k, :], w_raw[:, k % 2, :], w_hi[:, k, :].bitcast(F32),
                                                ALU.subtract).then_inc(split_lo, 1)

                dve.wait_ge(vec_in, 48)

                def norm(t):
                    dve.wait_ge(o_sq, 2 * t + 2)
                    nc.vector.tensor_scalar(rt[:, t, 0:2], ss[:, t, 0:2], 1.0 / HALF, EPS, ALU.mult,
                                            ALU.add).then_inc(o_var, 1)
                    dve.wait_ge(o_root, t + 1)
                    own.inc(nc.vector.reciprocal(rs[:, t, 0:2], rt[:, t, 0:2]))
                    own.wait(dve)
                    for g in range(2):
                        og = K["o"][:, t, g * HALF:(g + 1) * HALF]
                        nc.vector.scalar_tensor_tensor(og, og, rs[:, t, g:g + 1], beta[:, g * HALF:(g + 1) * HALF],
                                                       ALU.mult, ALU.mult).then_inc(o_norm, 1)

                def turn(t):
                    for h in range(2):
                        dve.wait_ge(m_hi, 2 * t + h + 1)
                        nc.vector.tensor_tensor(mT_lo[:, t % 2, 4 * h:4 * h + 4, :],
                                                ps_x[:, h, :].rearrange("p (k n) -> p k n", k=4),
                                                mT_hi[:, t % 2, 4 * h:4 * h + 4, :].bitcast(F32),
                                                ALU.subtract).then_inc(m_lo, 1)

                def leave(t):
                    dve.wait_ge(product, t + 1)
                    dve.wait_ge(x_in[t % 2], 16 * (t // 2 + 1))
                    if t >= 2:
                        dve.wait_ge(h_out[t % 2], 16 * (t // 2))
                    for h in range(2):
                        r = slice(h * 512, (h + 1) * 512)
                        nc.vector.tensor_tensor(ht[:, t % 2, r], ps_y[:, h, :], xt[:, t % 2, r],
                                                ALU.add).then_inc(h_made, 1)

                def mix(t):
                    dve.wait_ge(h_sq, t + 1)
                    nc.vector.tensor_scalar(rt[:, t, 2:3], ss[:, t, 2:3], 1.0 / D, EPS, ALU.mult,
                                            ALU.add).then_inc(h_var, 1)
                    dve.wait_ge(h_root, t + 1)
                    own.inc(nc.vector.reciprocal(rs[:, t, 2:3], rt[:, t, 2:3]))
                    own.wait(dve)
                    if t >= 2:
                        dve.wait_ge(u_out[t % 2], 16 * (t // 2))
                        dve.wait_ge(u_turned, 2 * (t - 1))
                    nc.vector.scalar_tensor_tensor(ut[:, t % 2, :], ht[:, t % 2, :], rs[:, t, 2:3], gain[:],
                                                   ALU.mult, ALU.mult).then_inc(u_made, 1)

                def route(t):
                    pass

                tiles(norm, turn, leave, mix, route, split)
                dve.wait_ge(logits, NT)
                own.inc(nc.vector.tensor_copy(K["lg"][:], ps_l[:, 0:NT * (NG + NE)].rearrange("p (t n) -> p t n", t=NT)))
                own.wait(dve)

            @block.tensor
            def _(pe):
                ident = K["c"][:, K_ID:K_ID + P]

                def turn(t):
                    pe.wait_ge(o_norm, 2 * t + 2)
                    for h in range(2):
                        if t:
                            pe.wait_ge(m_lo, 2 * t + h - 1)
                        for j in range(4):
                            k = 4 * h + j
                            last = nc.tensor.transpose(ps_x[:, h, j * P:(j + 1) * P],
                                                       K["o"][:, t, k * P:(k + 1) * P], ident)
                        last.then_inc(turned, 1)

                def mix(t):
                    pe.wait_ge(m_lo, 2 * t + 2)
                    for h in range(2):
                        if t:
                            pe.wait_ge(h_made, 2 * t + h - 1)
                        for k in range(KD):
                            if t == 0 and h == 0:
                                pe.wait_ge(split_lo, k + 1)
                            last = mm3(nc, ps_y[:, h, :], mT_hi[:, t % 2, k, :], mT_lo[:, t % 2, k, :],
                                       w_hi[:, k, h * 512:(h + 1) * 512], w_lo[:, k, h * 512:(h + 1) * 512],
                                       k == 0, k == KD - 1)
                    last.then_inc(product, 1)

                def turn_u(t):
                    pe.wait_ge(u_made, t + 1)
                    for h in range(2):
                        if t:
                            pe.wait_ge(u_copied, 2 * t + h - 1)
                        for j in range(4):
                            k = 4 * h + j
                            last = nc.tensor.transpose(ps_u[:, h, j * P:(j + 1) * P],
                                                       ut[:, t % 2, k * P:(k + 1) * P], ident)
                        last.then_inc(u_turned, 1)

                def route(t):
                    pe.wait_ge(u_copied, 2 * t + 2)
                    pe.wait_ge(rt_in, 64)
                    out = ps_l[:, t * (NG + NE):(t + 1) * (NG + NE)]
                    for k in range(KD):
                        nc.tensor.matmul(out, uT[:, k, :], w_rt[:, k, :], start=(k == 0), stop=False)
                    nc.tensor.matmul(out, K["c"][0:1, K_ONE:K_ONE + P], b_rt[:], start=False,
                                     stop=True).then_inc(logits, 1)

                turn(0)
                for i in range(NT + 2):
                    if i + 1 < NT:
                        turn(i + 1)
                    if i >= 2:
                        route(i - 2)
                    if i < NT:
                        mix(i)
                    if 1 <= i <= NT:
                        turn_u(i - 1)


def stage_route(nc, K, T):
    with Scope(nc, "rte") as sc:
        def sb(name, *shape):
            return sc.sb(name, [P, *shape])

        gmax, gsum, gp, pm = (sb(n, NT) for n in ("gmax", "gsum", "gp", "pm"))
        dlt, pri, ohg, il, oh1, oh2, il2 = (sb(n, NT, 4) for n in ("dlt", "pri", "ohg", "il", "oh1", "oh2", "il2"))
        m1, m2, e2, v1 = (sb(n, NT) for n in ("m1", "m2", "e2", "v1"))
        prod = sb("prod", NT, NG, EPG)
        pick = [sb(f"pick{k}", NT, NG, EPG) for k in range(2)]
        both = sb("both", NT * NE)
        off = sb("off", NT + 1, NE)
        tot = sb("tot", NT, NE)
        where = sb("where", NT, NE)
        cnt_i = sc.sb("cnt_i", [P, NE], I32)
        ntl, cend, cbeg, ones = (sb(n, NE) for n in ("ntl", "cend", "cbeg", "ones"))
        tile_ge = sb("tile_ge", 32, NE)
        tile_e = sb("tile_e", 32)
        n_last = sb("n_last", 1)
        slot_f = sb("slot_f", NT)
        tok_i = sc.sb("tok_i", [P, NT], U32)
        y_zero = sc.sb("y_zero", [P, D])
        zeros_i = sc.sb("zeros_i", [P, SLOTS // P], U32)
        ps_r = sc.ps("ps_r", [P, 512])
        ps_t = sc.ps("ps_t", [P, 512])
        own_dve, expd, want_exp, ranked, both_made, slots_made, zero_made, last_made, y_zeroed = (
            sc.sem(n) for n in ("own_dve", "expd", "want_exp", "ranked", "both_made", "slots_made", "zero_made",
                                "last_made", "y_zeroed"))
        zero_out, scattered, back = T["zero_out"], T["scattered"], T["back"]
        c = K["c"]
        lg = K["lg"]
        slots_d = T["slots"]
        with sc.block() as block:
            @block.vector
            def _(dve):
                own = Tally(own_dve)

                def step(ins):
                    own.inc(ins)
                    own.wait(dve)

                V = nc.vector

                def wide(x, n=4):
                    return x[:].unsqueeze(2).to_broadcast((P, NT, n))

                def first_max(x, top, out):
                    step(V.tensor_tensor(pri[:], x, wide(top), ALU.is_equal))
                    step(V.tensor_tensor(pri[:], pri[:], c[:, K_PRI:K_PRI + 4].unsqueeze(1).to_broadcast((P, NT, 4)),
                                         ALU.mult))
                    step(V.tensor_reduce(pm[:], pri[:], X, ALU.max))
                    step(V.tensor_tensor(out[:], pri[:], wide(pm), ALU.is_equal))

                V.memset(zeros_i[:], 0).then_inc(zero_made, 1)
                V.memset(y_zero[:], 0.0).then_inc(zero_made, 1)
                step(V.memset(ones[:], 1.0))
                step(V.tensor_reduce(gmax[:], lg[:, :, 0:NG], X, ALU.max))
                V.tensor_tensor(dlt[:], lg[:, :, 0:NG], wide(gmax), ALU.subtract).then_inc(want_exp, 1)
                first_max(lg[:, :, 0:NG], gmax, ohg)
                step(V.tensor_tensor(prod[:], lg[:, :, NG:].rearrange("p t (g j) -> p t g j", g=NG),
                                     ohg[:].unsqueeze(3).to_broadcast((P, NT, NG, EPG)), ALU.mult))
                step(V.tensor_reduce(il[:], prod[:].rearrange("p t g j -> p t j g"), X, ALU.add))
                step(V.tensor_reduce(m1[:], il[:], X, ALU.max))
                first_max(il[:], m1, oh1)
                step(V.scalar_tensor_tensor(il2[:], oh1[:], NEG, il[:], ALU.mult, ALU.add))
                step(V.tensor_reduce(m2[:], il2[:], X, ALU.max))
                first_max(il2[:], m2, oh2)
                V.tensor_tensor(e2[:], m2[:], m1[:], ALU.subtract).then_inc(want_exp, 1)
                for k, oh in enumerate((oh1, oh2)):
                    step(V.tensor_tensor(pick[k][:], ohg[:].unsqueeze(3).to_broadcast((P, NT, NG, EPG)),
                                         oh[:].unsqueeze(2).to_broadcast((P, NT, NG, EPG)), ALU.mult))
                V.tensor_tensor(both[:], pick[0][:].rearrange("p t g j -> p (t g j)"),
                                pick[1][:].rearrange("p t g j -> p (t g j)"), ALU.add).then_inc(both_made, 1)
                dve.wait_ge(expd, 2)
                step(V.tensor_reduce(gsum[:], dlt[:], X, ALU.add))
                step(V.reciprocal(gp[:], gsum[:]))
                step(V.tensor_scalar(v1[:], e2[:], 1.0, None, ALU.add))
                step(V.reciprocal(v1[:], v1[:]))
                step(V.tensor_tensor(K["cw"][:, 0, :], v1[:], gp[:], ALU.mult))
                step(V.tensor_tensor(K["cw"][:, 1, :], K["cw"][:, 0, :], e2[:], ALU.mult))
                dve.wait_ge(ranked, 2)
                step(V.tensor_copy(tot[:], ps_t[:, 0:NT * NE].rearrange("p (t e) -> p t e", t=NT)))
                step(V.memset(off[:, 0, :], 0.0))
                for t in range(NT):
                    step(V.tensor_tensor(off[:, t + 1, :], off[:, t, :], tot[:, t, :], ALU.add))
                step(V.tensor_scalar(ntl[:], off[:, NT, :], float(P - 1), None, ALU.add))
                step(V.tensor_copy(cnt_i[:], ntl[:]))
                step(V.tensor_scalar(cnt_i[:], cnt_i[:], 7, None, ALU.arith_shift_right))
                step(V.tensor_copy(ntl[:], cnt_i[:]))
                step(V.tensor_tensor_scan(cend[:], ones[:], ntl[:], 0.0, ALU.mult, ALU.add))
                step(V.tensor_tensor(cbeg[:], cend[:], ntl[:], ALU.subtract))
                step(V.tensor_tensor(where[:], ps_r[:, 0:NT * NE].rearrange("p (t e) -> p t e", t=NT),
                                     off[:, 0:NT, :], ALU.add))
                step(V.scalar_tensor_tensor(where[:], cbeg[:].unsqueeze(1).to_broadcast((P, NT, NE)), float(P),
                                            where[:], ALU.mult, ALU.add))
                for k in range(2):
                    step(V.tensor_tensor(prod[:].rearrange("p t g j -> p t (g j)"), where[:],
                                         pick[k][:].rearrange("p t g j -> p t (g j)"), ALU.mult))
                    step(V.tensor_reduce(slot_f[:], prod[:].rearrange("p t g j -> p t (g j)"), X, ALU.add))
                    step(V.tensor_copy(K["slot"][:, k, :], slot_f[:]))
                step(V.tensor_tensor(tile_ge[:], c[:, K_TILE:K_TILE + 32].unsqueeze(2).to_broadcast((P, 32, NE)),
                                     cend[:].unsqueeze(1).to_broadcast((P, 32, NE)), ALU.is_ge))
                step(V.tensor_reduce(tile_e[:], tile_ge[:], X, ALU.add))
                step(V.tensor_scalar(tile_e[:], tile_e[:], float(NE - 1), None, ALU.min))
                step(V.tensor_copy(K["texp"][:], tile_e[:]))
                step(V.tensor_scalar(n_last[:], cend[:, NE - 1:NE], -1.0, None, ALU.add))
                V.tensor_copy(K["last"][:], n_last[:]).then_inc(last_made, 1)
                step(V.memset(K["tnew"][:], 1))
                step(V.tensor_tensor(K["tnew"][:, 1:], tile_e[:, 1:], tile_e[:, 0:31], ALU.not_equal))
                V.tensor_copy(tok_i[:], c[:, K_TOK:K_TOK + NT]).then_inc(slots_made, 1)

            @block.sync
            def _(sp):
                sp.wait_ge(zero_made, 2)
                sp.wait_ge(last_made, 1)
                end = sp.value_load(K["last"][0:1, 0:1], min_val=FEWEST - 1, max_val=TILES - 1)
                with sp.Fori(FEWEST, TILES) as i:
                    with sp.If(i < end + 1):
                        sp.sem_inc(y_zeroed, 16)
                    with sp.Else():
                        sp.dma_start(T["y"][bass.ds(i * P, P), :], y_zero[:]).then_inc(y_zeroed, 16)
                sp.wait_ge(y_zeroed, 16 * (TILES - FEWEST))

            @block.scalar
            def _(act):
                act.wait_ge(want_exp, 1)
                nc.scalar.activation(dlt[:], dlt[:], ACT.Exp).then_inc(expd, 1)
                act.wait_ge(want_exp, 2)
                nc.scalar.activation(e2[:], e2[:], ACT.Exp).then_inc(expd, 1)

            @block.tensor
            def _(pe):
                pe.wait_ge(both_made, 1)
                nc.tensor.matmul(ps_r[:, 0:NT * NE], c[:, K_LT:K_LT + P], both[:], start=True, stop=True).then_inc(ranked, 1)
                nc.tensor.matmul(ps_t[:, 0:NT * NE], c[:, K_ONE:K_ONE + P], both[:], start=True, stop=True).then_inc(ranked, 1)

            @block.gpsimd
            def _(pool):
                pool.wait_ge(zero_made, 1)
                pool.dma_start(slots_d.rearrange("(p n) a -> p (n a)", p=P), zeros_i[:]).then_inc(zero_out, 16)
                pool.wait_ge(zero_out, 16)
                pool.wait_ge(slots_made, 1)
                for k in range(2):
                    for t in range(NT):
                        pool.indirect_dma_start(slots_d, bass.IndirectOffsetOnAxis(ap=K["slot"][:, k, t:t + 1], axis=0),
                                                tok_i[:, t:t + 1], None).then_inc(scattered, 16)
                pool.wait_ge(scattered, 16 * 2 * NT)
                pool.dma_start(K["stok"][:], slots_d.rearrange("(n p) a -> p (n a)", p=P),
                               allow_slow_non_contiguous=True).then_inc(back, 16)
                pool.wait_ge(back, 16)


def stage_moe(nc, a, K, T):
    GC, DC = KD, KF
    EARLY = 4
    GR, DR = GC, DC
    with Scope(nc, "moe") as sc:
        g_raw = sc.sb("g_raw", [P, GC, 2, FE])
        d_raw = sc.sb("d_raw", [P, DC, D])
        g_hi = sc.sb("g_hi", [P, GR, 2, FE], F32R)
        g_lo = sc.sb("g_lo", [P, GR, 2, FE], F32R)
        d_hi = sc.sb("d_hi", [P, DR, D], F32R)
        d_lo = sc.sb("d_lo", [P, DR, D], F32R)
        xg = sc.sb("xg", [P, D])
        idx = sc.sb("idx", [P, 1], U32)
        xT_hi = sc.sb("xT_hi", [P, KD, P], F32R)
        xT_lo = sc.sb("xT_lo", [P, KD, P], F32R)
        act_g = sc.sb("act_g", [P, FE])
        hid = sc.sb("hid", [P, FE])
        hT_hi = sc.sb("hT_hi", [P, KF, P], F32R)
        hT_lo = sc.sb("hT_lo", [P, KF, P], F32R)
        y = sc.sb("y", [P, D])
        ps_x = sc.ps("ps_x", [P, 2, 512])
        ps_g = sc.ps("ps_g", [P, 2, 512])
        ps_h = sc.ps("ps_h", [P, 512])
        ps_y = sc.ps("ps_y", [P, 2, 512])
        g_in = [sc.sem(f"g_in{c}") for c in range(GC)]
        d_in = [sc.sem(f"d_in{c}") for c in range(DC)]
        (s_ghi, s_glo, s_dhi, s_dlo, g_used, d_used, idx_set, x_turned, x_hi, x_lo, silu_made, h_made, h_turned,
         h_hi, h_lo, y_made, y_out) = (
            sc.sem(n) for n in ("s_ghi", "s_glo", "s_dhi", "s_dlo", "g_used", "d_used", "idx_set", "x_turned",
                                "x_hi", "x_lo", "silu_made", "h_made", "h_turned", "h_hi", "h_lo", "y_made", "y_out"))
        passed, ended = sc.sem("passed"), sc.sem("ended")
        x_in = T["xg_in"]
        wg_d, wu_d, wd_d = a["w_gate_e"][0], a["w_up_e"][0], a["w_down_e"][0]
        c = K["c"]

        def turns(eng, first, end, body, ahead=0):
            with eng.Fori(first, FEWEST + ahead) as i:
                body(i)
            with eng.Fori(FEWEST + ahead, TILES + ahead) as i:
                with eng.If(i < end + (1 + ahead)):
                    body(i)

        def last_used(eng):
            return eng.value_load(K["last"][0:1, 0:1], min_val=FEWEST - 1, max_val=TILES - 1)

        with sc.block() as block:
            @block.sync
            def _(sp):
                def load_g(e, i=None):
                    for ch in range(GC):
                        if i is not None:
                            sp.wait_ge(s_ghi, (i - 1) * GC + (ch + 1))
                            sp.wait_ge(s_glo, (i - 1) * GC + (ch + 1))
                        for m, w in enumerate((wg_d, wu_d)):
                            src = w[bass.ds(e, 1), ch * P:(ch + 1) * P, :].rearrange("a p n -> p (a n)")
                            sp.dma_start(g_raw[:, ch, m, :], src).then_inc(g_in[ch], 16)

                def load_d(e, i=None):
                    for ch in range(DC):
                        if i is not None:
                            sp.wait_ge(s_dhi, (i - 1) * DC + (ch + 1))
                            sp.wait_ge(s_dlo, (i - 1) * DC + (ch + 1))
                        src = wd_d[bass.ds(e, 1), ch * P:(ch + 1) * P, :].rearrange("a p n -> p (a n)")
                        sp.dma_start(d_raw[:, ch, :], src).then_inc(d_in[ch], 16)

                def same_g(i):
                    for ch in range(GC):
                        sp.wait_ge(s_ghi, (i - 1) * GC + (ch + 1))
                        sp.sem_inc(g_in[ch], 32)

                def same_d(i):
                    for ch in range(DC):
                        sp.wait_ge(s_dhi, (i - 1) * DC + (ch + 1))
                        sp.sem_inc(d_in[ch], 16)

                e0 = sp.value_load(K["texp"][0:1, 0:1], min_val=0, max_val=NE - 1)
                load_g(e0)
                load_d(e0)
                end = last_used(sp)

                def load(i):
                    new = sp.value_load(K["tnew"][0:1, bass.ds(i, 1)], min_val=0, max_val=1)
                    with sp.If(new != 0):
                        e = sp.value_load(K["texp"][0:1, bass.ds(i, 1)], min_val=0, max_val=NE - 1)
                        load_g(e, i)
                        load_d(e, i)
                    with sp.Else():
                        same_g(i)
                        same_d(i)

                turns(sp, 1, end, load, ahead=1)
                for ch in range(GC):
                    wait_alone(sp, g_in[ch], end * 32 + 64, ended)
                for ch in range(DC):
                    wait_alone(sp, d_in[ch], end * 16 + 32, ended)

            @block.gpsimd
            def _(pool):
                def gather(i):
                    nc.gpsimd.tensor_copy(idx[:], K["stok"][:, bass.ds(i, 1)]).then_inc(idx_set, 1)
                    wait_alone(pool, idx_set, i + 1, passed)
                    pool.indirect_dma_start(xg[:], None, T["u"],
                                            bass.IndirectOffsetOnAxis(ap=idx[:, 0:1], axis=0)).then_inc(x_in, 16)

                end = last_used(pool)

                def gather_next(i):
                    wait_alone(pool, x_turned, i * 2, passed)
                    gather(i)

                gather(0)
                turns(pool, 1, end, gather_next, ahead=1)
                wait_alone(pool, x_in, end * 16 + 32, passed)

            @block.scalar
            def _(act):
                def split_g(i, ch, room=True):
                    act.wait_ge(g_in[ch], i * 32 + 32)
                    if room:
                        act.wait_ge(g_used, i * GC + (ch + 1 - GR))
                    nc.scalar.activation(g_hi[:, ch % GR], g_raw[:, ch], ACT.Copy).then_inc(s_ghi, 1)

                def split_d(i, ch, room=True):
                    act.wait_ge(d_in[ch], i * 16 + 16)
                    if room:
                        act.wait_ge(d_used, i * DC + (ch + 1 - DR))
                    nc.scalar.activation(d_hi[:, ch % DR], d_raw[:, ch], ACT.Copy).then_inc(s_dhi, 1)

                def x_part(i):
                    for h in range(2):
                        act.wait_ge(x_turned, i * 2 + (h + 1))
                        nc.scalar.activation(xT_hi[:, 4 * h:4 * h + 4, :],
                                             ps_x[:, h, :].rearrange("p (k n) -> p k n", k=4),
                                             ACT.Copy).then_inc(x_hi, 1)

                def silu(i):
                    act.wait_ge(g_used, i * GC + GC)
                    nc.scalar.activation(act_g[:], ps_g[:, 0, :], ACT.Silu).then_inc(silu_made, 1)

                def h_part(i):
                    act.wait_ge(h_turned, i + 1)
                    nc.scalar.activation(hT_hi[:], ps_h[:].rearrange("p (k n) -> p k n", k=KF),
                                         ACT.Copy).then_inc(h_hi, 1)

                def y_copy(i, first=False):
                    act.wait_ge(d_used, i * DC + DC)
                    if not first:
                        act.wait_ge(y_out, i * 16)
                    nc.scalar.activation(y[:], ps_y[:].rearrange("p a n -> p (a n)"), ACT.Copy).then_inc(y_made, 1)
                    act.wait_ge(y_made, i + 1)
                    act.dma_start(T["y"][bass.ds(i * P, P), :], y[:]).then_inc(y_out, 16)

                end = last_used(act)
                x_part(0)
                for ch in range(GC):
                    split_g(0, ch, False)
                silu(0)
                x_part(1)
                for ch in range(EARLY):
                    split_g(1, ch)
                h_part(0)

                def turn(i, first=False):
                    for ch in range(EARLY, GC):
                        split_g(i, ch)
                    for ch in range(DC):
                        split_d(i - 1, ch, not first)
                    silu(i)
                    x_part(i + 1)
                    for ch in range(EARLY):
                        split_g(i + 1, ch)
                    y_copy(i - 1, first)
                    h_part(i)

                turn(1, first=True)
                turns(act, 2, end, turn)
                for ch in range(DC):
                    split_d(end, ch, False)
                y_copy(end)
                wait_alone(act, y_out, end * 16 + 16, ended)

            @block.vector
            def _(dve):
                def split_g(i, ch):
                    dve.wait_ge(s_ghi, i * GC + (ch + 1))
                    nc.vector.tensor_tensor(g_lo[:, ch % GR], g_raw[:, ch], g_hi[:, ch % GR].bitcast(F32),
                                            ALU.subtract).then_inc(s_glo, 1)

                def split_d(i, ch):
                    dve.wait_ge(s_dhi, i * DC + (ch + 1))
                    nc.vector.tensor_tensor(d_lo[:, ch % DR], d_raw[:, ch], d_hi[:, ch % DR].bitcast(F32),
                                            ALU.subtract).then_inc(s_dlo, 1)

                def x_part(i):
                    for h in range(2):
                        dve.wait_ge(x_hi, i * 2 + (h + 1))
                        nc.vector.tensor_tensor(xT_lo[:, 4 * h:4 * h + 4, :],
                                                ps_x[:, h, :].rearrange("p (k n) -> p k n", k=4),
                                                xT_hi[:, 4 * h:4 * h + 4, :].bitcast(F32),
                                                ALU.subtract).then_inc(x_lo, 1)

                def hidden(i):
                    dve.wait_ge(silu_made, i + 1)
                    nc.vector.tensor_tensor(hid[:], act_g[:], ps_g[:, 1, :], ALU.mult).then_inc(h_made, 1)

                def h_part(i):
                    dve.wait_ge(h_hi, i + 1)
                    nc.vector.tensor_tensor(hT_lo[:], ps_h[:].rearrange("p (k n) -> p k n", k=KF),
                                            hT_hi[:].bitcast(F32), ALU.subtract).then_inc(h_lo, 1)

                end = last_used(dve)
                x_part(0)
                for ch in range(GC):
                    split_g(0, ch)
                hidden(0)
                x_part(1)
                for ch in range(EARLY):
                    split_g(1, ch)
                h_part(0)

                def turn(i):
                    for ch in range(EARLY, GC):
                        split_g(i, ch)
                    for ch in range(DC):
                        split_d(i - 1, ch)
                    hidden(i)
                    x_part(i + 1)
                    for ch in range(EARLY):
                        split_g(i + 1, ch)
                    h_part(i)

                turns(dve, 1, end, turn)
                for ch in range(DC):
                    split_d(end, ch)

            @block.tensor
            def _(pe):
                ident = c[:, K_ID:K_ID + P]

                def turn_x(i, first=False):
                    pe.wait_ge(x_in, i * 16 + 16)
                    for h in range(2):
                        if not first:
                            pe.wait_ge(x_lo, i * 2 + (h - 1))
                        for j in range(4):
                            k = 4 * h + j
                            last = nc.tensor.transpose(ps_x[:, h, j * P:(j + 1) * P], xg[:, k * P:(k + 1) * P], ident)
                        last.then_inc(x_turned, 1)

                def gate_up(i, first=False):
                    pe.wait_ge(x_lo, i * 2 + 2)
                    if not first:
                        pe.wait_ge(h_made, i)
                    for ch in range(GC):
                        pe.wait_ge(s_glo, i * GC + (ch + 1))
                        for m in range(2):
                            last = mm3(nc, ps_g[:, m, :], xT_hi[:, ch, :], xT_lo[:, ch, :],
                                       g_hi[:, ch % GR, m, :], g_lo[:, ch % GR, m, :], ch == 0, ch == GC - 1)
                        last.then_inc(g_used, 1)

                def turn_h(i):
                    pe.wait_ge(h_made, i + 1)
                    for j in range(KF):
                        last = nc.tensor.transpose(ps_h[:, j * P:(j + 1) * P], hid[:, j * P:(j + 1) * P], ident)
                    last.then_inc(h_turned, 1)

                def down(i, first=False):
                    pe.wait_ge(h_lo, i + 1)
                    if not first:
                        pe.wait_ge(y_made, i)
                    for ch in range(DC):
                        pe.wait_ge(s_dlo, i * DC + (ch + 1))
                        for m in range(2):
                            r = slice(m * 512, (m + 1) * 512)
                            last = mm3(nc, ps_y[:, m, :], hT_hi[:, ch, :], hT_lo[:, ch, :],
                                       d_hi[:, ch % DR, r], d_lo[:, ch % DR, r], ch == 0, ch == DC - 1)
                        last.then_inc(d_used, 1)

                end = last_used(pe)
                turn_x(0, True)
                gate_up(0, True)
                turn_x(1)
                turn_h(0)
                gate_up(1)
                turn_x(2)
                down(0, True)
                turn_h(1)

                def turn(i):
                    gate_up(i)
                    turn_x(i + 1)
                    down(i - 1)
                    turn_h(i)

                turns(pe, 2, end, turn)
                down(end)


def stage_finish(nc, a, K, T, out):
    with Scope(nc, "fin") as sc:
        WR, HB = 4, 4
        w_raw = sc.sb("w_raw", [P, WR, D])
        w_hi = sc.sb("w_hi", [P, KD + KP, D], F32R)
        w_lo = sc.sb("w_lo", [P, KD + KP, D], F32R)
        gain = sc.sb("gain", [P, D])
        gfin = sc.sb("gfin", [P, D])
        bgate = sc.sb("bgate", [1, D])
        junk = sc.sb("junk", [P, D], BF16)
        ss = sc.sb("ss", [P, NT, 2])
        rt = sc.sb("rt", [P, NT, 2])
        rs = sc.sb("rs", [P, NT, 2])
        ht = sc.sb("h", [P, HB, D])
        ys = sc.sb("y", [P, 2, 2, D])
        pt = sc.sb("p", [P, HB, PLE])
        vt = sc.sb("v", [P, D])
        vT_hi = sc.sb("vT_hi", [P, 2, KD + KP, P], F32R)
        vT_lo = sc.sb("vT_lo", [P, 2, KD + KP, P], F32R)
        gate = sc.sb("gate", [P, D])
        ot = sc.sb("o", [P, D])
        ps_x = sc.ps("ps_x", [P, 3, 512])
        ps_g = sc.ps("ps_g", [P, 2, 512])
        ps_p = sc.ps("ps_p", [P, 2, 512])
        w_in = [sc.sem(f"w_in{i}") for i in range(WR)]
        h_in = [sc.sem(f"h_in{i}") for i in range(HB)]
        y_in = T["y_in"]
        (mixed, vec_in, split_hi, split_lo, summed, sq, var, root, v_made, turned, v_hi, v_lo, gated, projected,
         sig, added, f_var, f_root, o_made, o_out, own_dve) = (
            sc.sem(n) for n in ("mixed", "vec_in", "split_hi", "split_lo", "summed", "sq", "var", "root",
                                "v_made", "turned", "v_hi", "v_lo", "gated", "projected", "sig", "added", "f_var",
                                "f_root", "o_made", "o_out", "own_dve"))
        f_sq = sc.sem("f_sq")
        wg_d = a["w_ple_gate"].rearrange("l (k p) n -> (l k) p n", p=P)
        wp_d = a["w_ple_proj"].rearrange("l (k p) n -> (l k) p n", p=P)
        p_d = a["p"].rearrange("l b (t p) d -> (l b t) p d", p=P)
        out_d = out.rearrange("b (t p) d -> (b t) p d", p=P)
        with sc.block() as block:
            @block.sync
            def _(sp):
                sp.dma_start(gain[:], a["g_ple"].to_broadcast((P, D))).then_inc(vec_in, 16)
                sp.dma_start(gfin[:], a["g_final"].rearrange("(a n) -> a n", a=1).to_broadcast((P, D))).then_inc(vec_in, 16)
                sp.dma_start(bgate[:], a["b_ple_gate"]).then_inc(vec_in, 16)
                def rows(t):
                    sp.dma_start(ht[:, t % HB, :], T["h"][t]).then_inc(h_in[t % HB], 16)
                    sp.dma_start(pt[:, t % HB, :], p_d[t]).then_inc(h_in[t % HB], 16)

                rows(0)
                for k in range(KD + KP):
                    if k >= WR:
                        sp.wait_ge(split_lo, k - WR + 1)
                    sp.dma_start(w_raw[:, k % WR, :], wg_d[k] if k < KD else wp_d[k - KD]).then_inc(w_in[k % WR], 16)
                    if k < HB - 1:
                        rows(k + 1)
                for t in range(NT):
                    sp.wait_ge(o_made, t + 1)
                    sp.dma_start(out_d[t], ot[:]).then_inc(o_out, 16)
                    if t + HB < NT:
                        rows(t + HB)
                sp.wait_ge(o_out, 16 * NT)

            @block.gpsimd
            def _(pool):
                for t in range(NT):
                    if t >= 2:
                        pool.wait_ge(summed, 2 * t - 2)
                    for k in range(2):
                        pool.indirect_dma_start(ys[:, t % 2, k, :], None, T["y"],
                                                bass.IndirectOffsetOnAxis(ap=K["slot"][:, k, t:t + 1], axis=0)
                                                ).then_inc(y_in[t % 2], 16)

            def tiles(head, turn, weigh, tail, split):
                head(0)
                turn(0)
                head(1)
                split()
                for i in range(NT + 1):
                    if i:
                        weigh(i - 1)
                    if i + 1 < NT:
                        turn(i + 1)
                    if i + 2 < NT:
                        head(i + 2)
                    if i:
                        tail(i - 1)

            @block.scalar
            def _(act):
                def split():
                    for k in range(KD + KP):
                        act.wait_ge(w_in[k % WR], 16 * (k // WR + 1))
                        nc.scalar.activation(w_hi[:, k, :], w_raw[:, k % WR, :], ACT.Copy).then_inc(split_hi, 1)

                def head(t):
                    act.wait_ge(summed, 2 * t + 2)
                    nc.scalar.activation(junk[:], ht[:, t % HB, :], ACT.Square,
                                         accum_out=ss[:, t, 0:1]).then_inc(sq, 1)
                    act.wait_ge(var, t + 1)
                    nc.scalar.activation(rt[:, t, 0:1], rt[:, t, 0:1], ACT.Sqrt).then_inc(root, 1)

                def turn(t):
                    for h in range(3):
                        act.wait_ge(turned, 3 * t + h + 1)
                        if t >= 2:
                            act.wait_ge(projected, t - 1)
                        n = 4 if h < 2 else KP
                        nc.scalar.activation(vT_hi[:, t % 2, 4 * h:4 * h + n, :],
                                             ps_x[:, h, 0:n * P].rearrange("p (k n) -> p k n", k=n),
                                             ACT.Copy).then_inc(v_hi, 1)

                def weigh(t):
                    act.wait_ge(gated, t + 1)
                    if t:
                        act.wait_ge(added, t)
                    nc.scalar.activation(gate[:], ps_g[:].rearrange("p a n -> p (a n)"), ACT.Sigmoid).then_inc(sig, 1)

                def tail(t):
                    act.wait_ge(added, t + 1)
                    nc.scalar.activation(junk[:], ht[:, t % HB, :], ACT.Square,
                                         accum_out=ss[:, t, 1:2]).then_inc(f_sq, 1)
                    act.wait_ge(f_var, t + 1)
                    nc.scalar.activation(rt[:, t, 1:2], rt[:, t, 1:2], ACT.Sqrt).then_inc(f_root, 1)

                tiles(head, turn, weigh, tail, split)

            @block.vector
            def _(dve):
                own = Tally(own_dve)

                def split():
                    for k in range(KD + KP):
                        dve.wait_ge(split_hi, k + 1)
                        nc.vector.tensor_tensor(w_lo[:, k, :], w_raw[:, k % WR, :], w_hi[:, k, :].bitcast(F32),
                                                ALU.subtract).then_inc(split_lo, 1)

                dve.wait_ge(vec_in, 48)

                def head(t):
                    h = ht[:, t % HB, :]
                    dve.wait_ge(h_in[t % HB], 32 * (t // HB + 1))
                    dve.wait_ge(y_in[t % 2], 32 * (t // 2 + 1))
                    for k in range(2):
                        nc.vector.scalar_tensor_tensor(h, ys[:, t % 2, k, :], K["cw"][:, k, t:t + 1], h, ALU.mult,
                                                       ALU.add).then_inc(summed, 1)
                        dve.wait_ge(summed, 2 * t + k + 1)
                    dve.wait_ge(sq, t + 1)
                    nc.vector.tensor_scalar(rt[:, t, 0:1], ss[:, t, 0:1], 1.0 / D, EPS, ALU.mult,
                                            ALU.add).then_inc(var, 1)
                    dve.wait_ge(root, t + 1)
                    own.inc(nc.vector.reciprocal(rs[:, t, 0:1], rt[:, t, 0:1]))
                    own.wait(dve)
                    if t:
                        dve.wait_ge(turned, 3 * t)
                    nc.vector.scalar_tensor_tensor(vt[:], h, rs[:, t, 0:1], gain[:], ALU.mult,
                                                   ALU.mult).then_inc(v_made, 1)

                def turn(t):
                    for h in range(3):
                        dve.wait_ge(v_hi, 3 * t + h + 1)
                        n = 4 if h < 2 else KP
                        nc.vector.tensor_tensor(vT_lo[:, t % 2, 4 * h:4 * h + n, :],
                                                ps_x[:, h, 0:n * P].rearrange("p (k n) -> p k n", k=n),
                                                vT_hi[:, t % 2, 4 * h:4 * h + n, :].bitcast(F32),
                                                ALU.subtract).then_inc(v_lo, 1)

                def weigh(t):
                    dve.wait_ge(sig, t + 1)
                    dve.wait_ge(projected, t + 1)
                    nc.vector.tensor_tensor(gate[:], gate[:], ps_p[:].rearrange("p a n -> p (a n)"),
                                            ALU.mult).then_inc(mixed, 1)

                def tail(t):
                    h = ht[:, t % HB, :]
                    dve.wait_ge(mixed, t + 1)
                    nc.vector.tensor_tensor(h, h, gate[:], ALU.add).then_inc(added, 1)
                    dve.wait_ge(f_sq, t + 1)
                    nc.vector.tensor_scalar(rt[:, t, 1:2], ss[:, t, 1:2], 1.0 / D, EPS, ALU.mult,
                                            ALU.add).then_inc(f_var, 1)
                    dve.wait_ge(f_root, t + 1)
                    own.inc(nc.vector.reciprocal(rs[:, t, 1:2], rt[:, t, 1:2]))
                    own.wait(dve)
                    if t:
                        dve.wait_ge(o_out, 16 * t)
                    nc.vector.scalar_tensor_tensor(ot[:], h, rs[:, t, 1:2], gfin[:], ALU.mult,
                                                   ALU.mult).then_inc(o_made, 1)

                tiles(head, turn, weigh, tail, split)

            @block.tensor
            def _(pe):
                ident = K["c"][:, K_ID:K_ID + P]

                def turn(t):
                    pe.wait_ge(v_made, t + 1)
                    pe.wait_ge(h_in[t % HB], 32 * (t // HB + 1))
                    for h in range(3):
                        if t:
                            pe.wait_ge(v_lo, 3 * t + h - 2)
                        for j in range(4 if h < 2 else KP):
                            src = vt[:, (4 * h + j) * P:(4 * h + j + 1) * P] if h < 2 else pt[:, t % HB, j * P:(j + 1) * P]
                            last = nc.tensor.transpose(ps_x[:, h, j * P:(j + 1) * P], src, ident)
                        last.then_inc(turned, 1)

                turn(0)
                for t in range(NT):
                    if t + 1 < NT:
                        turn(t + 1)
                    pe.wait_ge(v_lo, 3 * t + 3)
                    if t:
                        pe.wait_ge(sig, t)
                    for out_, ks, sem in ((ps_g, range(KD), gated), (ps_p, range(KD, KD + KP), projected)):
                        if t and ks[0]:
                            pe.wait_ge(mixed, t)
                        for h in range(2):
                            r = slice(h * 512, (h + 1) * 512)
                            for k in ks:
                                if t == 0 and h == 0:
                                    pe.wait_ge(split_lo, k + 1)
                                last = mm3(nc, out_[:, h, :], vT_hi[:, t % 2, k, :], vT_lo[:, t % 2, k, :], w_hi[:, k, r],
                                           w_lo[:, k, r], k == ks[0], k == ks[-1] and ks[0] > 0)
                            if ks[0] == 0:
                                last = nc.tensor.matmul(out_[:, h, :], K["c"][0:1, K_ONE:K_ONE + P], bgate[:, r],
                                                        start=False, stop=True)
                        last.then_inc(sem, 1)


def build(nc, a, out):
    T = {
        "feat": nc.dram_tensor("feat", [16, P, S], F32).ap(),
        "cum": nc.dram_tensor("cum", [NH, 2, S], F32).ap(),
        "h": nc.dram_tensor("h_rows", [NT, P, D], F32).ap(),
        "u": nc.dram_tensor("u_rows", [S, D], F32).ap(),
        "slots": nc.dram_tensor("slots", [SLOTS, 1], U32).ap(),
        "y": nc.dram_tensor("y_rows", [TILES * P, D], F32).ap(),
    }
    K = {}
    with Scope(nc, "all") as outer:
        T["stored"] = [outer.sem(f"stored{i}") for i in range(2)]
        T["y_in"] = [outer.sem(f"y_in{i}") for i in range(2)]
        for name in ("zero_out", "scattered", "back", "xg_in"):
            T[name] = outer.sem(name)
        for name, shape, dt in (("c", [P, K_COLS], F32), ("lg", [P, NT, NG + NE], F32), ("cw", [P, 2, NT], F32),
                                ("slot", [P, 2, NT], U32), ("texp", [P, 32], I32),
                                ("tnew", [P, 32], I32), ("last", [P, 1], I32), ("stok", [P, SLOTS // P], U32)):
            K[name] = outer.sb(name, shape, dt)
        with Scope(nc, "att") as inner:
            for name, shape, dt in (("o", [P, NT, D], F32),):
                K[name] = inner.sb(name, shape, dt)
            with Scope(nc, "tok") as tok:
                for name, shape, dt in (
                        ("maskb", [P, (2 + NT) * P], BF16), ("identb", [P, P], BF16), ("cos", [P, S], F32),
                        ("sin", [P, S], F32), ("vb", [P, NT, NH * HD], F32), ("vsw", [P, NT, 288], F32),
                        ("gate", [P, NT, 3 * NH], F32), ("vc", [P, GROUPS, HD], F32),
                        ("kc_raw", [P, GROUPS, P], F32), ("kc_hi", [P, GROUPS, P], F32R),
                        ("kc_lo", [P, GROUPS, P], F32R)):
                    K[name] = tok.sb(name, shape, dt)
                K["tokT"] = K["o"][:, 0:2, :]
                stage_load(nc, a, K)
                stage_project(nc, a, K, T)
                stage_compress(nc, a, K, T)
                stage_attention(nc, K, T, sparse=True)
                stage_attention(nc, K, T, sparse=False)
            stage_mix(nc, a, K, T)
        stage_route(nc, K, T)
        stage_moe(nc, a, K, T)
        stage_finish(nc, a, K, T, out)


_INS = ["x", "p", "positions", "g_mix", "w_in", "b_nsa_gate", "b_forget", "pe_cmp_k", "w_cmp_k1", "w_cmp_k2",
        "pe_cmp_v", "w_cmp_v1", "w_cmp_v2", "beta_nsa", "beta_fox", "w_out", "g_ffn", "w_group", "b_group",
        "w_router", "b_router", "w_gate_e", "w_up_e", "w_down_e", "g_ple", "w_ple_gate", "b_ple_gate",
        "w_ple_proj", "g_final"]


def kernel(**inputs):
    import concourse.bacc as bacc
    from concourse.bass_utils import run_bass_kernel_spmd as run

    nc = bacc.Bacc("TRN2", target_bir_lowering=False, num_devices=1)
    arrays, a = {}, {}
    for name in _INS:
        v = np.ascontiguousarray(inputs[name])
        arrays[f"in_{name}"] = v
        a[name] = nc.dram_tensor(f"in_{name}", v.shape, mybir.dt.from_np(v.dtype), kind="ExternalInput").ap()
    c = constants()
    arrays["in_consts"] = c
    a["consts"] = nc.dram_tensor("in_consts", c.shape, F32, kind="ExternalInput").ap()
    out = nc.dram_tensor("out", (1, S, D), F32, kind="ExternalOutput").ap()
    build(nc, a, out)
    r = run(nc, [arrays], core_ids=[0])
    return r.results[0]["out"]
```

```python
from contextlib import ExitStack

import numpy as np

import concourse.bass as bass
from concourse import mybir

F32 = mybir.dt.float32
F32R = mybir.dt.float32r
BF16 = mybir.dt.bfloat16
I32 = mybir.dt.int32
U32 = mybir.dt.uint32
ALU = mybir.AluOpType
ACT = mybir.ActivationFunctionType
X = mybir.AxisListType.X

P = 128
D = 1024
S = 1024
KD = D // P
NT = S // P
HD = 64
NH = 8
GROUPS = 2
SCALE = HD ** -0.5
CMP_BLOCK, CMP_STRIDE = 32, 16
N_CMP = (S - CMP_BLOCK) // CMP_STRIDE + 1
WINDOW = 512
WB = WINDOW // P
NG, EPG = 4, 4
NE = NG * EPG
FE = D // 2
KF = FE // P
PLE = 256
KP = PLE // P
EPS = 1e-6
NEG = -1e30
TILES = (2 * S) // P + NE - 1
FEWEST = (2 * S) // P
SLOTS = (TILES + 1) * P
ROPE_HALF = HD // 8

C_Q, C_KC, C_VC, C_KS, C_VS, C_KW, C_VW, C_GATE = 0, 512, 640, 768, 896, 1024, 1152, 1280
C_QB, C_KB, C_VB, C_F = 1304, 1816, 2328, 2840

K_ID, K_ROT, K_LT, K_ONE, K_DIAG, K_FAR, K_CMP = 0, 128, 256, 384, 512, 640, 768
K_FREQ = K_CMP + NT * P
K_ISROPE, K_NOROPE, K_VALID, K_PRI, K_TILE, K_COLS = (
    K_FREQ + 1, K_FREQ + 2, K_FREQ + 3, K_FREQ + 4, K_FREQ + 8, K_FREQ + 8 + 32)
K_TOK = K_COLS
K_IOTA = K_TOK + NT
K_COLS = K_IOTA + P


def constants():
    c = np.zeros((P, K_COLS), np.float32)
    a = np.arange(P)
    c[:, K_ID:K_ID + P] = np.eye(P)
    rot = np.zeros((P, P), np.float32)
    for h in (0, HD):
        for d in range(ROPE_HALF):
            rot[h + d + ROPE_HALF, h + d] = -1.0
            rot[h + d, h + d + ROPE_HALF] = 1.0
    c[:, K_ROT:K_ROT + P] = rot
    c[:, K_LT:K_LT + P] = (a[:, None] < a[None, :])
    c[:, K_ONE:K_ONE + P] = 1.0
    c[:, K_DIAG:K_DIAG + P] = np.where(a[None, :] <= a[:, None], 0.0, -NEG)
    c[:, K_FAR:K_FAR + P] = np.where(a[None, :] > a[:, None], 0.0, -NEG)
    for qt in range(NT):
        t = qt * P + a
        end = a * CMP_STRIDE + CMP_BLOCK - 1
        c[:, K_CMP + qt * P:K_CMP + (qt + 1) * P] = np.where(
            (end[None, :] <= t[:, None]) & (a[None, :] < N_CMP), 0.0, -NEG)
    inv = np.power(np.float32(500000.0), -np.arange(ROPE_HALF, dtype=np.float32) / np.float32(ROPE_HALF))
    rope = (a % HD) < 2 * ROPE_HALF
    c[:, K_FREQ] = np.where(rope, inv[a % ROPE_HALF], 0.0)
    c[:, K_ISROPE] = rope
    c[:, K_NOROPE] = ~rope
    c[:, K_VALID] = (a >= CMP_BLOCK - 1)
    c[:, K_PRI:K_PRI + 4] = np.arange(4, 0, -1)[None, :]
    c[:, K_TILE:K_TILE + 32] = np.arange(32)[None, :]
    c[:, K_TOK:K_TOK + NT] = a[:, None] + P * np.arange(NT)[None, :]
    c[:, K_IOTA:K_IOTA + P] = a[None, :]
    return c


class Tally:

    def __init__(self, sem, base=0):
        self.sem, self.base, self.n = sem, base, 0

    def inc(self, ins):
        ins.then_inc(self.sem, 1)
        self.n += 1

    def wait(self, eng):
        eng.wait_ge(self.sem, self.base + self.n)


def mm3(nc, out, a_hi, a_lo, b_hi, b_lo, first, last):
    nc.tensor.matmul(out, a_hi, b_hi, start=first, stop=False)
    nc.tensor.matmul(out, a_hi, b_lo, start=False, stop=False)
    return nc.tensor.matmul(out, a_lo, b_hi, start=False, stop=last)


def wait_alone(eng, sem, value, passed):
    eng.wait_ge(sem, value)
    eng.sem_inc(passed, 1)


class Scope:

    def __init__(self, nc, name):
        self.nc, self.name, self.ctx, self.sems = nc, name, ExitStack(), []

    def __enter__(self):
        self.ctx.__enter__()
        return self

    def __exit__(self, *a):
        if self.sems:
            self.nc.all_engine_barrier()
            self.nc.clear_and_free_semaphores(self.sems)
            self.nc.all_engine_barrier()
        return self.ctx.__exit__(*a)

    def sb(self, name, shape, dt=F32):
        return self.ctx.enter_context(self.nc.sbuf_tensor(f"{self.name}_{name}", shape, dt))

    def ps(self, name, shape, dt=F32):
        return self.ctx.enter_context(self.nc.psum_tensor(f"{self.name}_{name}", shape, dt))

    def sem(self, name):
        self.sems.append(self.nc.alloc_semaphore(f"{self.name}_{name}"))
        return self.sems[-1]

    def block(self):
        return self.nc.Block()


def stage_project(nc, a, K, T):
    PI = float(np.pi)
    TWO_PI_HI = 6.28125
    TWO_PI_LO = float(2 * np.pi - TWO_PI_HI)
    with Scope(nc, "prj") as sc:
        XR = 3
        ss = sc.sb("ss", [P, NT])
        rstd = sc.sb("rstd", [P, 2 * NT])
        hT_hi = sc.sb("hT_hi", [P, KD, S], F32R)
        hT_lo = sc.sb("hT_lo", [P, KD, S], F32R)
        w_raw = sc.sb("w_raw", [P, 2, KD, P])
        w_hi = sc.sb("w_hi", [P, 2, KD, P], F32R)
        w_lo = sc.sb("w_lo", [P, 2, KD, P], F32R)
        feat = sc.sb("feat", [P, 2, S])
        turn = sc.sb("turn", [P, S // 2])
        cos_t = K["cos"]
        sin_t = K["sin"]
        VW = 256 + 24 + 8
        v_raw = K["o"][:, 2:5, :].rearrange("p a n -> p (a n)")[:, 0:KD * VW].rearrange("p (k n) -> p k n", k=KD)
        with Scope(nc, "prj_x") as early:
            xt = early.sb("x", [P, XR, D])
            xn = early.sb("xn", [P, 2, D])
            gain = early.sb("gain", [P, D])
            sq = early.sb("sq", [P, D], BF16)
        ang, whole, over, ang_c = (K["vb"][:, 2 * n:2 * n + 2, :].rearrange("p a n -> p (a n)") for n in range(4))
        pos, turns = (K["vsw"][:].rearrange("p a n -> p (a n)")[:, n * S:(n + 1) * S].bitcast(I32) for n in range(2))
        v_hi = sc.sb("v_hi", [P, KD, VW], F32R)
        v_lo = sc.sb("v_lo", [P, KD, VW], F32R)
        ps_x = sc.ps("ps_x", [P, 2, 512])
        ps_w = sc.ps("ps_w", [P, 2, 512])
        ps_r = sc.ps("ps_r", [P, 512])

        x_in = [sc.sem(f"x_in{i}") for i in range(XR)]
        gain_in, normed, scaled, turned, up_hi, up_lo, own_act, own_dve = (
            sc.sem(n) for n in ("gain_in", "normed", "scaled", "turned", "up_hi", "up_lo", "own_act", "own_dve"))
        squared = sc.sem("squared")
        const_in, pos_in, made, reduced, looked = (
            sc.sem(n) for n in ("const_in", "pos_in", "made", "reduced", "looked"))
        rooted = sc.sem("rooted")
        var = sc.sem("var")
        w_in_ = [sc.sem(f"w_in{i}") for i in range(2)]
        split_hi, split_lo, product, evac, rotated, turn_made = (
            sc.sem(n) for n in ("split_hi", "split_lo", "product", "evac", "rotated", "turn_made"))
        roped = sc.sem("roped")
        stored = T["stored"]
        v_in = sc.sem("v_in")
        vs_hi, vs_lo, v_product, v_evac = (sc.sem(n) for n in ("vs_hi", "vs_lo", "v_product", "v_evac"))

        x_d = a["x"].rearrange("b (t p) d -> (b t) p d", p=P)
        w_d = a["w_in"].rearrange("l (k p) n -> (l p) k n", p=P)
        FIXED = [(C_KC, None, False), (C_VC, None, False)] + [(C_Q + P * j, j, True) for j in range(4)] + [
            (C_KS, 6, True), (C_KW, 7, True)]
        NFIX = len(FIXED)

        def stores_before(n):
            return sum(1 for m in range(n % 2, n, 2) if FIXED[m][1] is not None)

        VP = 4
        VK = KD // VP
        VCH = [[(C_VB, 256)], [(C_VB + 256, 256)], [(C_VS, 128), (C_VW, 128), (C_GATE, 24), (C_F, 8)]]

        with sc.block() as block:
            @block.sync
            def _(sp):
                sp.dma_start(xt[:, 0, :], x_d[0]).then_inc(x_in[0], 16)
                sp.dma_start(gain[:], a["g_mix"].to_broadcast((P, D))).then_inc(gain_in, 16)
                sp.dma_start(K["c"][:], a["consts"]).then_inc(const_in, 16)
                for t in range(1, NT):
                    if t >= XR:
                        sp.wait_ge(scaled, t - XR + 1)
                    sp.dma_start(xt[:, t % XR, :], x_d[t]).then_inc(x_in[t % XR], 16)
                    if t < 3:
                        c = FIXED[t - 1][0]
                        sp.dma_start(w_raw[:, t - 1, :, :], w_d[:, :, c:c + P]).then_inc(w_in_[t - 1], 16)
                    if t == 3:
                        sp.dma_start(pos, a["positions"].to_broadcast((P, S))).then_inc(pos_in, 16)
                for n in range(2, NFIX):
                    sp.wait_ge(split_hi, n - 1)
                    sp.wait_ge(split_lo, n - 1)
                    c = FIXED[n][0]
                    sp.dma_start(w_raw[:, n % 2, :, :], w_d[:, :, c:c + P]).then_inc(w_in_[n % 2], 16)
                with sp.Fori(0, NFIX // 2) as i:
                    for s in range(2):
                        sp.wait_ge(split_hi, i * 2 + (NFIX + s - 1))
                        sp.wait_ge(split_lo, i * 2 + (NFIX + s - 1))
                        sp.dma_start(w_raw[:, s, :, :],
                                     w_d[:, :, bass.ds(i * (2 * P) + (C_QB + s * P), P)]).then_inc(w_in_[s], 16)
                for n, cols in enumerate(VCH):
                    if n:
                        sp.wait_ge(vs_hi, VP * n)
                        sp.wait_ge(vs_lo, VP * n)
                    o = 0
                    for c, w in cols:
                        sp.dma_start(v_raw[:, :, o:o + w], w_d[:, :, c:c + w]).then_inc(v_in, 16)
                        o += w

            @block.gpsimd
            def _(pool):
                halves = 0
                for n, (_, row, rope) in enumerate(FIXED):
                    if row is None:
                        continue
                    if rope:
                        halves += 2
                        pool.wait_ge(roped, halves)
                    pool.dma_start(T["feat"][row], feat[:, n % 2, :]).then_inc(stored[n % 2], 16)
                with pool.Fori(0, NFIX // 2) as i:
                    for s in range(2):
                        pool.wait_ge(evac, i * 4 + (2 * NFIX + 2 * s + 2))
                        pool.dma_start(T["feat"][bass.ds(i * 2 + (NFIX + s), 1)].rearrange("a p n -> p (a n)"),
                                       feat[:, s, :]).then_inc(stored[s], 16)
                for s in range(2):
                    pool.wait_ge(stored[s], 16 * (stores_before(NFIX + s) + NFIX // 2))

            @block.scalar
            def _(act):
                def norm(t):
                    act.wait_ge(x_in[t % XR], 16 * (t // XR + 1))
                    if t:
                        act.wait_ge(squared, t)
                    nc.scalar.activation(sq[:], xt[:, t % XR, :], ACT.Square,
                                         accum_out=ss[:, t:t + 1]).then_inc(squared, 1)
                    act.wait_ge(var, t + 1)
                    nc.scalar.activation(rstd[:, NT + t:NT + t + 1], rstd[:, t:t + 1], ACT.Sqrt).then_inc(rooted, 1)

                norm(0)
                for t in range(NT):
                    if t + 1 < NT:
                        norm(t + 1)
                    for h in range(2):
                        act.wait_ge(turned, 2 * t + h + 1)
                        nc.scalar.activation(hT_hi[:, 4 * h:4 * h + 4, t * P:(t + 1) * P],
                                             ps_x[:, h, :].rearrange("p (k n) -> p k n", k=4),
                                             ACT.Copy).then_inc(up_hi, 1)

                def split(n, s):
                    act.wait_ge(w_in_[s], n[0])
                    act.wait_ge(product, n[1])
                    nc.scalar.activation(w_hi[:, s], w_raw[:, s], ACT.Copy).then_inc(split_hi, 1)

                def copy_out(s, h, product_at, stored_at, kept=None, scale=1.0):
                    act.wait_ge(product, product_at)
                    if stored_at is not None:
                        act.wait_ge(stored[s], stored_at)
                    out = feat[:, s, :] if kept is None else K["tokT"][:, kept, :]
                    nc.scalar.activation(out[:, h * 512:(h + 1) * 512], ps_w[:, h, :], ACT.Copy,
                                         scale=scale).then_inc(evac, 1)

                for s in range(2):
                    act.wait_ge(w_in_[s], 16)
                    nc.scalar.activation(w_hi[:, s], w_raw[:, s], ACT.Copy).then_inc(split_hi, 1)
                for n in range(NFIX):
                    row = FIXED[n][1]
                    kept = n if row is None else None
                    for h in range(2):
                        copy_out(n % 2, h, 2 * n + h + 1, 16 * stores_before(n) or None, kept,
                                 -SCALE if row is not None and row < 4 else 1.0)
                    split((16 * (n // 2 + 2), 2 * n + 2), n % 2)
                    if n == 0:
                        act.wait_ge(reduced, 1)
                        nc.scalar.activation(K["sin"][:], ang, ACT.Sin).then_inc(looked, 1)
                        nc.scalar.activation(K["cos"][:], ang_c, ACT.Sin).then_inc(looked, 1)
                SB = [stores_before(NFIX + s) for s in range(2)]
                for first, end, scale in ((0, NFIX // 4, -SCALE), (NFIX // 4, NFIX // 2 - 1, 1.0)):
                    with act.Fori(first, end) as i:
                        for s in range(2):
                            for h in range(2):
                                copy_out(s, h, i * 4 + (2 * NFIX + 2 * s + h + 1), i * 16 + 16 * SB[s], scale=scale)
                            split((i * 16 + 16 * (NFIX // 2 + 2), i * 4 + (2 * NFIX + 2 * s + 2)), s)
                for s in range(2):
                    for h in range(2):
                        copy_out(s, h, 4 * NFIX - 4 + 2 * s + h + 1, 16 * (SB[s] + NFIX // 2 - 1))

                for n in range(3):
                    act.wait_ge(v_in, 16 * (6 if n == 2 else n + 1))
                    if n:
                        act.wait_ge(v_product, NT * n)
                    w = sum(x[1] for x in VCH[n])
                    for k in range(0, KD, VK):
                        nc.scalar.activation(v_hi[:, k:k + VK, 0:w], v_raw[:, k:k + VK, 0:w],
                                             ACT.Copy).then_inc(vs_hi, 1)

            @block.vector
            def _(dve):
                own = Tally(own_dve)
                dve.wait_ge(gain_in, 16)

                def norm(t):
                    dve.wait_ge(squared, t + 1)
                    nc.vector.tensor_scalar(rstd[:, t:t + 1], ss[:, t:t + 1], 1.0 / D, EPS, ALU.mult,
                                            ALU.add).then_inc(var, 1)
                    dve.wait_ge(rooted, t + 1)
                    own.inc(nc.vector.reciprocal(rstd[:, t:t + 1], rstd[:, NT + t:NT + t + 1]))
                    own.wait(dve)
                    if t >= 2:
                        dve.wait_ge(turned, 2 * (t - 1))
                    nc.vector.scalar_tensor_tensor(xn[:, t % 2, :], xt[:, t % XR, :], rstd[:, t:t + 1], gain[:],
                                                   ALU.mult, ALU.mult).then_inc(scaled, 1)

                norm(0)
                for t in range(NT):
                    if t + 1 < NT:
                        norm(t + 1)
                    for h in range(2):
                        dve.wait_ge(up_hi, 2 * t + h + 1)
                        nc.vector.tensor_tensor(hT_lo[:, 4 * h:4 * h + 4, t * P:(t + 1) * P],
                                                ps_x[:, h, :].rearrange("p (k n) -> p k n", k=4),
                                                hT_hi[:, 4 * h:4 * h + 4, t * P:(t + 1) * P].bitcast(F32),
                                                ALU.subtract).then_inc(up_lo, 1)

                def split(s, at):
                    dve.wait_ge(split_hi, at)
                    nc.vector.tensor_tensor(w_lo[:, s], w_raw[:, s], w_hi[:, s].bitcast(F32),
                                            ALU.subtract).then_inc(split_lo, 1)

                for s in range(2):
                    split(s, s + 1)

                c = K["c"]
                steps = Tally(made)

                def step(ins):
                    steps.inc(ins)
                    steps.wait(dve)

                def wrap(x):
                    step(nc.vector.tensor_scalar(over, x, PI, -2 * PI, ALU.is_gt, ALU.mult))
                    step(nc.vector.tensor_tensor(x, x, over, ALU.add))
                    step(nc.vector.tensor_scalar(over, x, -PI, 2 * PI, ALU.is_lt, ALU.mult))
                    step(nc.vector.tensor_tensor(x, x, over, ALU.add))
                    step(nc.vector.tensor_scalar(x, x, 3.1415925, -3.1415925, ALU.min, ALU.max))

                dve.wait_ge(pos_in, 16)
                dve.wait_ge(const_in, 16)
                step(nc.vector.tensor_copy(ang, pos))
                step(nc.vector.tensor_scalar(ang, ang, c[:, K_FREQ:K_FREQ + 1], None, ALU.mult))
                step(nc.vector.tensor_scalar(whole, ang, 1.0 / (2 * PI), None, ALU.mult))
                step(nc.vector.tensor_copy(turns, whole))
                step(nc.vector.tensor_copy(whole, turns))
                step(nc.vector.scalar_tensor_tensor(ang, whole, -TWO_PI_HI, ang, ALU.mult, ALU.add))
                step(nc.vector.scalar_tensor_tensor(ang, whole, -TWO_PI_LO, ang, ALU.mult, ALU.add))
                wrap(ang)
                step(nc.vector.tensor_scalar(ang_c, ang, PI / 2, None, ALU.add))
                wrap(ang_c)
                nc.vector.tensor_copy(over[:, 0:1], ang_c[:, 0:1]).then_inc(reduced, 1)
                steps.inc(nc.vector.tensor_copy(K["maskb"][:], c[:, K_DIAG:K_DIAG + (2 + NT) * P]))
                steps.inc(nc.vector.tensor_copy(K["identb"][:], c[:, K_ID:K_ID + P]))
                split(0, 3)
                dve.wait_ge(looked, 2)
                step(nc.vector.tensor_scalar(K["sin"][:], K["sin"][:], c[:, K_ISROPE:K_ISROPE + 1], None, ALU.mult))
                step(nc.vector.tensor_scalar(K["cos"][:], K["cos"][:], c[:, K_ISROPE:K_ISROPE + 1],
                                             c[:, K_NOROPE:K_NOROPE + 1], ALU.mult, ALU.add))
                halves = 0
                for n, (_, _, rope) in enumerate(FIXED):
                    if rope:
                        for h in range(2):
                            halves += 1
                            dve.wait_ge(rotated, halves)
                            f = feat[:, n % 2, h * 512:(h + 1) * 512]
                            nc.vector.tensor_tensor(turn[:], ps_r[:], sin_t[:, h * 512:(h + 1) * 512],
                                                    ALU.mult).then_inc(turn_made, 1)
                            own.inc(nc.vector.tensor_tensor(f, f, cos_t[:, h * 512:(h + 1) * 512], ALU.mult))
                            own.wait(dve)
                            dve.wait_ge(turn_made, halves)
                            nc.vector.tensor_tensor(f, f, turn[:], ALU.add).then_inc(roped, 1)
                            dve.wait_ge(roped, halves)
                    if n:
                        split(n % 2, n + 3)
                with dve.Fori(0, NFIX // 2 - 1) as i:
                    for s in range(2):
                        split(s, i * 2 + (NFIX + s + 3))

                def v_split(n):
                    w = sum(x[1] for x in VCH[n])
                    for k in range(0, KD, VK):
                        dve.wait_ge(vs_hi, VP * n + k // VK + 1)
                        nc.vector.tensor_tensor(v_lo[:, k:k + VK, 0:w], v_raw[:, k:k + VK, 0:w],
                                                v_hi[:, k:k + VK, 0:w].bitcast(F32), ALU.subtract).then_inc(vs_lo, 1)

                v_split(0)
                for n in range(3):
                    w = sum(x[1] for x in VCH[n])
                    for t in range(NT):
                        dve.wait_ge(v_product, n * NT + t + 1)
                        out = K["vb"][:, t, n * 256:(n + 1) * 256] if n < 2 else K["vsw"][:, t, 0:w]
                        nc.vector.tensor_copy(out, ps_w[:, t % 2, 0:w]).then_inc(v_evac, 1)
                    if n < 2:
                        v_split(n + 1)

            @block.tensor
            def _(pe):
                ident = K["c"][:, K_ID:K_ID + P]
                pe.wait_ge(const_in, 16)
                for t in range(NT):
                    pe.wait_ge(scaled, t + 1)
                    for h in range(2):
                        if t:
                            pe.wait_ge(up_lo, 2 * t + h - 1)
                        for j in range(4):
                            k = 4 * h + j
                            last = nc.tensor.transpose(ps_x[:, h, j * P:(j + 1) * P],
                                                       xn[:, t % 2, k * P:(k + 1) * P], ident)
                        last.then_inc(turned, 1)
                pe.wait_ge(up_lo, 2 * NT)

                def block_of(s, split_at, evac_at):
                    pe.wait_ge(split_hi, split_at)
                    pe.wait_ge(split_lo, split_at)
                    for h in range(2):
                        if evac_at is not None:
                            pe.wait_ge(evac, evac_at + h)
                        for k in range(KD):
                            last = mm3(nc, ps_w[:, h, :], w_hi[:, s, k, :], w_lo[:, s, k, :],
                                       hT_hi[:, k, h * 512:(h + 1) * 512], hT_lo[:, k, h * 512:(h + 1) * 512],
                                       k == 0, k == KD - 1)
                        last.then_inc(product, 1)

                halves = 0
                for n, (_, _, rope) in enumerate(FIXED):
                    block_of(n % 2, n + 1, 2 * n - 1 if n else None)
                    if rope:
                        for h in range(2):
                            pe.wait_ge(evac, 2 * n + h + 1)
                            if halves:
                                pe.wait_ge(turn_made, halves)
                            nc.tensor.matmul(ps_r[:], K["c"][:, K_ROT:K_ROT + P],
                                             feat[:, n % 2, h * 512:(h + 1) * 512], start=True,
                                             stop=True).then_inc(rotated, 1)
                            halves += 1
                with pe.Fori(0, NFIX // 2) as i:
                    for s in range(2):
                        block_of(s, i * 2 + (NFIX + s + 1), i * 4 + (2 * NFIX + 2 * s - 1))
                pe.wait_ge(evac, 4 * NFIX)
                for n in range(3):
                    w = sum(x[1] for x in VCH[n])
                    for t in range(NT):
                        m = n * NT + t
                        if m >= 2:
                            pe.wait_ge(v_evac, m - 1)
                        for k in range(KD):
                            if t == 0 and k % VK == 0:
                                pe.wait_ge(vs_hi, VP * n + k // VK + 1)
                                pe.wait_ge(vs_lo, VP * n + k // VK + 1)
                            ts = slice(t * P, (t + 1) * P)
                            last = mm3(nc, ps_w[:, t % 2, 0:w], hT_hi[:, k, ts], hT_lo[:, k, ts],
                                       v_hi[:, k, 0:w], v_lo[:, k, 0:w], k == 0, k == KD - 1)
                        last.then_inc(v_product, 1)


def stage_compress(nc, a, K, T):
    with Scope(nc, "cmp") as sc:
        PAIRS = CMP_BLOCK // 2
        N_WIN = S // CMP_STRIDE + 1
        tok = sc.sb("tok", [P, 2, GROUPS, S + CMP_BLOCK])
        w1 = sc.sb("w1", [P, 2, PAIRS, P])
        w2 = sc.sb("w2", [P, 2, HD])
        pe_rows = sc.sb("pe_rows", [PAIRS, 2, 2 * HD])
        bias = sc.sb("bias", [P, 2])
        hid = sc.sb("hid", [P, 4, 64])
        kc = sc.sb("kc", [P, 64])
        kc_turn = sc.sb("kc_turn", [P, 64])
        kc_dup = sc.sb("kc_dup", [P, GROUPS, 64])
        fT = sc.sb("fT", [NH, S])
        fe = sc.sb("fe", [NH, S])
        ones = sc.sb("ones", [NH, S])
        cum = sc.sb("cum", [NH, S])
        bf = sc.sb("bf", [NH, 1])
        cum_hi = sc.sb("cum_hi", [NH, S], F32R)
        cum_lo = sc.sb("cum_lo", [NH, S], F32R)
        bg = sc.sb("bg", [P, 3 * NH])
        ps_h = sc.ps("ps_h", [P, 2, 512])
        ps_b = sc.ps("ps_b", [P, 512])
        ps_k = sc.ps("ps_k", [P, 512])
        ps_f = sc.ps("ps_f", [P, 1024])
        pe_in, tok_in, small_in, own_dve, own_act, dup_in, cum_out = (
            sc.sem(n) for n in ("pe_in", "tok_in", "small_in", "own_dve", "own_act", "dup_in", "cum_out"))
        f_turned, f_copied, f_exp, f_ln, cum_made, pe_turned, pe_copied, bias_copied = (
            sc.sem(n) for n in ("f_turned", "f_copied", "f_exp", "f_ln", "cum_made", "pe_turned", "pe_copied",
                                "bias_copied"))
        hid_made, hid_act, k_made, k_copied, k_rotated, k_roped, v_made, fe_made = (
            sc.sem(n) for n in ("hid_made", "hid_act", "k_made", "k_copied", "k_rotated", "k_roped", "v_made",
                                "fe_made"))
        w1_in = [sc.sem(f"w1_in{kv}") for kv in range(2)]
        g_exp, gate_in = sc.sem("g_exp"), sc.sem("gate_in")
        hid_sig = sc.sem("hid_sig")
        c = K["c"]

        def hid_of(kv):
            return ps_h[:, kv, 0:GROUPS * N_WIN].rearrange("p (g n) -> p g n", g=GROUPS)

        with sc.block() as block:
            @block.sync
            def _(sp):
                for kv, pe_ in enumerate(("pe_cmp_k", "pe_cmp_v")):
                    sp.dma_start(pe_rows[:, kv, :], a[pe_][0].rearrange("(m h) d -> m (h d)", h=2)).then_inc(pe_in, 16)
                for g in range(GROUPS):
                    for h in range(2):
                        sp.dma_start(tok[h * HD:(h + 1) * HD, :, g, 0:S - h],
                                     K["tokT"][g * HD:(g + 1) * HD, :, h:S]).then_inc(tok_in, 16)
                for kv, w in enumerate(("w_cmp_k1", "w_cmp_v1")):
                    sp.dma_start(w1[:, kv, :, :], a[w].rearrange("l (m p) n -> (l p) m n", p=P)).then_inc(w1_in[kv], 16)
                sp.wait_ge(k_roped, 1)
                for g in range(GROUPS):
                    for half in range(2):
                        sp.dma_start(kc_dup[half * HD:(half + 1) * HD, g, :],
                                     kc[g * HD:(g + 1) * HD, :]).then_inc(dup_in, 16)
                sp.wait_ge(cum_made, 1)
                sp.dma_start(T["cum"][:, 0, :], cum_hi[:].bitcast(F32)).then_inc(cum_out, 16)
                sp.dma_start(T["cum"][:, 1, :], cum_lo[:].bitcast(F32)).then_inc(cum_out, 16)
                sp.wait_ge(cum_out, 32)

            @block.tensor
            def _(pe):
                ident = c[:, K_ID:K_ID + P]
                for t in range(NT):
                    last = nc.tensor.transpose(ps_f[0:NH, t * P:(t + 1) * P], K["vsw"][:, t, 280:288], ident)
                last.then_inc(f_turned, 1)
                pe.wait_ge(pe_in, 32)
                for kv in range(2):
                    last = nc.tensor.transpose(ps_b[:, kv * PAIRS:(kv + 1) * PAIRS], pe_rows[:, kv, :],
                                               ident[0:PAIRS, 0:PAIRS])
                last.then_inc(pe_turned, 1)
                pe.wait_ge(pe_copied, 2)
                pe.wait_ge(tok_in, 64)
                for kv in range(2):
                    pe.wait_ge(w1_in[kv], 16)
                    for m in range(PAIRS):
                        win = tok[:, kv, :, 2 * m:2 * m + CMP_STRIDE * (N_WIN - 1) + 1:CMP_STRIDE]
                        last = nc.tensor.matmul(hid_of(kv), w1[:, kv, m, :], win, start=(m == 0), stop=(m == PAIRS - 1))
                    last.then_inc(hid_made, 1)
                pe.wait_ge(small_in, 48)
                pe.wait_ge(hid_act, 2)
                for g in range(GROUPS):
                    last = nc.tensor.matmul(ps_k[g * HD:(g + 1) * HD, 0:N_CMP], w2[:, 0, :], hid[:, g, 0:N_CMP],
                                            start=True, stop=True)
                last.then_inc(k_made, 1)
                for g in range(GROUPS):
                    last = nc.tensor.matmul(ps_b[0:N_CMP, 256 + g * HD:256 + (g + 1) * HD], hid[:, 2 + g, 0:N_CMP],
                                            w2[:, 1, :], start=(g == 0), stop=(g == 1), skip_group_check=True)
                last.then_inc(v_made, 1)
                pe.wait_ge(k_copied, 1)
                nc.tensor.matmul(ps_k[:, 256:256 + N_CMP], c[:, K_ROT:K_ROT + P], kc[:, 0:N_CMP], start=True,
                                 stop=True).then_inc(k_rotated, 1)

            @block.scalar
            def _(act):
                act.dma_start(bf[:], a["b_forget"].rearrange("l h -> h l")).then_inc(small_in, 16)
                act.dma_start(bg[:], a["b_nsa_gate"].to_broadcast((P, 3 * NH))).then_inc(gate_in, 16)
                act.dma_start(w2[:, 0, :], a["w_cmp_k2"][0]).then_inc(small_in, 16)
                act.dma_start(w2[:, 1, :], a["w_cmp_v2"][0]).then_inc(small_in, 16)
                act.wait_ge(fe_made, 1)
                nc.scalar.activation(fe[:], fe[:], ACT.Exp).then_inc(f_exp, 1)
                act.wait_ge(gate_in, 17)
                nc.scalar.activation(K["gate"][:], K["gate"][:], ACT.Exp, scale=-1.0).then_inc(g_exp, 1)
                act.wait_ge(f_exp, 1)
                nc.scalar.activation(fe[:], fe[:], ACT.Ln, bias=1.0).then_inc(f_ln, 1)
                act.wait_ge(bias_copied, 1)
                for kv in range(2):
                    nc.scalar.activation(hid[:, 2 * kv:2 * kv + 2, 0:N_CMP], hid_of(kv)[:, :, 0:N_CMP], ACT.Sigmoid,
                                         bias=bias[:, kv:kv + 1]).then_inc(hid_sig, 1)

            @block.vector
            def _(dve):
                own = Tally(own_dve)

                def step(ins):
                    own.inc(ins)
                    own.wait(dve)

                own.inc(nc.vector.memset(ones[:], 1.0))
                own.inc(nc.vector.memset(K["vc"][:], 0.0))
                own.inc(nc.vector.memset(K["kc_raw"][:], 0.0))
                own.inc(nc.vector.memset(kc[:], 0.0))
                dve.wait_ge(pe_turned, 1)
                for g in range(GROUPS):
                    nc.vector.tensor_copy(tok[:, :, g, S:S + CMP_BLOCK - 1:2],
                                          ps_b[:, 0:2 * PAIRS].rearrange("p (a j) -> p a j", a=2)).then_inc(pe_copied, 1)
                dve.wait_ge(small_in, 48)
                dve.wait_ge(f_turned, 1)
                step(nc.vector.tensor_scalar(fT[:], ps_f[0:NH, :], bf[:, 0:1], None, ALU.add))
                step(nc.vector.tensor_scalar(fe[:], fT[:], -1.0, None, ALU.mult))
                step(nc.vector.tensor_tensor(fe[:], fe[:], fT[:], ALU.min))
                nc.vector.tensor_scalar(fT[:], fT[:], 0.0, None, ALU.min).then_inc(fe_made, 1)
                dve.wait_ge(gate_in, 16)
                nc.vector.tensor_tensor(K["gate"][:], K["vsw"][:, :, 256:280],
                                        bg[:].unsqueeze(1).to_broadcast((P, NT, 3 * NH)),
                                        ALU.add).then_inc(gate_in, 1)
                dve.wait_ge(g_exp, 1)
                step(nc.vector.tensor_scalar(K["gate"][:], K["gate"][:], 1.0, None, ALU.add))
                step(nc.vector.reciprocal(K["gate"][:], K["gate"][:]))
                dve.wait_ge(f_ln, 1)
                dve.wait_ge(fe_made, 1)
                step(nc.vector.tensor_tensor(fT[:], fT[:], fe[:], ALU.subtract))
                step(nc.vector.tensor_tensor_scan(cum[:], ones[:], fT[:], 0.0, ALU.mult, ALU.add))
                step(nc.vector.tensor_copy(cum_hi[:], cum[:]))
                nc.vector.tensor_tensor(cum_lo[:], cum[:], cum_hi[:].bitcast(F32), ALU.subtract).then_inc(cum_made, 1)
                dve.wait_ge(hid_made, 2)
                nc.vector.tensor_copy(bias[:], ps_h[:, :, N_WIN - 1]).then_inc(bias_copied, 1)
                dve.wait_ge(bias_copied, 1)
                for kv in range(2):
                    dve.wait_ge(hid_sig, kv + 1)
                    h = hid[:, 2 * kv:2 * kv + 2, 0:N_CMP]
                    nc.vector.scalar_tensor_tensor(h, hid_of(kv)[:, :, 0:N_CMP], bias[:, kv:kv + 1], h, ALU.add,
                                                   ALU.mult).then_inc(hid_act, 1)
                dve.wait_ge(k_made, 1)
                nc.vector.tensor_copy(kc[:, 0:N_CMP], ps_k[:, 0:N_CMP]).then_inc(k_copied, 1)
                dve.wait_ge(k_copied, 1)
                dve.wait_ge(v_made, 1)
                step(nc.vector.tensor_copy(K["vc"][0:N_CMP, :, :],
                                           ps_b[0:N_CMP, 256:384].rearrange("p (g d) -> p g d", g=GROUPS)))
                dve.wait_ge(k_rotated, 1)
                ends = slice(CMP_BLOCK - 1, CMP_BLOCK + CMP_STRIDE * (N_CMP - 1), CMP_STRIDE)
                step(nc.vector.tensor_tensor(kc_turn[:, 0:N_CMP], ps_k[:, 256:256 + N_CMP], K["sin"][:, ends], ALU.mult))
                step(nc.vector.tensor_tensor(kc[:, 0:N_CMP], kc[:, 0:N_CMP], K["cos"][:, ends], ALU.mult))
                nc.vector.tensor_tensor(kc[:, 0:N_CMP], kc[:, 0:N_CMP], kc_turn[:, 0:N_CMP], ALU.add
                                        ).then_inc(k_roped, 1)
                dve.wait_ge(dup_in, 64)
                step(nc.vector.tensor_copy(K["kc_raw"][:, :, 0:64], kc_dup[:]))
                step(nc.vector.tensor_copy(K["kc_hi"][:], K["kc_raw"][:]))
                step(nc.vector.tensor_tensor(K["kc_lo"][:], K["kc_raw"][:], K["kc_hi"][:].bitcast(F32), ALU.subtract))


class Soft:

    def __init__(self, at, blocks, gate):
        self.at, self.blocks, self.gate = at, blocks, gate


def attention_steps(sparse):
    steps = []
    for qt in range(NT):
        full = [("k", kt, "diag" if kt == qt else None) for kt in range(qt + 1)]
        steps.append((qt, full, [Soft(0, [("v", kt) for kt in range(qt + 1)], 1)]))
        if sparse:
            lo = max(0, qt - WB)
            near = [("w", kt, "diag" if kt == qt else "far" if kt == qt - WB else None) for kt in range(lo, qt + 1)]
            steps.append((qt, near + [("c", 0, ("cmp", qt))],
                          [Soft(0, [("vw", kt) for kt in range(lo, qt + 1)], 2), Soft(len(near), [("vc", 0)], 0)]))
    return steps


def stage_attention(nc, K, T, sparse):
    name = "nsa" if sparse else "fox"
    with Scope(nc, name) as sc:
        q_raw = [sc.sb(f"q_raw{s}", [P, S]) for s in range(2)]
        q_st = [sc.sb(f"q_st{s}", [P, S], F32R) for s in range(2)]
        NK = GROUPS if sparse else 2
        k_raw = [sc.sb(f"k_raw{s}", [P, S]) for s in range(NK)]
        k_hi = [sc.sb(f"k_hi{s}", [P, S], F32R) for s in range(NK)]
        k_lo = [sc.sb(f"k_lo{s}", [P, S], F32R) for s in range(NK)]
        if sparse:
            w_hi = [sc.sb(f"w_hi{s}", [P, S], F32R) for s in range(NK)]
            w_lo = [sc.sb(f"w_lo{s}", [P, S], F32R) for s in range(NK)]
            gate_h = [sc.sb(f"gate_h{s}", [P, NT, 3]) for s in range(2)]
        else:
            v_h = [sc.sb(f"v_h{s}", [P, NT, HD]) for s in range(2)]
            cum_k = [sc.sb(f"cum_k{s}", [P, S], F32R) for s in range(2)]
            sel2 = sc.sb("sel2", [P, P], F32R)
        prob = sc.sb("prob", [P, 2, S])
        probT = sc.sb("probT", [P, 4, 4, P])
        o_h = [sc.sb(f"o_h{s}", [P, NT, HD]) for s in range(2)]
        mx = sc.sb("mx", [P, 2, 2])
        sums = sc.sb("sums", [P, 8, 2])
        wt = sc.sb("wt", [P, 8, 2])
        ps_s = sc.ps("ps_s", [P, 2, 1024])
        ps_t = sc.ps("ps_t", [P, 2, 512])
        ps_o = sc.ps("ps_o", [P, 2, 512])

        q_in = [sc.sem(f"q_in{s}") for s in range(2)]
        k_in = [sc.sem(f"k_in{s}") for s in range(2)]
        head_ready, head_done, v_ready, o_kept, o_made = (
            [sc.sem(f"{n}{s}") for s in range(2)] for n in ("head_ready", "head_done", "v_ready", "o_kept", "o_made"))
        scored, maxed, expd, turned, weighed = (
            sc.sem(n) for n in ("scored", "maxed", "expd", "turned", "weighed"))
        evac = [sc.sem(f"evac{b}") for b in range(2)]
        passed, q_rounded, head_part = sc.sem("passed"), sc.sem("q_rounded"), sc.sem("head_part")
        q_bytes = 32 if sparse else 64
        pv_group, own_pool, own_dve, k_rounded = (
            sc.sem(n) for n in ("pv_group", "own_pool", "own_dve", "k_rounded"))
        k_ready = [sc.sem(f"k_ready{g}") for g in range(GROUPS)]
        k_rounded1 = sc.sem("k_rounded1")

        def at(softs, i):
            return slice(len(softs) - 1 - i, len(softs) - i)

        one = attention_steps(sparse)
        steps = [(s, *x) for s in range(2) for x in one]
        N = len(steps)
        groups = []
        for n, (s, qt, cols, softs) in enumerate(steps):
            for b in range(0, len(cols), 4):
                groups.append((n, b, min(4, len(cols) - b)))
        NGR = len(groups)
        assert NGR % 2 == 0
        first_group = [min(i for i, g in enumerate(groups) if g[0] == n) for n in range(N)] + [NGR]
        TURNS = NH // 2
        runs = [(0, 0, 2), (1, 2, 4)] if sparse else [(None, 0, TURNS)]
        head0 = 0 if sparse else NH

        def feat_rows(row, half):
            return T["feat"][row, half * HD:(half + 1) * HD, :]

        with sc.block() as block:
            @block.sync
            def _(sp):
                def load_raw(s, it):
                    for row0, dst in ((0 if sparse else 8, q_raw[s]),) + (() if sparse else ((12, k_raw[s]),)):
                        row = T["feat"][bass.ds(it + row0, 1)].rearrange("a p n -> p (a n)")
                        for half in range(2):
                            sp.dma_start(dst[half * HD:(half + 1) * HD, :],
                                         row[s * HD:(s + 1) * HD, :]).then_inc(q_in[s], 16)

                def load_cum(s, it):
                    sp.dma_start(cum_k[s][0:2, :].bitcast(F32),
                                 T["cum"][bass.ds(it * 2 + s, 1)].rearrange("a b n -> (a b) n")).then_inc(k_in[s], 16)

                def load_keys(w, g):
                    if w:
                        sp.wait_ge(k_ready[g], 1)
                    for half in range(2):
                        sp.dma_start(k_raw[g][half * HD:(half + 1) * HD, :], feat_rows(6 + w, g)).then_inc(k_in[g], 16)

                if sparse:
                    load_keys(0, 0)
                for s in range(2):
                    load_raw(s, 0)
                if sparse:
                    for w, g in ((1, 0), (0, 1), (1, 1)):
                        load_keys(w, g)
                if not sparse:
                    sp.wait_ge(own_dve, 3)
                    for s in range(2):
                        load_cum(s, 0)
                with sp.Fori(1, TURNS) as it:
                    for s in range(2):
                        sp.wait_ge(head_ready[s], it)
                        load_raw(s, it)
                    if not sparse:
                        for s in range(2):
                            sp.wait_ge(head_done[s], it)
                            load_cum(s, it)

            @block.gpsimd
            def _(pool):
                for s in range(2):
                    pool.sem_inc(o_kept[s], 1)
                PER = 2 if sparse else 3

                def prepare(s, it, before):
                    own = Tally(own_pool, before * (2 * PER) + s * PER)
                    wait_alone(pool, q_in[s], it * q_bytes + q_bytes, passed)
                    own.inc(nc.gpsimd.tensor_copy(q_st[s][:], q_raw[s][:]))
                    if sparse:
                        own.inc(nc.gpsimd.tensor_copy(gate_h[s][:], K["gate"][:, :, bass.ds(it * 6 + s * 3, 3)]))
                    else:
                        own.inc(nc.gpsimd.tensor_copy(k_hi[s][:], k_raw[s][:]))
                        wait_alone(pool, own.sem, own.base + own.n, passed)
                        own.inc(nc.gpsimd.tensor_tensor(k_lo[s][:], k_raw[s][:], k_hi[s][:].bitcast(F32),
                                                        ALU.subtract))
                    wait_alone(pool, own.sem, own.base + own.n, passed)
                    nc.gpsimd.tensor_tensor(q_st[s][HD:P, :], q_raw[s][HD:P, :], q_st[s][HD:P, :].bitcast(F32),
                                            ALU.subtract).then_inc(head_ready[s], 1)
                    wait_alone(pool, head_ready[s], it + 1, passed)
                    if not sparse:
                        nc.gpsimd.tensor_copy(v_h[s][:], K["vb"][:, :, bass.ds(it * (2 * HD) + s * HD, HD)]
                                              ).then_inc(v_ready[s], 1)

                def keep(s, it):
                    wait_alone(pool, o_made[s], it + 1, passed)
                    nc.gpsimd.tensor_copy(K["o"][:, :, bass.ds(it * (2 * HD) + (head0 * HD + s * HD), HD)],
                                          o_h[s][:]).then_inc(o_kept[s], 1)

                if sparse:
                    for w, (hi, lo) in enumerate(((k_hi, k_lo), (w_hi, w_lo))):
                        pool.wait_ge(k_in[1], 32 * (w + 1))
                        nc.gpsimd.tensor_copy(hi[1][:], k_raw[1][:]).then_inc(k_rounded1, 1)
                        pool.wait_ge(k_rounded1, w + 1)
                        nc.gpsimd.tensor_tensor(lo[1][:], k_raw[1][:], hi[1][:].bitcast(F32),
                                                ALU.subtract).then_inc(k_ready[1], 1)
                with pool.Fori(0, TURNS - 1) as it:
                    for s in range(2):
                        if sparse:
                            keep(s, it)
                        wait_alone(pool, head_done[s], it + 1, passed)
                        prepare(s, it + 1, it)
                        if not sparse:
                            keep(s, it)
                for s in range(2):
                    keep(s, TURNS - 1)
                    pool.wait_ge(o_kept[s], TURNS + 1)

            def turns(eng, body):
                for g, a0, a1 in runs:
                    with eng.Fori(a0, a1) as it:
                        body(g, it)

            @block.tensor
            def _(pe):
                ident = K["c"][:, K_ID:K_ID + P]
                if not sparse:
                    pe.wait_ge(own_dve, 3)

                def scores(g, it, n):
                    s, qt, cols, softs = steps[n]
                    if n % len(one) == 0:
                        pe.wait_ge(head_ready[s], it + 1)
                        if sparse:
                            pe.wait_ge(k_ready[g], 1)
                        else:
                            pe.wait_ge(k_in[s], it * 16 + 16)
                    if sparse and n == 1:
                        pe.wait_ge(k_ready[g], 2)
                    pe.wait_ge(expd, it * N + (n - 1 if n >= 2 else 0) + 1)
                    q = q_st[s][:, qt * P:(qt + 1) * P]
                    pieces, b = [], 0
                    while b < len(cols):
                        e = b + 1
                        while e < len(cols) and e % 4 and cols[e][0] == cols[b][0]:
                            e += 1
                        pieces.append((b, e))
                        b = e
                    started = set()
                    for i, (b, e) in enumerate(pieces):
                        src, kt, _ = cols[b]
                        out = ps_s[:, n % 2, b * P:e * P]
                        ks = slice(kt * P, (kt + e - b) * P)
                        kk = g if sparse else s
                        if src == "k":
                            parts = (k_hi[kk][:, ks], k_lo[kk][:, ks])
                        elif src == "w":
                            parts = (w_hi[kk][:, ks], w_lo[kk][:, ks])
                        else:
                            parts = (K["kc_hi"][:, kk, :], K["kc_lo"][:, kk, :])
                        bank = b // 4
                        masks = [(j, cols[j][2]) for j in range(b, e) if cols[j][2]]
                        lastpiece = i + 1 == len(pieces) or pieces[i + 1][0] // 4 != bank
                        last = nc.tensor.matmul(out, q, parts[0], start=bank not in started, stop=False,
                                                skip_group_check=True)
                        started.add(bank)
                        last = nc.tensor.matmul(out, q, parts[1], start=False,
                                                stop=lastpiece and not masks and sparse, skip_group_check=True)
                        if not sparse:
                            last = nc.tensor.matmul(out, sel2[:], cum_k[s][:, ks], start=False,
                                                    stop=lastpiece and not masks, skip_group_check=True)
                        for m, (j, kind) in enumerate(masks):
                            col = 0 if kind == "diag" else P if kind == "far" else (2 + kind[1]) * P
                            last = nc.tensor.matmul(ps_s[:, n % 2, j * P:(j + 1) * P], K["identb"][:],
                                                    K["maskb"][:, col:col + P], start=False,
                                                    stop=lastpiece and m == len(masks) - 1, skip_group_check=True)
                    last.then_inc(scored, 1)

                def turn_group(g, it, gr):
                    n, b, w = groups[gr]
                    pe.wait_ge(evac[gr % 2], it * (NGR // 2) + (gr // 2) + 1)
                    for j in range(w):
                        last = nc.tensor.transpose(ps_t[:, gr % 2, j * P:(j + 1) * P],
                                                   prob[:, n % 2, (b + j) * P:(b + j + 1) * P], ident)
                    last.then_inc(turned, 1)

                def values(g, it, gr):
                    n, b, w = groups[gr]
                    s, qt, cols, softs = steps[n]
                    pe.wait_ge(evac[gr % 2], it * (NGR // 2) + (gr // 2) + 2)
                    if not sparse and gr == first_group[n] and n % len(one) == 0:
                        pe.wait_ge(v_ready[s], it + 1)
                    if gr == first_group[n]:
                        pe.wait_ge(weighed, it * N + (n - 1 if n >= 2 else 0) + 1)
                    for j in range(w):
                        blk = b + j
                        i = max(k for k, so in enumerate(softs) if so.at <= blk)
                        src, kt = softs[i].blocks[blk - softs[i].at]
                        if src == "v":
                            val = K["vsw"][:, kt, g * HD:(g + 1) * HD] if sparse else v_h[s][:, kt, :]
                        elif src == "vw":
                            val = K["vsw"][:, kt, 128 + g * HD:128 + (g + 1) * HD]
                        else:
                            val = K["vc"][:, g, :]
                        last = nc.tensor.matmul(ps_o[:, n % 2, i * HD:(i + 1) * HD], probT[:, gr % 4, j, :], val,
                                                start=(blk == 0), stop=(blk == softs[i].at + len(softs[i].blocks) - 1),
                                                skip_group_check=True)
                    last.then_inc(pv_group, 1)

                def body(g, it):
                    scores(g, it, 0)
                    scores(g, it, 1)
                    for n in range(N + 1):
                        if n < N:
                            pe.wait_ge(expd, it * N + (n + 2))
                            for gr in range(first_group[n], first_group[n + 1]):
                                turn_group(g, it, gr)
                        if n + 2 < N:
                            scores(g, it, n + 2)
                        if n:
                            for gr in range(first_group[n - 1], first_group[n]):
                                values(g, it, gr)
                        if n and n % len(one) == 0:
                            pe.wait_ge(pv_group, it * NGR + first_group[n])
                            pe.sem_inc(head_done[steps[n - 1][0]], 1)

                turns(pe, body)

            def copy_group(eng, it, gr, copy):
                n, b, w = groups[gr]
                eng.wait_ge(turned, it * NGR + (gr + 1))
                if gr >= 4:
                    eng.wait_ge(pv_group, it * NGR + (gr - 3))
                copy(probT[:, gr % 4, 0:w, :], ps_t[:, gr % 2, 0:w * P].rearrange("p (j n) -> p j n", n=P)
                     ).then_inc(evac[gr % 2], 1)

            @block.scalar
            def _(act):
                act.sem_inc(expd, 1)
                act.sem_inc(evac[1], 1)
                def keys(w):
                    act.wait_ge(k_in[0], 32 * (w + 1))
                    nc.scalar.activation((w_hi if w else k_hi)[0][:], k_raw[0][:], ACT.Copy).then_inc(k_rounded, 1)

                def first_head(s):
                    act.wait_ge(q_in[s], q_bytes)
                    if not sparse:
                        nc.scalar.activation(k_hi[s][:], k_raw[s][:], ACT.Copy).then_inc(k_rounded, 1)
                    nc.scalar.activation(q_st[s][:], q_raw[s][:], ACT.Copy).then_inc(q_rounded, 1)

                if sparse:
                    keys(0)
                    first_head(0)
                    keys(1)
                    first_head(1)
                else:
                    first_head(0)
                    first_head(1)

                def exps(it, n):
                    s, qt, cols, softs = steps[n]
                    act.wait_ge(maxed, it * N + (n + 1))
                    if n >= 2:
                        act.wait_ge(turned, it * NGR + first_group[n - 1])
                    for i, so in enumerate(softs):
                        r = slice(so.at * P, (so.at + len(so.blocks)) * P)
                        last = nc.scalar.activation(prob[:, n % 2, r], ps_s[:, n % 2, r], ACT.Exp,
                                                    bias=mx[:, n % 2, i:i + 1], scale=-1.0,
                                                    accum_out=sums[:, n % 8, at(softs, i)])
                    last.then_inc(expd, 1)

                def body(g, it):
                    exps(it, 0)
                    exps(it, 1)
                    for n in range(N):
                        for gr in range(first_group[n], first_group[n + 1]):
                            if gr % 2 == 1:
                                copy_group(act, it, gr, lambda o, x: nc.scalar.activation(o, x, ACT.Copy))
                        if n + 2 < N:
                            exps(it, n + 2)

                turns(act, body)

            @block.vector
            def _(dve):
                dve.sem_inc(evac[0], 1)
                dve.sem_inc(weighed, 1)
                def keys(w):
                    hi, lo = (w_hi, w_lo) if w else (k_hi, k_lo)
                    dve.wait_ge(k_rounded, w + 1)
                    nc.vector.tensor_tensor(lo[0][:], k_raw[0][:], hi[0][:].bitcast(F32),
                                            ALU.subtract).then_inc(k_ready[0], 1)

                def first_head(s):
                    dve.wait_ge(q_in[s], q_bytes)
                    if sparse:
                        nc.vector.tensor_copy(gate_h[s][:], K["gate"][:, :, 3 * s:3 * s + 3]).then_inc(head_part, 1)
                    else:
                        nc.vector.tensor_copy(v_h[s][:], K["vb"][:, :, s * HD:(s + 1) * HD]).then_inc(v_ready[s], 1)
                        dve.wait_ge(k_rounded, s + 1)
                        nc.vector.tensor_tensor(k_lo[s][:], k_raw[s][:], k_hi[s][:].bitcast(F32),
                                                ALU.subtract).then_inc(head_part, 1)
                    dve.wait_ge(q_rounded, s + 1)
                    dve.wait_ge(head_part, s + 1)
                    nc.vector.tensor_tensor(q_st[s][HD:P, :], q_raw[s][HD:P, :], q_st[s][HD:P, :].bitcast(F32),
                                            ALU.subtract).then_inc(head_ready[s], 1)

                if sparse:
                    keys(0)
                    first_head(0)
                    keys(1)
                    first_head(1)
                else:
                    nc.vector.tensor_copy(sel2[:], K["c"][:, K_ONE:K_ONE + P]).then_inc(own_dve, 1)
                    for s in range(2):
                        nc.vector.tensor_scalar(cum_k[s][:], K["cos"][:], 0.0, None, ALU.mult).then_inc(own_dve, 1)
                    first_head(0)
                    first_head(1)

                OWN0 = 0 if sparse else 3

                def max_of(it, n):
                    s, qt, cols, softs = steps[n]
                    dve.wait_ge(scored, it * N + (n + 1))
                    if n >= 2:
                        dve.wait_ge(expd, it * N + n)
                    else:
                        dve.wait_ge(expd, it * N + 1)
                    for i, so in enumerate(softs):
                        r = slice(so.at * P, (so.at + len(so.blocks)) * P)
                        last = nc.vector.tensor_reduce(mx[:, n % 2, i:i + 1], ps_s[:, n % 2, r], X, ALU.min)
                    last.then_inc(maxed, 1)

                def weigh(it, n, own):
                    s, qt, cols, softs = steps[n]
                    k = len(softs)
                    dve.wait_ge(pv_group, it * NGR + first_group[n + 1])
                    w = wt[:, n % 8, 0:k]
                    own.inc(nc.vector.reciprocal(w, sums[:, n % 8, 0:k]))
                    own.wait(dve)
                    o = o_h[s][:, qt, :]
                    if n % len(one) == 0:
                        dve.wait_ge(o_kept[s], it + 1)
                    if not sparse:
                        nc.vector.tensor_scalar(o, ps_o[:, n % 2, 0:HD], w, None,
                                                ALU.mult).then_inc(weighed, 1)
                    elif k == 1:
                        nc.vector.tensor_scalar(o, ps_o[:, n % 2, 0:HD], w, gate_h[s][:, qt, 1:2],
                                                ALU.mult, ALU.mult).then_inc(weighed, 1)
                    else:
                        own.inc(nc.vector.tensor_tensor(w, w, gate_h[s][:, qt, 0:3:2], ALU.mult))
                        own.wait(dve)
                        if qt == 0:
                            own.inc(nc.vector.tensor_tensor(wt[:, n % 8, 0:1], wt[:, n % 8, 0:1],
                                                            K["c"][:, K_VALID:K_VALID + 1], ALU.mult))
                            own.wait(dve)
                        dve.wait_ge(weighed, it * N + (n + 1))
                        own.inc(nc.vector.scalar_tensor_tensor(o, ps_o[:, n % 2, 0:HD], wt[:, n % 8, 1:2], o,
                                                               ALU.mult, ALU.add))
                        own.wait(dve)
                        nc.vector.scalar_tensor_tensor(o, ps_o[:, n % 2, HD:2 * HD], wt[:, n % 8, 0:1], o,
                                                       ALU.mult, ALU.add).then_inc(weighed, 1)
                    if n % len(one) == len(one) - 1:
                        dve.wait_ge(weighed, it * N + (n + 2))
                        dve.sem_inc(o_made[s], 1)

                def plan(own, it):
                    max_of(it, 0)
                    max_of(it, 1)
                    for n in range(N):
                        for gr in range(first_group[n], first_group[n + 1]):
                            if gr % 2 == 0:
                                copy_group(dve, it, gr, nc.vector.tensor_copy)
                        if n + 2 < N:
                            max_of(it, n + 2)
                        if n >= 2:
                            weigh(it, n - 2, own)
                    weigh(it, N - 2, own)
                    weigh(it, N - 1, own)

                OWN = 2 * N + 2 if sparse else N

                def body(g, it):
                    own = Tally(own_dve, it * OWN + OWN0)
                    plan(own, it)
                    assert own.n == OWN, (own.n, OWN)

                turns(dve, body)


def stage_mix(nc, a, K, T):
    with Scope(nc, "mix") as sc:
        HALF = NH * HD
        w_raw = sc.sb("w_raw", [P, 2, D])
        w_hi = sc.sb("w_hi", [P, KD, D], F32R)
        w_lo = sc.sb("w_lo", [P, KD, D], F32R)
        beta = sc.sb("beta", [P, D])
        gain = sc.sb("gain", [P, D])
        w_rt = sc.sb("w_rt", [P, KD, NG + NE])
        b_rt = sc.sb("b_rt", [1, NG + NE])
        junk = sc.sb("junk", [P, D], BF16)
        ss = sc.sb("ss", [P, NT, 3])
        rt = sc.sb("rt", [P, NT, 3])
        rs = sc.sb("rs", [P, NT, 3])
        xt = sc.sb("x", [P, 2, D])
        mT_hi = sc.sb("mT_hi", [P, 2, KD, P], F32R)
        mT_lo = sc.sb("mT_lo", [P, 2, KD, P], F32R)
        ht = sc.sb("h", [P, 2, D])
        ut = sc.sb("u", [P, 2, D])
        uT = sc.sb("uT", [P, KD, P])
        ps_x = sc.ps("ps_x", [P, 2, 512])
        ps_y = sc.ps("ps_y", [P, 2, 512])
        ps_u = sc.ps("ps_u", [P, 2, 512])
        ps_l = sc.ps("ps_l", [P, 512])
        w_in = [sc.sem(f"w_in{i}") for i in range(2)]
        x_in = [sc.sem(f"x_in{i}") for i in range(2)]
        h_out = [sc.sem(f"h_out{i}") for i in range(2)]
        u_out = [sc.sem(f"u_out{i}") for i in range(2)]
        (vec_in, rt_in, split_hi, split_lo, o_sq, o_var, o_root, o_norm, turned, m_hi, m_lo, product, h_made, h_sq,
         h_var, h_root, u_made, u_turned, u_copied, logits, own_dve) = (
            sc.sem(n) for n in ("vec_in", "rt_in", "split_hi", "split_lo", "o_sq", "o_var", "o_root", "o_norm",
                                "turned", "m_hi", "m_lo", "product", "h_made", "h_sq", "h_var", "h_root", "u_made",
                                "u_turned", "u_copied", "logits", "own_dve"))
        x_d = a["x"].rearrange("b (t p) d -> (b t) p d", p=P)
        w_d = a["w_out"].rearrange("l (k p) n -> (l k) p n", p=P)
        with sc.block() as block:
            @block.sync
            def _(sp):
                sp.dma_start(beta[:, 0:HALF], a["beta_nsa"].to_broadcast((P, HALF))).then_inc(vec_in, 16)
                sp.dma_start(beta[:, HALF:D], a["beta_fox"].to_broadcast((P, HALF))).then_inc(vec_in, 16)
                sp.dma_start(gain[:], a["g_ffn"].to_broadcast((P, D))).then_inc(vec_in, 16)
                for k in range(KD):
                    if k >= 2:
                        sp.wait_ge(split_hi, k - 1)
                        sp.wait_ge(split_lo, k - 1)
                    sp.dma_start(w_raw[:, k % 2, :], w_d[k]).then_inc(w_in[k % 2], 16)
                    if k < 2:
                        sp.dma_start(xt[:, k, :], x_d[k]).then_inc(x_in[k], 16)
                sp.dma_start(w_rt[:, :, 0:NG], a["w_group"].rearrange("l (k p) n -> (l p) k n", p=P)).then_inc(rt_in, 16)
                sp.dma_start(w_rt[:, :, NG:], a["w_router"].rearrange("l (k p) n -> (l p) k n", p=P)).then_inc(rt_in, 16)
                sp.dma_start(b_rt[:, 0:NG], a["b_group"]).then_inc(rt_in, 16)
                sp.dma_start(b_rt[:, NG:], a["b_router"]).then_inc(rt_in, 16)
                for t in range(NT):
                    sp.wait_ge(h_made, 2 * t + 2)
                    sp.dma_start(T["h"][t], ht[:, t % 2, :]).then_inc(h_out[t % 2], 16)
                    if t + 2 < NT:
                        sp.dma_start(xt[:, t % 2, :], x_d[t + 2]).then_inc(x_in[t % 2], 16)
                    sp.wait_ge(u_made, t + 1)
                    sp.dma_start(T["u"][t * P:(t + 1) * P, :], ut[:, t % 2, :]).then_inc(u_out[t % 2], 16)
                for s in range(2):
                    sp.wait_ge(h_out[s], 16 * (NT // 2))
                    sp.wait_ge(u_out[s], 16 * (NT // 2))

            def tiles(norm, turn, leave, mix, route, split):
                norm(0)
                turn(0)
                norm(1)
                split()
                for i in range(NT + 2):
                    if i >= 2:
                        route(i - 2)
                    if 1 <= i <= NT:
                        leave(i - 1)
                    if i + 1 < NT:
                        turn(i + 1)
                    if 1 <= i <= NT:
                        mix(i - 1)
                    if i + 2 < NT:
                        norm(i + 2)

            @block.scalar
            def _(act):
                def split():
                    for k in range(KD):
                        act.wait_ge(w_in[k % 2], 16 * (k // 2 + 1))
                        nc.scalar.activation(w_hi[:, k, :], w_raw[:, k % 2, :], ACT.Copy).then_inc(split_hi, 1)

                def norm(t):
                    for g in range(2):
                        nc.scalar.activation(junk[:, g * HALF:(g + 1) * HALF],
                                             K["o"][:, t, g * HALF:(g + 1) * HALF], ACT.Square,
                                             accum_out=ss[:, t, g:g + 1]).then_inc(o_sq, 1)
                    act.wait_ge(o_var, t + 1)
                    nc.scalar.activation(rt[:, t, 0:2], rt[:, t, 0:2], ACT.Sqrt).then_inc(o_root, 1)

                def turn(t):
                    for h in range(2):
                        act.wait_ge(turned, 2 * t + h + 1)
                        if t >= 2:
                            act.wait_ge(product, t - 1)
                        nc.scalar.activation(mT_hi[:, t % 2, 4 * h:4 * h + 4, :],
                                             ps_x[:, h, :].rearrange("p (k n) -> p k n", k=4),
                                             ACT.Copy).then_inc(m_hi, 1)

                def leave(t):
                    pass

                def mix(t):
                    act.wait_ge(h_made, 2 * t + 2)
                    nc.scalar.activation(junk[:], ht[:, t % 2, :], ACT.Square,
                                         accum_out=ss[:, t, 2:3]).then_inc(h_sq, 1)
                    act.wait_ge(h_var, t + 1)
                    nc.scalar.activation(rt[:, t, 2:3], rt[:, t, 2:3], ACT.Sqrt).then_inc(h_root, 1)

                def route(t):
                    for h in range(2):
                        act.wait_ge(u_turned, 2 * t + h + 1)
                        if t:
                            act.wait_ge(logits, t)
                        nc.scalar.activation(uT[:, 4 * h:4 * h + 4, :],
                                             ps_u[:, h, :].rearrange("p (k n) -> p k n", k=4),
                                             ACT.Copy).then_inc(u_copied, 1)

                tiles(norm, turn, leave, mix, route, split)

            @block.vector
            def _(dve):
                own = Tally(own_dve)

                def split():
                    for k in range(KD):
                        dve.wait_ge(split_hi, k + 1)
                        nc.vector.tensor_tensor(w_lo[:, k, :], w_raw[:, k % 2, :], w_hi[:, k, :].bitcast(F32),
                                                ALU.subtract).then_inc(split_lo, 1)

                dve.wait_ge(vec_in, 48)

                def norm(t):
                    dve.wait_ge(o_sq, 2 * t + 2)
                    nc.vector.tensor_scalar(rt[:, t, 0:2], ss[:, t, 0:2], 1.0 / HALF, EPS, ALU.mult,
                                            ALU.add).then_inc(o_var, 1)
                    dve.wait_ge(o_root, t + 1)
                    own.inc(nc.vector.reciprocal(rs[:, t, 0:2], rt[:, t, 0:2]))
                    own.wait(dve)
                    for g in range(2):
                        og = K["o"][:, t, g * HALF:(g + 1) * HALF]
                        nc.vector.scalar_tensor_tensor(og, og, rs[:, t, g:g + 1], beta[:, g * HALF:(g + 1) * HALF],
                                                       ALU.mult, ALU.mult).then_inc(o_norm, 1)

                def turn(t):
                    for h in range(2):
                        dve.wait_ge(m_hi, 2 * t + h + 1)
                        nc.vector.tensor_tensor(mT_lo[:, t % 2, 4 * h:4 * h + 4, :],
                                                ps_x[:, h, :].rearrange("p (k n) -> p k n", k=4),
                                                mT_hi[:, t % 2, 4 * h:4 * h + 4, :].bitcast(F32),
                                                ALU.subtract).then_inc(m_lo, 1)

                def leave(t):
                    dve.wait_ge(product, t + 1)
                    dve.wait_ge(x_in[t % 2], 16 * (t // 2 + 1))
                    if t >= 2:
                        dve.wait_ge(h_out[t % 2], 16 * (t // 2))
                    for h in range(2):
                        r = slice(h * 512, (h + 1) * 512)
                        nc.vector.tensor_tensor(ht[:, t % 2, r], ps_y[:, h, :], xt[:, t % 2, r],
                                                ALU.add).then_inc(h_made, 1)

                def mix(t):
                    dve.wait_ge(h_sq, t + 1)
                    nc.vector.tensor_scalar(rt[:, t, 2:3], ss[:, t, 2:3], 1.0 / D, EPS, ALU.mult,
                                            ALU.add).then_inc(h_var, 1)
                    dve.wait_ge(h_root, t + 1)
                    own.inc(nc.vector.reciprocal(rs[:, t, 2:3], rt[:, t, 2:3]))
                    own.wait(dve)
                    if t >= 2:
                        dve.wait_ge(u_out[t % 2], 16 * (t // 2))
                        dve.wait_ge(u_turned, 2 * (t - 1))
                    nc.vector.scalar_tensor_tensor(ut[:, t % 2, :], ht[:, t % 2, :], rs[:, t, 2:3], gain[:],
                                                   ALU.mult, ALU.mult).then_inc(u_made, 1)

                def route(t):
                    pass

                tiles(norm, turn, leave, mix, route, split)
                dve.wait_ge(logits, NT)
                own.inc(nc.vector.tensor_copy(K["lg"][:], ps_l[:, 0:NT * (NG + NE)].rearrange("p (t n) -> p t n", t=NT)))
                own.wait(dve)

            @block.tensor
            def _(pe):
                ident = K["c"][:, K_ID:K_ID + P]

                def turn(t):
                    pe.wait_ge(o_norm, 2 * t + 2)
                    for h in range(2):
                        if t:
                            pe.wait_ge(m_lo, 2 * t + h - 1)
                        for j in range(4):
                            k = 4 * h + j
                            last = nc.tensor.transpose(ps_x[:, h, j * P:(j + 1) * P],
                                                       K["o"][:, t, k * P:(k + 1) * P], ident)
                        last.then_inc(turned, 1)

                def mix(t):
                    pe.wait_ge(m_lo, 2 * t + 2)
                    for h in range(2):
                        if t:
                            pe.wait_ge(h_made, 2 * t + h - 1)
                        for k in range(KD):
                            if t == 0 and h == 0:
                                pe.wait_ge(split_lo, k + 1)
                            last = mm3(nc, ps_y[:, h, :], mT_hi[:, t % 2, k, :], mT_lo[:, t % 2, k, :],
                                       w_hi[:, k, h * 512:(h + 1) * 512], w_lo[:, k, h * 512:(h + 1) * 512],
                                       k == 0, k == KD - 1)
                    last.then_inc(product, 1)

                def turn_u(t):
                    pe.wait_ge(u_made, t + 1)
                    for h in range(2):
                        if t:
                            pe.wait_ge(u_copied, 2 * t + h - 1)
                        for j in range(4):
                            k = 4 * h + j
                            last = nc.tensor.transpose(ps_u[:, h, j * P:(j + 1) * P],
                                                       ut[:, t % 2, k * P:(k + 1) * P], ident)
                        last.then_inc(u_turned, 1)

                def route(t):
                    pe.wait_ge(u_copied, 2 * t + 2)
                    pe.wait_ge(rt_in, 64)
                    out = ps_l[:, t * (NG + NE):(t + 1) * (NG + NE)]
                    for k in range(KD):
                        nc.tensor.matmul(out, uT[:, k, :], w_rt[:, k, :], start=(k == 0), stop=False)
                    nc.tensor.matmul(out, K["c"][0:1, K_ONE:K_ONE + P], b_rt[:], start=False,
                                     stop=True).then_inc(logits, 1)

                turn(0)
                for i in range(NT + 2):
                    if i + 1 < NT:
                        turn(i + 1)
                    if i >= 2:
                        route(i - 2)
                    if i < NT:
                        mix(i)
                    if 1 <= i <= NT:
                        turn_u(i - 1)


def stage_route(nc, K, T):
    with Scope(nc, "rte") as sc:
        def sb(name, *shape):
            return sc.sb(name, [P, *shape])

        gmax, gsum, gp, pm = (sb(n, NT) for n in ("gmax", "gsum", "gp", "pm"))
        dlt, pri, ohg, il, oh1, oh2, il2 = (sb(n, NT, 4) for n in ("dlt", "pri", "ohg", "il", "oh1", "oh2", "il2"))
        m1, m2, e2, v1 = (sb(n, NT) for n in ("m1", "m2", "e2", "v1"))
        prod = sb("prod", NT, NG, EPG)
        pick = [sb(f"pick{k}", NT, NG, EPG) for k in range(2)]
        both = sb("both", NT * NE)
        off = sb("off", NT + 1, NE)
        tot = sb("tot", NT, NE)
        where = sb("where", NT, NE)
        cnt_i = sc.sb("cnt_i", [P, NE], I32)
        ntl, cend, cbeg, ones = (sb(n, NE) for n in ("ntl", "cend", "cbeg", "ones"))
        tile_ge = sb("tile_ge", 32, NE)
        tile_e = sb("tile_e", 32)
        tile_new = sb("tile_new", 32)
        tile_ord = sb("tile_ord", 32)
        n_last = sb("n_last", 1)
        slot_f = sb("slot_f", 2, NT)
        row_f = sb("row_f", 2, NT)
        in_tile = sb("in_tile", 2, NT)
        slot_i = sc.sb("slot_i", [P, 2, NT], I32)
        is_row = sb("is_row", 2 * NT, P)
        is_tile = sb("is_tile", 2 * NT, SLOTS // P)
        ps_r = sc.ps("ps_r", [P, 512])
        ps_t = sc.ps("ps_t", [P, 512])
        ps_s = sc.ps("ps_s", [P, 512])
        own_dve, expd, want_exp, ranked, both_made, slots_made, named = (
            sc.sem(n) for n in ("own_dve", "expd", "want_exp", "ranked", "both_made", "slots_made", "named"))
        c = K["c"]
        lg = K["lg"]
        with sc.block() as block:
            @block.vector
            def _(dve):
                own = Tally(own_dve)

                def step(ins):
                    own.inc(ins)
                    own.wait(dve)

                V = nc.vector

                def wide(x, n=4):
                    return x[:].unsqueeze(2).to_broadcast((P, NT, n))

                def first_max(x, top, out):
                    step(V.tensor_tensor(pri[:], x, wide(top), ALU.is_equal))
                    step(V.tensor_tensor(pri[:], pri[:], c[:, K_PRI:K_PRI + 4].unsqueeze(1).to_broadcast((P, NT, 4)),
                                         ALU.mult))
                    step(V.tensor_reduce(pm[:], pri[:], X, ALU.max))
                    step(V.tensor_tensor(out[:], pri[:], wide(pm), ALU.is_equal))

                step(V.memset(ones[:], 1.0))
                step(V.tensor_reduce(gmax[:], lg[:, :, 0:NG], X, ALU.max))
                V.tensor_tensor(dlt[:], lg[:, :, 0:NG], wide(gmax), ALU.subtract).then_inc(want_exp, 1)
                first_max(lg[:, :, 0:NG], gmax, ohg)
                step(V.tensor_tensor(prod[:], lg[:, :, NG:].rearrange("p t (g j) -> p t g j", g=NG),
                                     ohg[:].unsqueeze(3).to_broadcast((P, NT, NG, EPG)), ALU.mult))
                step(V.tensor_reduce(il[:], prod[:].rearrange("p t g j -> p t j g"), X, ALU.add))
                step(V.tensor_reduce(m1[:], il[:], X, ALU.max))
                first_max(il[:], m1, oh1)
                step(V.scalar_tensor_tensor(il2[:], oh1[:], NEG, il[:], ALU.mult, ALU.add))
                step(V.tensor_reduce(m2[:], il2[:], X, ALU.max))
                first_max(il2[:], m2, oh2)
                V.tensor_tensor(e2[:], m2[:], m1[:], ALU.subtract).then_inc(want_exp, 1)
                for k, oh in enumerate((oh1, oh2)):
                    step(V.tensor_tensor(pick[k][:], ohg[:].unsqueeze(3).to_broadcast((P, NT, NG, EPG)),
                                         oh[:].unsqueeze(2).to_broadcast((P, NT, NG, EPG)), ALU.mult))
                V.tensor_tensor(both[:], pick[0][:].rearrange("p t g j -> p (t g j)"),
                                pick[1][:].rearrange("p t g j -> p (t g j)"), ALU.add).then_inc(both_made, 1)
                dve.wait_ge(expd, 2)
                step(V.tensor_reduce(gsum[:], dlt[:], X, ALU.add))
                step(V.reciprocal(gp[:], gsum[:]))
                step(V.tensor_scalar(v1[:], e2[:], 1.0, None, ALU.add))
                step(V.reciprocal(v1[:], v1[:]))
                step(V.tensor_tensor(K["cw"][:, 0, :], v1[:], gp[:], ALU.mult))
                step(V.tensor_tensor(K["cw"][:, 1, :], K["cw"][:, 0, :], e2[:], ALU.mult))
                dve.wait_ge(ranked, 2)
                step(V.tensor_copy(tot[:], ps_t[:, 0:NT * NE].rearrange("p (t e) -> p t e", t=NT)))
                step(V.memset(off[:, 0, :], 0.0))
                for t in range(NT):
                    step(V.tensor_tensor(off[:, t + 1, :], off[:, t, :], tot[:, t, :], ALU.add))
                step(V.tensor_scalar(ntl[:], off[:, NT, :], float(P - 1), None, ALU.add))
                step(V.tensor_copy(cnt_i[:], ntl[:]))
                step(V.tensor_scalar(cnt_i[:], cnt_i[:], 7, None, ALU.arith_shift_right))
                step(V.tensor_copy(ntl[:], cnt_i[:]))
                step(V.tensor_tensor_scan(cend[:], ones[:], ntl[:], 0.0, ALU.mult, ALU.add))
                step(V.tensor_tensor(cbeg[:], cend[:], ntl[:], ALU.subtract))
                step(V.tensor_tensor(where[:], ps_r[:, 0:NT * NE].rearrange("p (t e) -> p t e", t=NT),
                                     off[:, 0:NT, :], ALU.add))
                step(V.scalar_tensor_tensor(where[:], cbeg[:].unsqueeze(1).to_broadcast((P, NT, NE)), float(P),
                                            where[:], ALU.mult, ALU.add))
                for k in range(2):
                    step(V.tensor_tensor(prod[:].rearrange("p t g j -> p t (g j)"), where[:],
                                         pick[k][:].rearrange("p t g j -> p t (g j)"), ALU.mult))
                    step(V.tensor_reduce(slot_f[:, k, :], prod[:].rearrange("p t g j -> p t (g j)"), X, ALU.add))
                step(V.tensor_copy(K["slot"][:], slot_f[:]))
                step(V.tensor_copy(slot_i[:], slot_f[:]))
                step(V.tensor_scalar(slot_i[:], slot_i[:], 7, None, ALU.arith_shift_right))
                step(V.tensor_copy(in_tile[:], slot_i[:]))
                step(V.scalar_tensor_tensor(row_f[:], in_tile[:], -float(P), slot_f[:], ALU.mult, ALU.add))
                step(V.tensor_tensor(is_tile[:], c[:, K_TILE:K_TILE + 32].unsqueeze(1).to_broadcast((P, 2 * NT, 32)),
                                     in_tile[:].rearrange("p k t -> p (k t)").unsqueeze(2).to_broadcast((P, 2 * NT, 32)),
                                     ALU.is_equal))
                for k in range(2):
                    tile_of = is_tile[:, k * NT:(k + 1) * NT, :]
                    step(V.tensor_tensor(tile_of, tile_of, c[:, K_TOK:K_TOK + NT].unsqueeze(2).to_broadcast((P, NT, 32)), ALU.mult))
                V.tensor_tensor(is_row[:], c[:, K_IOTA:K_IOTA + P].unsqueeze(1).to_broadcast((P, 2 * NT, P)),
                                row_f[:].rearrange("p k t -> p (k t)").unsqueeze(2).to_broadcast((P, 2 * NT, P)),
                                ALU.is_equal).then_inc(slots_made, 1)
                step(V.tensor_tensor(tile_ge[:], c[:, K_TILE:K_TILE + 32].unsqueeze(2).to_broadcast((P, 32, NE)),
                                     cend[:].unsqueeze(1).to_broadcast((P, 32, NE)), ALU.is_ge))
                step(V.tensor_reduce(tile_e[:], tile_ge[:], X, ALU.add))
                step(V.tensor_scalar(tile_e[:], tile_e[:], float(NE - 1), None, ALU.min))
                step(V.tensor_copy(K["texp"][:], tile_e[:]))
                step(V.tensor_scalar(n_last[:], cend[:, NE - 1:NE], -1.0, None, ALU.add))
                step(V.tensor_copy(K["last"][:], n_last[:]))
                step(V.memset(tile_new[:], 0.0))
                step(V.tensor_tensor(tile_new[:, 1:], tile_e[:, 1:], tile_e[:, 0:31], ALU.not_equal))
                step(V.tensor_copy(K["tnew"][:], tile_new[:]))
                step(V.tensor_copy(tile_ge[:, :, 0], tile_new[:]))
                step(V.memset(tile_ge[:, :, 1], 1.0))
                step(V.tensor_tensor_scan(tile_ord[:], tile_ge[:, :, 1], tile_ge[:, :, 0], 0.0, ALU.mult, ALU.add))
                step(V.tensor_copy(K["tord"][:], tile_ord[:]))
                dve.wait_ge(named, 1)
                step(V.tensor_copy(K["stok"][:], ps_s[:, 0:SLOTS // P]))

            @block.scalar
            def _(act):
                act.wait_ge(want_exp, 1)
                nc.scalar.activation(dlt[:], dlt[:], ACT.Exp).then_inc(expd, 1)
                act.wait_ge(want_exp, 2)
                nc.scalar.activation(e2[:], e2[:], ACT.Exp).then_inc(expd, 1)

            @block.tensor
            def _(pe):
                pe.wait_ge(both_made, 1)
                nc.tensor.matmul(ps_r[:, 0:NT * NE], c[:, K_LT:K_LT + P], both[:], start=True, stop=True).then_inc(ranked, 1)
                nc.tensor.matmul(ps_t[:, 0:NT * NE], c[:, K_ONE:K_ONE + P], both[:], start=True, stop=True).then_inc(ranked, 1)
                pe.wait_ge(slots_made, 1)
                for n in range(2 * NT):
                    last = nc.tensor.matmul(ps_s[:, 0:SLOTS // P], is_row[:, n, :], is_tile[:, n, :], start=(n == 0),
                                            stop=(n == 2 * NT - 1))
                last.then_inc(named, 1)


def stage_moe(nc, a, K, T):
    GC, DC = KD, KF
    EARLY = 4
    GR, DR = GC, DC
    with Scope(nc, "moe") as sc:
        g_raw = sc.sb("g_raw", [P, GC, 2, FE])
        d_raw = sc.sb("d_raw", [P, DC, D])
        g_hi = sc.sb("g_hi", [P, GR, 2, FE], F32R)
        g_lo = sc.sb("g_lo", [P, GR, 2, FE], F32R)
        d_hi = sc.sb("d_hi", [P, DR, D], F32R)
        d_lo = sc.sb("d_lo", [P, DR, D], F32R)
        xg = sc.sb("xg", [P, D])
        idx = sc.sb("idx", [P, 1], U32)
        xT_hi = sc.sb("xT_hi", [P, KD, P], F32R)
        xT_lo = sc.sb("xT_lo", [P, KD, P], F32R)
        act_g = sc.sb("act_g", [P, FE])
        hid = sc.sb("hid", [P, FE])
        hT_hi = sc.sb("hT_hi", [P, KF, P], F32R)
        hT_lo = sc.sb("hT_lo", [P, KF, P], F32R)
        y = sc.sb("y", [P, D])
        ZW = 256
        zeros = sc.sb("zeros", [P, ZW])
        ps_x = sc.ps("ps_x", [P, 2, 512])
        ps_g = sc.ps("ps_g", [P, 2, 512])
        ps_h = sc.ps("ps_h", [P, 512])
        ps_y = sc.ps("ps_y", [P, 2, 512])
        g_in = [sc.sem(f"g_in{c}") for c in range(GC)]
        d_in = [sc.sem(f"d_in{c}") for c in range(DC)]
        (s_ghi, s_glo, s_dhi, s_dlo, g_used, d_used, idx_set, x_turned, x_hi, x_lo, silu_made, h_made, h_turned,
         h_hi, h_lo, y_made, y_out) = (
            sc.sem(n) for n in ("s_ghi", "s_glo", "s_dhi", "s_dlo", "g_used", "d_used", "idx_set", "x_turned",
                                "x_hi", "x_lo", "silu_made", "h_made", "h_turned", "h_hi", "h_lo", "y_made", "y_out"))
        passed, ended, zero_made, zero_out = (sc.sem(n) for n in ("passed", "ended", "zero_made", "zero_out"))
        x_in = T["xg_in"]
        wg_d, wu_d, wd_d = a["w_gate_e"][0], a["w_up_e"][0], a["w_down_e"][0]
        c = K["c"]

        def turns(eng, first, end, body, ahead=0):
            with eng.Fori(first, FEWEST + ahead) as i:
                body(i)
            with eng.Fori(FEWEST + ahead, TILES + ahead) as i:
                with eng.If(i < end + (1 + ahead)):
                    body(i)

        def is_new(eng, i):
            return eng.value_load(K["tnew"][0:1, bass.ds(i, 1)], min_val=0, max_val=1)

        def place(eng, i):
            return eng.value_load(K["tord"][0:1, bass.ds(i, 1)], min_val=0, max_val=NE - 1)

        def last_used(eng):
            return eng.value_load(K["last"][0:1, 0:1], min_val=FEWEST - 1, max_val=TILES - 1)

        with sc.block() as block:
            @block.sync
            def _(sp):
                def load_g(e, before=None):
                    for ch in range(GC):
                        if before is not None:
                            sp.wait_ge(s_ghi, before * GC + (ch + 1))
                            sp.wait_ge(s_glo, before * GC + (ch + 1))
                        for m, w in enumerate((wg_d, wu_d)):
                            src = w[bass.ds(e, 1), ch * P:(ch + 1) * P, :].rearrange("a p n -> p (a n)")
                            sp.dma_start(g_raw[:, ch, m, :], src).then_inc(g_in[ch], 16)

                def load_d(e, before=None):
                    for ch in range(DC):
                        if before is not None:
                            sp.wait_ge(s_dhi, before * DC + (ch + 1))
                            sp.wait_ge(s_dlo, before * DC + (ch + 1))
                        src = wd_d[bass.ds(e, 1), ch * P:(ch + 1) * P, :].rearrange("a p n -> p (a n)")
                        sp.dma_start(d_raw[:, ch, :], src).then_inc(d_in[ch], 16)

                end = last_used(sp)
                e0 = sp.value_load(K["texp"][0:1, 0:1], min_val=0, max_val=NE - 1)
                load_g(e0)
                load_d(e0)

                def load(i):
                    with sp.If(is_new(sp, i) != 0):
                        e = sp.value_load(K["texp"][0:1, bass.ds(i, 1)], min_val=0, max_val=NE - 1)
                        before = place(sp, i - 1)
                        load_g(e, before)
                        load_d(e, before)

                sp.wait_ge(zero_made, 1)
                assert TILES - FEWEST == FEWEST - 1
                with sp.Fori(1, FEWEST) as i:
                    load(i)
                    with sp.If(i + (FEWEST - 1) < end + 1):
                        sp.sem_inc(zero_out, 16)
                    with sp.Else():
                        sp.dma_start(T["y"][bass.ds(i * P + (FEWEST - 1) * P, P), :].rearrange("p (a n) -> p a n", n=ZW),
                                     zeros[:].unsqueeze(1).to_broadcast((P, D // ZW, ZW))).then_inc(zero_out, 16)
                turns(sp, FEWEST, end, load, ahead=1)
                sp.wait_ge(zero_out, 16 * (TILES - FEWEST))
                o = place(sp, end + 1)
                for ch in range(GC):
                    wait_alone(sp, g_in[ch], o * 32 + 32, ended)
                for ch in range(DC):
                    wait_alone(sp, d_in[ch], o * 16 + 16, ended)

            @block.gpsimd
            def _(pool):
                def gather(i):
                    nc.gpsimd.tensor_copy(idx[:], K["stok"][:, bass.ds(i, 1)]).then_inc(idx_set, 1)
                    wait_alone(pool, idx_set, i + 1, passed)
                    pool.indirect_dma_start(xg[:], None, T["u"],
                                            bass.IndirectOffsetOnAxis(ap=idx[:, 0:1], axis=0)).then_inc(x_in, 16)

                end = last_used(pool)

                def gather_next(i):
                    wait_alone(pool, x_turned, i * 2, passed)
                    gather(i)

                gather(0)
                turns(pool, 1, end, gather_next, ahead=1)
                wait_alone(pool, x_in, end * 16 + 32, passed)

            @block.scalar
            def _(act):
                def split_g(i, o, ch, room=True):
                    act.wait_ge(g_in[ch], o * 32 + 32)
                    if room:
                        act.wait_ge(g_used, i * GC + (ch + 1 - GR))
                    nc.scalar.activation(g_hi[:, ch % GR], g_raw[:, ch], ACT.Copy).then_inc(s_ghi, 1)

                def split_d(i, o, ch, room=True):
                    act.wait_ge(d_in[ch], o * 16 + 16)
                    if room:
                        act.wait_ge(d_used, i * DC + (ch + 1 - DR))
                    nc.scalar.activation(d_hi[:, ch % DR], d_raw[:, ch], ACT.Copy).then_inc(s_dhi, 1)

                def new_g(i, c0, c1):
                    with act.If(is_new(act, i) != 0):
                        o = place(act, i)
                        for ch in range(c0, c1):
                            split_g(i, o, ch)

                def new_d(i, room=True):
                    with act.If(is_new(act, i) != 0):
                        o = place(act, i)
                        for ch in range(DC):
                            split_d(i, o, ch, room)

                def x_part(i):
                    for h in range(2):
                        act.wait_ge(x_turned, i * 2 + (h + 1))
                        nc.scalar.activation(xT_hi[:, 4 * h:4 * h + 4, :],
                                             ps_x[:, h, :].rearrange("p (k n) -> p k n", k=4),
                                             ACT.Copy).then_inc(x_hi, 1)

                def silu(i):
                    act.wait_ge(g_used, i * GC + GC)
                    nc.scalar.activation(act_g[:], ps_g[:, 0, :], ACT.Silu).then_inc(silu_made, 1)

                def h_part(i):
                    act.wait_ge(h_turned, i + 1)
                    nc.scalar.activation(hT_hi[:], ps_h[:].rearrange("p (k n) -> p k n", k=KF),
                                         ACT.Copy).then_inc(h_hi, 1)

                def y_copy(i, first=False):
                    act.wait_ge(d_used, i * DC + DC)
                    if not first:
                        act.wait_ge(y_out, i * 16)
                    nc.scalar.activation(y[:], ps_y[:].rearrange("p a n -> p (a n)"), ACT.Copy).then_inc(y_made, 1)
                    act.wait_ge(y_made, i + 1)
                    act.dma_start(T["y"][bass.ds(i * P, P), :], y[:]).then_inc(y_out, 16)

                end = last_used(act)
                x_part(0)
                for ch in range(GC):
                    split_g(0, 0, ch, False)
                silu(0)
                x_part(1)
                new_g(1, 0, EARLY)
                h_part(0)

                def turn(i, first=False):
                    new_g(i, EARLY, GC)
                    if first:
                        for ch in range(DC):
                            split_d(0, 0, ch, False)
                    else:
                        new_d(i - 1)
                    silu(i)
                    x_part(i + 1)
                    new_g(i + 1, 0, EARLY)
                    y_copy(i - 1, first)
                    h_part(i)

                turn(1, first=True)
                turns(act, 2, end, turn)
                new_d(end, False)
                y_copy(end)
                wait_alone(act, y_out, end * 16 + 16, ended)

            @block.vector
            def _(dve):
                def split_g(o, ch):
                    dve.wait_ge(s_ghi, o * GC + (ch + 1))
                    nc.vector.tensor_tensor(g_lo[:, ch % GR], g_raw[:, ch], g_hi[:, ch % GR].bitcast(F32),
                                            ALU.subtract).then_inc(s_glo, 1)

                def split_d(o, ch):
                    dve.wait_ge(s_dhi, o * DC + (ch + 1))
                    nc.vector.tensor_tensor(d_lo[:, ch % DR], d_raw[:, ch], d_hi[:, ch % DR].bitcast(F32),
                                            ALU.subtract).then_inc(s_dlo, 1)

                def new_g(i, c0, c1):
                    with dve.If(is_new(dve, i) != 0):
                        o = place(dve, i)
                        for ch in range(c0, c1):
                            split_g(o, ch)

                def new_d(i):
                    with dve.If(is_new(dve, i) != 0):
                        o = place(dve, i)
                        for ch in range(DC):
                            split_d(o, ch)

                def x_part(i):
                    for h in range(2):
                        dve.wait_ge(x_hi, i * 2 + (h + 1))
                        nc.vector.tensor_tensor(xT_lo[:, 4 * h:4 * h + 4, :],
                                                ps_x[:, h, :].rearrange("p (k n) -> p k n", k=4),
                                                xT_hi[:, 4 * h:4 * h + 4, :].bitcast(F32),
                                                ALU.subtract).then_inc(x_lo, 1)

                def hidden(i):
                    dve.wait_ge(silu_made, i + 1)
                    nc.vector.tensor_tensor(hid[:], act_g[:], ps_g[:, 1, :], ALU.mult).then_inc(h_made, 1)

                def h_part(i):
                    dve.wait_ge(h_hi, i + 1)
                    nc.vector.tensor_tensor(hT_lo[:], ps_h[:].rearrange("p (k n) -> p k n", k=KF),
                                            hT_hi[:].bitcast(F32), ALU.subtract).then_inc(h_lo, 1)

                nc.vector.memset(zeros[:], 0.0).then_inc(zero_made, 1)
                end = last_used(dve)
                x_part(0)
                for ch in range(GC):
                    split_g(0, ch)
                hidden(0)
                x_part(1)
                new_g(1, 0, EARLY)
                h_part(0)

                def turn(i, first=False):
                    new_g(i, EARLY, GC)
                    if first:
                        for ch in range(DC):
                            split_d(0, ch)
                    else:
                        new_d(i - 1)
                    hidden(i)
                    x_part(i + 1)
                    new_g(i + 1, 0, EARLY)
                    h_part(i)

                turn(1, first=True)
                turns(dve, 2, end, turn)
                new_d(end)

            @block.tensor
            def _(pe):
                ident = c[:, K_ID:K_ID + P]

                def turn_x(i, first=False):
                    pe.wait_ge(x_in, i * 16 + 16)
                    for h in range(2):
                        if not first:
                            pe.wait_ge(x_lo, i * 2 + (h - 1))
                        for j in range(4):
                            k = 4 * h + j
                            last = nc.tensor.transpose(ps_x[:, h, j * P:(j + 1) * P], xg[:, k * P:(k + 1) * P], ident)
                        last.then_inc(x_turned, 1)

                def gate_up(i, first=False):
                    o = 0 if first else place(pe, i)
                    pe.wait_ge(x_lo, i * 2 + 2)
                    if not first:
                        pe.wait_ge(h_made, i)
                    for ch in range(GC):
                        pe.wait_ge(s_glo, o * GC + (ch + 1))
                        for m in range(2):
                            last = mm3(nc, ps_g[:, m, :], xT_hi[:, ch, :], xT_lo[:, ch, :],
                                       g_hi[:, ch % GR, m, :], g_lo[:, ch % GR, m, :], ch == 0, ch == GC - 1)
                        last.then_inc(g_used, 1)

                def turn_h(i):
                    pe.wait_ge(h_made, i + 1)
                    for j in range(KF):
                        last = nc.tensor.transpose(ps_h[:, j * P:(j + 1) * P], hid[:, j * P:(j + 1) * P], ident)
                    last.then_inc(h_turned, 1)

                def down(i, first=False):
                    o = 0 if first else place(pe, i)
                    pe.wait_ge(h_lo, i + 1)
                    if not first:
                        pe.wait_ge(y_made, i)
                    for ch in range(DC):
                        pe.wait_ge(s_dlo, o * DC + (ch + 1))
                        for m in range(2):
                            r = slice(m * 512, (m + 1) * 512)
                            last = mm3(nc, ps_y[:, m, :], hT_hi[:, ch, :], hT_lo[:, ch, :],
                                       d_hi[:, ch % DR, r], d_lo[:, ch % DR, r], ch == 0, ch == DC - 1)
                        last.then_inc(d_used, 1)

                end = last_used(pe)
                turn_x(0, True)
                gate_up(0, True)
                turn_x(1)
                turn_h(0)
                gate_up(1)
                turn_x(2)
                down(0, True)
                turn_h(1)

                def turn(i):
                    gate_up(i)
                    turn_x(i + 1)
                    down(i - 1)
                    turn_h(i)

                turns(pe, 2, end, turn)
                down(end)


def stage_finish(nc, a, K, T, out):
    with Scope(nc, "fin") as sc:
        WR, HB = 4, 4
        w_raw = sc.sb("w_raw", [P, WR, D])
        w_hi = sc.sb("w_hi", [P, KD + KP, D], F32R)
        w_lo = sc.sb("w_lo", [P, KD + KP, D], F32R)
        gain = sc.sb("gain", [P, D])
        gfin = sc.sb("gfin", [P, D])
        bgate = sc.sb("bgate", [1, D])
        junk = sc.sb("junk", [P, D], BF16)
        ss = sc.sb("ss", [P, NT, 2])
        rt = sc.sb("rt", [P, NT, 2])
        rs = sc.sb("rs", [P, NT, 2])
        ht = sc.sb("h", [P, HB, D])
        ys = sc.sb("y", [P, 2, 2, D])
        pt = sc.sb("p", [P, HB, PLE])
        vt = sc.sb("v", [P, D])
        vT_hi = sc.sb("vT_hi", [P, 2, KD + KP, P], F32R)
        vT_lo = sc.sb("vT_lo", [P, 2, KD + KP, P], F32R)
        gate = sc.sb("gate", [P, D])
        ot = sc.sb("o", [P, D])
        ps_x = sc.ps("ps_x", [P, 3, 512])
        ps_g = sc.ps("ps_g", [P, 2, 512])
        ps_p = sc.ps("ps_p", [P, 2, 512])
        w_in = [sc.sem(f"w_in{i}") for i in range(WR)]
        h_in = [sc.sem(f"h_in{i}") for i in range(HB)]
        y_in = T["y_in"]
        (mixed, vec_in, split_hi, split_lo, summed, sq, var, root, v_made, turned, v_hi, v_lo, gated, projected,
         sig, added, f_var, f_root, o_made, o_out, own_dve) = (
            sc.sem(n) for n in ("mixed", "vec_in", "split_hi", "split_lo", "summed", "sq", "var", "root",
                                "v_made", "turned", "v_hi", "v_lo", "gated", "projected", "sig", "added", "f_var",
                                "f_root", "o_made", "o_out", "own_dve"))
        f_sq = sc.sem("f_sq")
        wg_d = a["w_ple_gate"].rearrange("l (k p) n -> (l k) p n", p=P)
        wp_d = a["w_ple_proj"].rearrange("l (k p) n -> (l k) p n", p=P)
        p_d = a["p"].rearrange("l b (t p) d -> (l b t) p d", p=P)
        out_d = out.rearrange("b (t p) d -> (b t) p d", p=P)
        with sc.block() as block:
            @block.sync
            def _(sp):
                sp.dma_start(gain[:], a["g_ple"].to_broadcast((P, D))).then_inc(vec_in, 16)
                sp.dma_start(gfin[:], a["g_final"].rearrange("(a n) -> a n", a=1).to_broadcast((P, D))).then_inc(vec_in, 16)
                sp.dma_start(bgate[:], a["b_ple_gate"]).then_inc(vec_in, 16)
                def rows(t):
                    sp.dma_start(ht[:, t % HB, :], T["h"][t]).then_inc(h_in[t % HB], 16)
                    sp.dma_start(pt[:, t % HB, :], p_d[t]).then_inc(h_in[t % HB], 16)

                rows(0)
                for k in range(KD + KP):
                    if k >= WR:
                        sp.wait_ge(split_lo, k - WR + 1)
                    sp.dma_start(w_raw[:, k % WR, :], wg_d[k] if k < KD else wp_d[k - KD]).then_inc(w_in[k % WR], 16)
                    if k < HB - 1:
                        rows(k + 1)
                for t in range(NT):
                    sp.wait_ge(o_made, t + 1)
                    sp.dma_start(out_d[t], ot[:]).then_inc(o_out, 16)
                    if t + HB < NT:
                        rows(t + HB)
                sp.wait_ge(o_out, 16 * NT)

            @block.gpsimd
            def _(pool):
                for t in range(NT):
                    if t >= 2:
                        pool.wait_ge(summed, 2 * t - 2)
                    for k in range(2):
                        pool.indirect_dma_start(ys[:, t % 2, k, :], None, T["y"],
                                                bass.IndirectOffsetOnAxis(ap=K["slot"][:, k, t:t + 1], axis=0)
                                                ).then_inc(y_in[t % 2], 16)

            def tiles(head, turn, weigh, tail, split):
                head(0)
                turn(0)
                head(1)
                split()
                for i in range(NT + 1):
                    if i:
                        weigh(i - 1)
                    if i + 1 < NT:
                        turn(i + 1)
                    if i + 2 < NT:
                        head(i + 2)
                    if i:
                        tail(i - 1)

            @block.scalar
            def _(act):
                def split():
                    for k in range(KD + KP):
                        act.wait_ge(w_in[k % WR], 16 * (k // WR + 1))
                        nc.scalar.activation(w_hi[:, k, :], w_raw[:, k % WR, :], ACT.Copy).then_inc(split_hi, 1)

                def head(t):
                    act.wait_ge(summed, 2 * t + 2)
                    nc.scalar.activation(junk[:], ht[:, t % HB, :], ACT.Square,
                                         accum_out=ss[:, t, 0:1]).then_inc(sq, 1)
                    act.wait_ge(var, t + 1)
                    nc.scalar.activation(rt[:, t, 0:1], rt[:, t, 0:1], ACT.Sqrt).then_inc(root, 1)

                def turn(t):
                    for h in range(3):
                        act.wait_ge(turned, 3 * t + h + 1)
                        if t >= 2:
                            act.wait_ge(projected, t - 1)
                        n = 4 if h < 2 else KP
                        nc.scalar.activation(vT_hi[:, t % 2, 4 * h:4 * h + n, :],
                                             ps_x[:, h, 0:n * P].rearrange("p (k n) -> p k n", k=n),
                                             ACT.Copy).then_inc(v_hi, 1)

                def weigh(t):
                    act.wait_ge(gated, t + 1)
                    if t:
                        act.wait_ge(added, t)
                    nc.scalar.activation(gate[:], ps_g[:].rearrange("p a n -> p (a n)"), ACT.Sigmoid).then_inc(sig, 1)

                def tail(t):
                    act.wait_ge(added, t + 1)
                    nc.scalar.activation(junk[:], ht[:, t % HB, :], ACT.Square,
                                         accum_out=ss[:, t, 1:2]).then_inc(f_sq, 1)
                    act.wait_ge(f_var, t + 1)
                    nc.scalar.activation(rt[:, t, 1:2], rt[:, t, 1:2], ACT.Sqrt).then_inc(f_root, 1)

                tiles(head, turn, weigh, tail, split)

            @block.vector
            def _(dve):
                own = Tally(own_dve)

                def split():
                    for k in range(KD + KP):
                        dve.wait_ge(split_hi, k + 1)
                        nc.vector.tensor_tensor(w_lo[:, k, :], w_raw[:, k % WR, :], w_hi[:, k, :].bitcast(F32),
                                                ALU.subtract).then_inc(split_lo, 1)

                dve.wait_ge(vec_in, 48)

                def head(t):
                    h = ht[:, t % HB, :]
                    dve.wait_ge(h_in[t % HB], 32 * (t // HB + 1))
                    dve.wait_ge(y_in[t % 2], 32 * (t // 2 + 1))
                    for k in range(2):
                        nc.vector.scalar_tensor_tensor(h, ys[:, t % 2, k, :], K["cw"][:, k, t:t + 1], h, ALU.mult,
                                                       ALU.add).then_inc(summed, 1)
                        dve.wait_ge(summed, 2 * t + k + 1)
                    dve.wait_ge(sq, t + 1)
                    nc.vector.tensor_scalar(rt[:, t, 0:1], ss[:, t, 0:1], 1.0 / D, EPS, ALU.mult,
                                            ALU.add).then_inc(var, 1)
                    dve.wait_ge(root, t + 1)
                    own.inc(nc.vector.reciprocal(rs[:, t, 0:1], rt[:, t, 0:1]))
                    own.wait(dve)
                    if t:
                        dve.wait_ge(turned, 3 * t)
                    nc.vector.scalar_tensor_tensor(vt[:], h, rs[:, t, 0:1], gain[:], ALU.mult,
                                                   ALU.mult).then_inc(v_made, 1)

                def turn(t):
                    for h in range(3):
                        dve.wait_ge(v_hi, 3 * t + h + 1)
                        n = 4 if h < 2 else KP
                        nc.vector.tensor_tensor(vT_lo[:, t % 2, 4 * h:4 * h + n, :],
                                                ps_x[:, h, 0:n * P].rearrange("p (k n) -> p k n", k=n),
                                                vT_hi[:, t % 2, 4 * h:4 * h + n, :].bitcast(F32),
                                                ALU.subtract).then_inc(v_lo, 1)

                def weigh(t):
                    dve.wait_ge(sig, t + 1)
                    dve.wait_ge(projected, t + 1)
                    nc.vector.tensor_tensor(gate[:], gate[:], ps_p[:].rearrange("p a n -> p (a n)"),
                                            ALU.mult).then_inc(mixed, 1)

                def tail(t):
                    h = ht[:, t % HB, :]
                    dve.wait_ge(mixed, t + 1)
                    nc.vector.tensor_tensor(h, h, gate[:], ALU.add).then_inc(added, 1)
                    dve.wait_ge(f_sq, t + 1)
                    nc.vector.tensor_scalar(rt[:, t, 1:2], ss[:, t, 1:2], 1.0 / D, EPS, ALU.mult,
                                            ALU.add).then_inc(f_var, 1)
                    dve.wait_ge(f_root, t + 1)
                    own.inc(nc.vector.reciprocal(rs[:, t, 1:2], rt[:, t, 1:2]))
                    own.wait(dve)
                    if t:
                        dve.wait_ge(o_out, 16 * t)
                    nc.vector.scalar_tensor_tensor(ot[:], h, rs[:, t, 1:2], gfin[:], ALU.mult,
                                                   ALU.mult).then_inc(o_made, 1)

                tiles(head, turn, weigh, tail, split)

            @block.tensor
            def _(pe):
                ident = K["c"][:, K_ID:K_ID + P]

                def turn(t):
                    pe.wait_ge(v_made, t + 1)
                    pe.wait_ge(h_in[t % HB], 32 * (t // HB + 1))
                    for h in range(3):
                        if t:
                            pe.wait_ge(v_lo, 3 * t + h - 2)
                        for j in range(4 if h < 2 else KP):
                            src = vt[:, (4 * h + j) * P:(4 * h + j + 1) * P] if h < 2 else pt[:, t % HB, j * P:(j + 1) * P]
                            last = nc.tensor.transpose(ps_x[:, h, j * P:(j + 1) * P], src, ident)
                        last.then_inc(turned, 1)

                turn(0)
                for t in range(NT):
                    if t + 1 < NT:
                        turn(t + 1)
                    pe.wait_ge(v_lo, 3 * t + 3)
                    if t:
                        pe.wait_ge(sig, t)
                    for out_, ks, sem in ((ps_g, range(KD), gated), (ps_p, range(KD, KD + KP), projected)):
                        if t and ks[0]:
                            pe.wait_ge(mixed, t)
                        for h in range(2):
                            r = slice(h * 512, (h + 1) * 512)
                            for k in ks:
                                if t == 0 and h == 0:
                                    pe.wait_ge(split_lo, k + 1)
                                last = mm3(nc, out_[:, h, :], vT_hi[:, t % 2, k, :], vT_lo[:, t % 2, k, :], w_hi[:, k, r],
                                           w_lo[:, k, r], k == ks[0], k == ks[-1] and ks[0] > 0)
                            if ks[0] == 0:
                                last = nc.tensor.matmul(out_[:, h, :], K["c"][0:1, K_ONE:K_ONE + P], bgate[:, r],
                                                        start=False, stop=True)
                        last.then_inc(sem, 1)


def build(nc, a, out):
    T = {
        "feat": nc.dram_tensor("feat", [16, P, S], F32).ap(),
        "cum": nc.dram_tensor("cum", [NH, 2, S], F32).ap(),
        "h": nc.dram_tensor("h_rows", [NT, P, D], F32).ap(),
        "u": nc.dram_tensor("u_rows", [S, D], F32).ap(),
        "y": nc.dram_tensor("y_rows", [TILES * P, D], F32).ap(),
    }
    K = {}
    with Scope(nc, "all") as outer:
        T["stored"] = [outer.sem(f"stored{i}") for i in range(2)]
        T["y_in"] = [outer.sem(f"y_in{i}") for i in range(2)]
        for name in ("xg_in",):
            T[name] = outer.sem(name)
        for name, shape, dt in (("c", [P, K_COLS], F32), ("lg", [P, NT, NG + NE], F32), ("cw", [P, 2, NT], F32),
                                ("slot", [P, 2, NT], U32), ("texp", [P, 32], I32),
                                ("tnew", [P, 32], I32), ("tord", [P, 32], I32), ("last", [P, 1], I32), ("stok", [P, SLOTS // P], U32)):
            K[name] = outer.sb(name, shape, dt)
        with Scope(nc, "att") as inner:
            for name, shape, dt in (("o", [P, NT, D], F32),):
                K[name] = inner.sb(name, shape, dt)
            with Scope(nc, "tok") as tok:
                for name, shape, dt in (
                        ("maskb", [P, (2 + NT) * P], BF16), ("identb", [P, P], BF16), ("cos", [P, S], F32),
                        ("sin", [P, S], F32), ("vb", [P, NT, NH * HD], F32), ("vsw", [P, NT, 288], F32),
                        ("gate", [P, NT, 3 * NH], F32), ("vc", [P, GROUPS, HD], F32),
                        ("kc_raw", [P, GROUPS, P], F32), ("kc_hi", [P, GROUPS, P], F32R),
                        ("kc_lo", [P, GROUPS, P], F32R)):
                    K[name] = tok.sb(name, shape, dt)
                K["tokT"] = K["o"][:, 0:2, :]
                stage_project(nc, a, K, T)
                stage_compress(nc, a, K, T)
                stage_attention(nc, K, T, sparse=True)
                stage_attention(nc, K, T, sparse=False)
            stage_mix(nc, a, K, T)
        stage_route(nc, K, T)
        stage_moe(nc, a, K, T)
        stage_finish(nc, a, K, T, out)


_INS = ["x", "p", "positions", "g_mix", "w_in", "b_nsa_gate", "b_forget", "pe_cmp_k", "w_cmp_k1", "w_cmp_k2",
        "pe_cmp_v", "w_cmp_v1", "w_cmp_v2", "beta_nsa", "beta_fox", "w_out", "g_ffn", "w_group", "b_group",
        "w_router", "b_router", "w_gate_e", "w_up_e", "w_down_e", "g_ple", "w_ple_gate", "b_ple_gate",
        "w_ple_proj", "g_final"]


def kernel(**inputs):
    import concourse.bacc as bacc
    from concourse.bass_utils import run_bass_kernel_spmd as run

    nc = bacc.Bacc("TRN2", target_bir_lowering=False, num_devices=1)
    arrays, a = {}, {}
    for name in _INS:
        v = np.ascontiguousarray(inputs[name])
        arrays[f"in_{name}"] = v
        a[name] = nc.dram_tensor(f"in_{name}", v.shape, mybir.dt.from_np(v.dtype), kind="ExternalInput").ap()
    c = constants()
    arrays["in_consts"] = c
    a["consts"] = nc.dram_tensor("in_consts", c.shape, F32, kind="ExternalInput").ap()
    out = nc.dram_tensor("out", (1, S, D), F32, kind="ExternalOutput").ap()
    build(nc, a, out)
    r = run(nc, [arrays], core_ids=[0])
    return r.results[0]["out"]
```
